# Optimizing a Trainium2 kernel written in Bass

```python
import math
import jax, jax.numpy as jnp
from jax import lax
import numpy as np

D_MODEL = 1024
BATCH = 1
SEQ = 1024
DEPTH = 1

DN_HEADS = 8
DN_HEAD_DIM = 128
DN_QK = DN_HEADS * DN_HEAD_DIM
DN_V = DN_HEADS * DN_HEAD_DIM
DN_CONV = 4
DN_CHUNK = 64
DIL_GROUPS = ((128, 1), (512, 4), (2048, 16))
DIL_HEADS_PER_GROUP = 4
DIL_HEAD_DIM = 128
DIL_HEADS = len(DIL_GROUPS) * DIL_HEADS_PER_GROUP
DIL_W = DIL_HEADS * DIL_HEAD_DIM
DIL_OUT = DIL_HEADS_PER_GROUP * DIL_HEAD_DIM
DIL_BLOCK = 128
ROPE_THETA = 10000.0
MEM_TOKENS = 256
MEM_HEADS = 4
MEM_HEAD_DIM = D_MODEL // MEM_HEADS
D_FF = -(-8 * D_MODEL // (3 * 256)) * 256
IN_SIZES = (2 * DN_QK + DN_V, DN_V, DN_HEADS, DN_HEADS, DIL_W, DIL_W, DIL_W, D_MODEL, D_MODEL)
IN_WIDTH = sum(IN_SIZES)
DEEPNORM_ALPHA = (2.0 * DEPTH) ** 0.25
DEEPNORM_BETA = (8.0 * DEPTH) ** -0.25
LN_EPS = 1e-5
RMS_EPS = 1e-6

kernel_name = 'hybrid_deltanet_dilated_attn_block'

def layer_norm(x, g, b):
    xf = x.astype(jnp.float32)
    mu = jnp.mean(xf, -1, keepdims=True)
    var = jnp.mean(jnp.square(xf - mu), -1, keepdims=True)
    return ((xf - mu) * lax.rsqrt(var + LN_EPS) * g + b).astype(x.dtype)

def l2_normalize(x):
    return x * lax.rsqrt(jnp.sum(jnp.square(x), -1, keepdims=True) + RMS_EPS)

def causal_depthwise_conv(x, w):
    K = w.shape[0]
    S = x.shape[1]
    xp = jnp.pad(x, ((0, 0), (K - 1, 0), (0, 0)))
    out = xp[:, K - 1:K - 1 + S] * w[K - 1]
    for j in range(K - 1):
        out = out + xp[:, j:j + S] * w[j]
    return out

def rope(x, positions):
    D = x.shape[-1]
    inv_freq = ROPE_THETA ** (-jnp.arange(0, D, 2, dtype=jnp.float32) / D)
    ang = positions.astype(jnp.float32)[..., None] * inv_freq
    cos = jnp.cos(ang)[:, :, None]
    sin = jnp.sin(ang)[:, :, None]
    xf = x.astype(jnp.float32)
    x1, x2 = xf[..., :D // 2], xf[..., D // 2:]
    return jnp.concatenate([x1 * cos - x2 * sin, x2 * cos + x1 * sin], -1).astype(x.dtype)

def unit_lower_inverse(n):
    C = n.shape[-1]
    t = jnp.eye(C, dtype=n.dtype) + n
    p = n
    for _ in range(int(math.log2(C)) - 1):
        p = p @ p
        t = t + t @ p
    return t

def gated_delta_rule_chunked(q, k, v, g, beta):
    B, S, H, Dk = q.shape
    Dv = v.shape[-1]
    C = DN_CHUNK
    nc = S // C

    def chunks(t):
        return t.reshape(B, nc, C, H, -1).transpose(0, 3, 1, 2, 4)

    q, k, v = chunks(q), chunks(k), chunks(v)
    g = g.reshape(B, nc, C, H).transpose(0, 3, 1, 2)
    beta = beta.reshape(B, nc, C, H).transpose(0, 3, 1, 2)
    gam = jnp.cumsum(g, axis=-1)
    idx = jnp.arange(C)
    incl = idx[:, None] >= idx[None, :]
    strict = idx[:, None] > idx[None, :]
    dec_incl = jnp.exp(jnp.where(incl, gam[..., :, None] - gam[..., None, :], -jnp.inf))
    dec_strict = jnp.where(strict, dec_incl, 0.0)
    kb = k * beta[..., None]
    n = -jnp.einsum('bhncd,bhnsd->bhncs', kb, k) * dec_strict
    t = unit_lower_inverse(n)
    u = jnp.einsum('bhncs,bhnsd->bhncd', t, v * beta[..., None])
    w = jnp.einsum('bhncs,bhnsd->bhncd', t, kb * jnp.exp(gam)[..., None])
    qk = jnp.einsum('bhncd,bhnsd->bhncs', q, k) * dec_incl
    q_dec = q * jnp.exp(gam)[..., None]
    k_dec = k * jnp.exp(gam[..., -1:] - gam)[..., None]
    g_tot = jnp.exp(gam[..., -1])

    def step(state, xs):
        u_n, w_n, qk_n, qd_n, kd_n, gt_n = xs
        v_new = u_n - jnp.einsum('bhcd,bhde->bhce', w_n, state)
        o_n = jnp.einsum('bhcd,bhde->bhce', qd_n, state) + jnp.einsum('bhcs,bhse->bhce', qk_n, v_new)
        state = gt_n[..., None, None] * state + jnp.einsum('bhcd,bhce->bhde', kd_n, v_new)
        return state, o_n

    xs = (jnp.moveaxis(u, 2, 0), jnp.moveaxis(w, 2, 0), jnp.moveaxis(qk, 2, 0),
          jnp.moveaxis(q_dec, 2, 0), jnp.moveaxis(k_dec, 2, 0), jnp.moveaxis(g_tot, 2, 0))
    state0 = jnp.zeros((B, H, Dk, Dv), q.dtype)
    _, o = lax.scan(step, state0, xs)
    return o.transpose(1, 0, 3, 2, 4).reshape(B, S, H, Dv)

def banded_attention(q, k, v, window):
    Bt, L, H, D = q.shape
    blk = DIL_BLOCK
    nb = -(-L // blk)
    pad = nb * blk - L
    qb = jnp.pad(q, ((0, 0), (0, pad), (0, 0), (0, 0))).reshape(Bt, nb, blk, H, D)

    def key_blocks(t):
        t = jnp.pad(t, ((0, 0), (blk, pad), (0, 0), (0, 0))).reshape(Bt, nb + 1, blk, H, D)
        return jnp.concatenate([t[:, :-1], t[:, 1:]], axis=2)

    kb, vb = key_blocks(k), key_blocks(v)
    qpos = jnp.arange(nb)[:, None, None] * blk + jnp.arange(blk)[None, :, None]
    kpos = jnp.arange(nb)[:, None, None] * blk - blk + jnp.arange(2 * blk)[None, None, :]
    dist = qpos - kpos
    mask = (dist >= 0) & (dist <= window) & (kpos >= 0)
    s = jnp.einsum('bnqhd,bnkhd->bnhqk', qb, kb).astype(jnp.float32) * (D ** -0.5)
    s = jnp.where(mask[None, :, None], s, -jnp.inf)
    m = jnp.max(s, -1, keepdims=True)
    p = jnp.exp(s - m)
    l = jnp.sum(p, -1, keepdims=True)
    o = jnp.einsum('bnhqk,bnkhd->bnqhd', (p / l).astype(v.dtype), vb)
    lse = (m + jnp.log(l))[..., 0]
    o = o.reshape(Bt, nb * blk, H, D)[:, :L]
    lse = lse.transpose(0, 1, 3, 2).reshape(Bt, nb * blk, H)[:, :L]
    return o, lse

def dilated_sliding_window_attention(q, k, v):
    B, S, _, D = q.shape
    Hg = DIL_HEADS_PER_GROUP
    outs, lses = [], []
    for gi, (window, dil) in enumerate(DIL_GROUPS):
        lo, hi = gi * Hg, (gi + 1) * Hg

        def sub(t):
            return (t[:, :, lo:hi].reshape(B, S // dil, dil, Hg, D)
                    .transpose(0, 2, 1, 3, 4).reshape(B * dil, S // dil, Hg, D))

        o, lse = banded_attention(sub(q), sub(k), sub(v), window // dil)
        outs.append(o.reshape(B, dil, S // dil, Hg, D).transpose(0, 2, 1, 3, 4).reshape(B, S, Hg, D))
        lses.append(lse.reshape(B, dil, S // dil, Hg).transpose(0, 2, 1, 3).reshape(B, S, Hg))
    wts = jax.nn.softmax(jnp.stack(lses, 0), axis=0)
    return jnp.einsum('gbsh,gbshd->bshd', wts.astype(q.dtype), jnp.stack(outs, 0))

def hybrid_mixer(x, positions, w_in, conv_w, a_log, dt_bias, dn_norm_g, w_br_a, w_br_b, w_mix_out):
    B, S, _ = x.shape
    f32 = jnp.float32
    splits = np.cumsum(IN_SIZES)[:-1].tolist()
    a_qkv, a_z, a_decay, a_beta, b_q, b_k, b_v, gate_a, gate_b = jnp.split(x @ w_in, splits, axis=-1)

    qkv = jax.nn.silu(causal_depthwise_conv(a_qkv, conv_w)).astype(f32)
    dq, dk, dv = jnp.split(qkv, [DN_QK, 2 * DN_QK], axis=-1)
    hd = (B, S, DN_HEADS, DN_HEAD_DIM)
    dq = l2_normalize(dq.reshape(hd)) * (DN_HEAD_DIM ** -0.5)
    dk = l2_normalize(dk.reshape(hd))
    dv = dv.reshape(hd)
    g = -jnp.exp(a_log.astype(f32)) * jax.nn.softplus(a_decay.astype(f32) + dt_bias.astype(f32))
    beta = jax.nn.sigmoid(a_beta.astype(f32))
    o_a = gated_delta_rule_chunked(dq, dk, dv, g, beta)
    o_a = o_a * lax.rsqrt(jnp.mean(jnp.square(o_a), -1, keepdims=True) + RMS_EPS) * dn_norm_g.astype(f32)
    o_a = (o_a * jax.nn.silu(a_z.astype(f32)).reshape(hd)).reshape(B, S, DN_V).astype(x.dtype)
    y_a = o_a @ w_br_a

    hb = (B, S, DIL_HEADS, DIL_HEAD_DIM)
    bq = rope(b_q.reshape(hb), positions)
    bk = rope(b_k.reshape(hb), positions)
    o_b = dilated_sliding_window_attention(bq, bk, b_v.reshape(hb)).reshape(B, S, DIL_OUT)
    y_b = o_b @ w_br_b

    h = jax.nn.sigmoid(gate_a) * y_a + jax.nn.sigmoid(gate_b) * y_b
    return h @ w_mix_out

def memory_cross_attention(x, mem, w_q, w_kv, w_o):
    B, S, _ = x.shape
    M = mem.shape[1]
    q = (x @ w_q).reshape(B, S, MEM_HEADS, MEM_HEAD_DIM)
    k, v = jnp.split(mem @ w_kv, 2, axis=-1)
    k = k.reshape(B, M, MEM_HEADS, MEM_HEAD_DIM)
    v = v.reshape(B, M, MEM_HEADS, MEM_HEAD_DIM)
    s = jnp.einsum('bshd,bmhd->bhsm', q, k).astype(jnp.float32) * (MEM_HEAD_DIM ** -0.5)
    p = jax.nn.softmax(s, axis=-1).astype(x.dtype)
    o = jnp.einsum('bhsm,bmhd->bshd', p, v).reshape(B, S, D_MODEL)
    return o @ w_o

def swiglu_ffn(x, w13, w2):
    a, b = jnp.split(x @ w13, 2, axis=-1)
    return (jax.nn.silu(a) * b) @ w2

def setup_inputs(seed: int = 0) -> dict:
    key = jax.random.key(seed)
    ks = jax.random.split(key, 24)
    L = DEPTH
    f32 = jnp.float32

    def dense(k, fan_in, fan_out, scale=1.0):
        return jax.random.normal(k, (L, fan_in, fan_out), f32) * (scale * fan_in ** -0.5)

    def gain(k, n):
        return 1.0 + 0.02 * jax.random.normal(k, (L, n), f32)

    def bias(k, n):
        return 0.02 * jax.random.normal(k, (L, n), f32)

    x = jax.random.normal(ks[0], (BATCH, SEQ, D_MODEL), f32)
    mem = jax.random.normal(ks[1], (BATCH, MEM_TOKENS, D_MODEL), f32)
    offset = jax.random.randint(ks[2], (BATCH, 1), 0, 4096, jnp.int32)
    positions = offset + jnp.arange(SEQ, dtype=jnp.int32)[None, :]
    w_in = dense(ks[3], D_MODEL, IN_WIDTH)
    conv_w = 0.5 * jax.random.normal(ks[4], (L, DN_CONV, 2 * DN_QK + DN_V), f32)
    a_log = jnp.log(jax.random.uniform(ks[5], (L, DN_HEADS), f32, 1.0, 16.0))
    dt = jnp.exp(jax.random.uniform(ks[6], (L, DN_HEADS), f32, math.log(1e-3), math.log(1e-1)))
    dt_bias = dt + jnp.log(-jnp.expm1(-dt))
    dn_norm_g = gain(ks[7], DN_HEAD_DIM)
    w_br_a = dense(ks[8], DN_V, D_MODEL)
    w_br_b = dense(ks[9], DIL_OUT, D_MODEL)
    w_mix_out = dense(ks[10], D_MODEL, D_MODEL, DEEPNORM_BETA)
    ln1_g = gain(ks[11], D_MODEL)
    ln1_b = bias(ks[12], D_MODEL)
    w_xq = dense(ks[13], D_MODEL, D_MODEL)
    w_xkv = dense(ks[14], D_MODEL, 2 * D_MODEL)
    w_xo = dense(ks[15], D_MODEL, D_MODEL, DEEPNORM_BETA)
    ln2_g = gain(ks[16], D_MODEL)
    ln2_b = bias(ks[17], D_MODEL)
    w_ffn13 = dense(ks[18], D_MODEL, 2 * D_FF)
    w_ffn2 = dense(ks[19], D_FF, D_MODEL, DEEPNORM_BETA)
    ln3_g = gain(ks[20], D_MODEL)
    ln3_b = bias(ks[21], D_MODEL)
    return {'x': x, 'mem': mem, 'positions': positions, 'w_in': w_in, 'conv_w': conv_w,
            'a_log': a_log, 'dt_bias': dt_bias, 'dn_norm_g': dn_norm_g, 'w_br_a': w_br_a,
            'w_br_b': w_br_b, 'w_mix_out': w_mix_out, 'ln1_g': ln1_g, 'ln1_b': ln1_b,
            'w_xq': w_xq, 'w_xkv': w_xkv, 'w_xo': w_xo, 'ln2_g': ln2_g, 'ln2_b': ln2_b,
            'w_ffn13': w_ffn13, 'w_ffn2': w_ffn2, 'ln3_g': ln3_g, 'ln3_b': ln3_b}

def reference(x, mem, positions, w_in, conv_w, a_log, dt_bias, dn_norm_g, w_br_a, w_br_b,
              w_mix_out, ln1_g, ln1_b, w_xq, w_xkv, w_xo, ln2_g, ln2_b, w_ffn13, w_ffn2,
              ln3_g, ln3_b):
    for l in range(DEPTH):
        mix = hybrid_mixer(x, positions, w_in[l], conv_w[l], a_log[l], dt_bias[l], dn_norm_g[l],
                           w_br_a[l], w_br_b[l], w_mix_out[l])
        x = layer_norm(DEEPNORM_ALPHA * x + mix, ln1_g[l], ln1_b[l])
        cross = memory_cross_attention(x, mem, w_xq[l], w_xkv[l], w_xo[l])
        x = layer_norm(DEEPNORM_ALPHA * x + cross, ln2_g[l], ln2_b[l])
        ffn = swiglu_ffn(x, w_ffn13[l], w_ffn2[l])
        x = layer_norm(DEEPNORM_ALPHA * x + ffn, ln3_g[l], ln3_b[l])
    return x


_drawn_inputs = setup_inputs


def setup_inputs(seed=0):
    import zlib

    import numpy as np

    out = dict(_drawn_inputs(seed))
    spreads = {}
    factors = {'dn_norm_g': 22.96,
     'ln1_g': 2.721,
     'ln1_b': 2.764,
     'ln2_g': 2.75,
     'ln2_b': 2.759,
     'ln3_g': 25.806,
     'ln3_b': 23.997,
     'w_br_b': 4.694}
    for name, (base, spread) in spreads.items():
        noise = np.random.default_rng([zlib.crc32(name.encode()), seed]).standard_normal(out[name].shape)
        drawn = base * np.exp(spread * noise) if base else spread * noise
        out[name] = __import__('jax').numpy.asarray(drawn.astype(out[name].dtype))
    for name, factor in factors.items():
        out[name] = (out[name] * factor).astype(out[name].dtype)
    return out
```

```python
import math
from contextlib import ExitStack

import concourse.bass as bass
import numpy as np
from concourse import mybir

F32 = mybir.dt.float32
F32R = mybir.dt.float32r
I32 = mybir.dt.int32
ALU = mybir.AluOpType
ACT = mybir.ActivationFunctionType
AX_X = mybir.AxisListType.X

P = 128
D_MODEL = 1024
SEQ = 1024
KT = D_MODEL // P
TT = SEQ // P
HALF = SEQ // 2
HEADS = 8
CHUNK = 64
CONV = 4
HG = 4
DILATIONS = (1, 4, 16)
GROUPS = len(DILATIONS)
DIL_W = GROUPS * HG * P
MEM = 256
XH = 4
XD = 256
D_FF = 2816
FT = D_FF // P
ALPHA = 2.0 ** 0.25
LN_EPS = 1e-5
RMS_EPS = 1e-6
NEG = -1e30

COL_Q, COL_K, COL_V = 0, HEADS * P, 2 * HEADS * P
COL_Z = 3 * HEADS * P
COL_DB = COL_Z + HEADS * P
COL_BQ = COL_DB + 2 * HEADS
COL_BK = COL_BQ + DIL_W
COL_BV = COL_BK + DIL_W
COL_GA = COL_BV + DIL_W
COL_GB = COL_GA + D_MODEL

RAW_SLOTS = 2
SPLIT_SLOTS = 4
UNIT = 1024


class Names:
    pass


def bc(ap, n):
    m = ap.shape[1]
    return ap.rearrange("p (m a) -> p m a", a=1).broadcast_to([P, m, n])


def rep(ap, n):
    m = ap.shape[1]
    return ap.rearrange("p (a m) -> p a m", a=1).broadcast_to([P, n, m])


def tiles(ap, n=P):
    return ap.rearrange("p (t n) -> p t n", n=n)



def load_unit(k, sync, u, ap, dst=None):
    slot = k.raw[u % RAW_SLOTS]
    if u >= RAW_SLOTS:
        sync.wait_ge(k.w_split, u - RAW_SLOTS + 1)
    sync.dma_start(slot[:, :].rearrange("p (k n) -> p k n", k=ap.shape[1]), ap).then_inc(k.w_loaded[u % RAW_SLOTS], 16)


def round_unit(k, act, u, slot, raw):
    u, turn = u if isinstance(u, tuple) else (u, u // RAW_SLOTS)
    act.wait_ge(k.w_loaded[raw], 16 * (turn + 1))
    if not isinstance(u, int) or u >= SPLIT_SLOTS:
        act.wait_ge(k.w_used, u - SPLIT_SLOTS + 1)
    act.activation(k.whi[slot][:, :], k.raw[raw][:, :], ACT.Copy).then_inc(k.w_rounded, 1)


def rest_unit(k, dve, u, slot, raw):
    dve.wait_ge(k.w_rounded, u + 1)
    dve.tensor_tensor(k.wlo[slot][:, :], k.raw[raw][:, :], k.whi[slot][:, :].bitcast(F32),
                      ALU.subtract).then_inc(k.w_split, 1)


def columns(w, c0, n=P):
    return w[:, c0:c0 + n].rearrange("(k p) n -> p k n", p=P)


def three(pe, out, w_hi, w_lo, x_hi, x_lo, first, last):
    pe.matmul(out, w_hi, x_hi, start=first, stop=False)
    pe.matmul(out, w_hi, x_lo, start=False, stop=False)
    return pe.matmul(out, w_lo, x_hi, start=False, stop=last)


def clear_semaphores(nc, k):
    with nc.Block() as block:
        @block.sync
        def _(sync):
            for q in k.phase_sems:
                sync.sem_clear(q)
    k.phase_sems = []


def declare(nc, ctx, k):
    def sb(name, shape, dt=F32):
        t = ctx.enter_context(nc.sbuf_tensor(name, shape, dt))
        return t

    def sem(name):
        q = ctx.enter_context(nc.semaphore(name))
        k.phase_sems.append(q)
        return q
    return sb, sem


def setup(nc, k, a):
    with ExitStack() as ctx:
        sb, sem = declare(nc, ctx, k)
        xn = sb("xn", [P, TT, D_MODEL])
        wrows = sb("conv_rows", [96, P])
        dbT = sb("dbT", [16, SEQ])
        db = sb("db", [P, 16, TT])
        a_row = sb("a_row", [P, HEADS])
        dt_row = sb("dt_row", [P, HEADS])
        sp = sb("sp", [P, 2, 64])
        mag = sb("mag", [P, 2, 64])
        g = sb("g", [P, 64])
        ps = [ctx.enter_context(nc.psum_tensor(f"p0_{i}", [P, 512], F32)) for i in range(8)]
        with nc.Block() as block:
            @block.sync
            def _(sync):
                for t in range(TT):
                    sync.dma_start(xn[:, t, :], a["x"][0, t * P:(t + 1) * P, :]).then_inc(k.x_loaded, 16)
                sync.dma_start(wrows[:, :], a["conv_w"].rearrange("l j (t c) -> (l j t) c", c=P)).then_inc(k.small_loaded, 16)
                sync.dma_start(a_row[:, :], a["a_log"].partition_broadcast(P)).then_inc(k.small_loaded, 16)
                sync.dma_start(dt_row[:, :], a["dt_bias"].partition_broadcast(P)).then_inc(k.small_loaded, 16)
                sync.dma_start(k.dn_g[:, :], a["dn_norm_g"].rearrange("l (d o) -> (l d) o", o=1)).then_inc(k.small_loaded, 16)
                load_unit(k, sync, 0, columns(a["w_in"][0], COL_DB))
                load_unit(k, sync, 1, columns(a["w_in"][0], COL_Q))

            @block.gpsimd
            def _(pool):
                pool.memset(k.ident[:, :], 0.0).then_inc(k.const, 1)
                pool.memset(k.ones[:, :], 1.0).then_inc(k.const, 1)
                pool.memset(k.upto[:, :], 1.0).then_inc(k.const, 1)
                pool.memset(k.neg_strict[:, :], 0.0).then_inc(k.const, 1)
                pool.memset(k.neg_incl[:, :], 0.0).then_inc(k.const, 1)
                pool.memset(k.same[:, :], 0.0).then_inc(k.const, 1)
                pool.memset(k.other[:, :], 1.0).then_inc(k.const, 1)
                pool.wait_ge(k.const, 7)
                pool.affine_select(out=k.ident[:, :], in_=k.ident[:, :], compare_op=ALU.not_equal, fill=1.0,
                                   base=0, pattern=[[-1, P]], channel_multiplier=1).then_inc(k.const, 1)
                pool.affine_select(out=k.upto[:, :], in_=k.upto[:, :], compare_op=ALU.is_ge, fill=0.0,
                                   base=0, pattern=[[1, P]], channel_multiplier=-1).then_inc(k.const, 1)
                pool.affine_select(out=k.neg_incl[:, :], in_=k.neg_incl[:, :], compare_op=ALU.is_ge, fill=NEG,
                                   base=0, pattern=[[1, P]], channel_multiplier=-1).then_inc(k.const, 1)
                pool.affine_select(out=k.neg_strict[:, :], in_=k.neg_strict[:, :], compare_op=ALU.is_ge, fill=NEG,
                                   base=-1, pattern=[[1, P]], channel_multiplier=-1).then_inc(k.const, 1)
                for n, (m, v) in enumerate(((k.same, 1.0), (k.other, 0.0))):
                    pool.wait_ge(k.const, 11 + 2 * n)
                    pool.memset(m[0:CHUNK, 0:CHUNK], v).then_inc(k.const, 1)
                    pool.wait_ge(k.const, 12 + 2 * n)
                    pool.memset(m[CHUNK:P, CHUNK:P], v).then_inc(k.const, 1)
                pool.wait_ge(k.const, 15)
                pool.memset(k.xpad[0][:, 0:CONV - 1], 0.0).then_inc(k.const, 1)
                pool.memset(k.xpad[1][:, 0:CONV - 1], 0.0).then_inc(k.const, 1)
                for col, v in ((k.eps_rms, RMS_EPS), (k.eps_ln, LN_EPS), (k.one_col, 1.0)):
                    pool.memset(col[:, :], v).then_inc(k.const, 1)

            @block.tensor
            def _(pe):
                pe.wait_ge(k.const, 20)
                pe.wait_ge(k.x_loaded, 16 * TT)
                n = 0
                for m in range(KT):
                    for f in range(2):
                        if n >= 8:
                            pe.wait_ge(k.x_split, n - 7)
                        for t in range(4):
                            last = pe.transpose(ps[n % 8][:, t * P:(t + 1) * P],
                                                xn[:, 4 * f + t, m * P:(m + 1) * P], k.ident[:, :])
                        last.then_inc(k.x_turned, 1)
                        n += 1
                pe.wait_ge(k.w_split, 1)
                pe.wait_ge(k.x_split, 16)
                for f in range(2):
                    for m in range(KT):
                        last = three(pe, ps[f][:, :], k.whi[0][:, m * P:(m + 1) * P], k.wlo[0][:, m * P:(m + 1) * P],
                                     k.xh[:, m, f * HALF:(f + 1) * HALF], k.xl[:, m, f * HALF:(f + 1) * HALF],
                                     m == 0, m == KT - 1)
                last.then_inc(k.w_used, 1)
                pe.wait_ge(k.db_copied, 2)
                for t in range(TT):
                    last = pe.transpose(ps[2][:, t * 16:(t + 1) * 16], dbT[:, t * P:(t + 1) * P], k.ident[0:16, 0:16])
                last.then_inc(k.db_turned, 1)
                pe.wait_ge(k.small_loaded, 64)
                pe.transpose(ps[3][:, 0:96], wrows[:, :], k.ident[0:96, 0:96]).then_inc(k.conv_turned, 1)
                pe.wait_ge(k.g_ready, 1)
                pe.matmul(ps[4][:, 0:64], k.upto[:, :], g[:, :], start=True, stop=True)
                pe.matmul(ps[5][:, 0:64], k.ones[:, :], g[:, :], start=True, stop=True).then_inc(k.gam_done, 1)

            @block.scalar
            def _(act):
                round_unit(k, act, 0, 0, 0)
                for n in range(16):
                    m, f = n // 2, n % 2
                    act.wait_ge(k.x_turned, n + 1)
                    act.activation(k.xh[:, m, f * HALF:(f + 1) * HALF], ps[n % 8][:, :], ACT.Copy).then_inc(k.x_rounded, 1)
                round_unit(k, act, 1, 1, 1)
                act.wait_ge(k.w_used, 1)
                for f in range(2):
                    act.activation(dbT[:, f * HALF:(f + 1) * HALF], ps[f][0:16, :], ACT.Copy).then_inc(k.db_copied, 1)
                act.wait_ge(k.mag_ready, 1)
                act.activation(sp[:, :, :], mag[:, :, :], ACT.Exp, scale=-1.0).then_inc(k.sp_step, 1)
                act.wait_ge(k.sp_step, 1)
                act.activation(sp[:, :, :], sp[:, :, :], ACT.Ln, bias=k.one_col[:, :]).then_inc(k.sp_step, 1)
                act.activation(a_row[:, :], a_row[:, :], ACT.Exp).then_inc(k.sp_step, 1)
                act.wait_ge(k.lnb_ready, 1)
                act.activation(k.beta[:, :, :], k.lnb[:, :, :], ACT.Exp).then_inc(k.sp_step, 1)
                act.wait_ge(k.gam_read, 2)
                act.activation(k.gtot_e[:, :, :], k.gtot[:, :, :], ACT.Exp).then_inc(k.sp_step, 1)

            @block.vector
            def _(dve):
                rest_unit(k, dve, 0, 0, 0)
                for n in range(16):
                    m, f = n // 2, n % 2
                    dve.wait_ge(k.x_rounded, n + 1)
                    dve.tensor_tensor(k.xl[:, m, f * HALF:(f + 1) * HALF], ps[n % 8][:, :],
                                      k.xh[:, m, f * HALF:(f + 1) * HALF].bitcast(F32), ALU.subtract).then_inc(k.x_split, 1)
                rest_unit(k, dve, 1, 1, 1)
                dve.wait_ge(k.conv_turned, 1)
                dve.tensor_copy(k.cw[:, :], ps[3][:, 0:96]).then_inc(k.dve_setup, 1)
                dve.wait_ge(k.db_turned, 1)
                dve.tensor_copy(db[:, :, :], ps[2][:, 0:128].rearrange("p (t c) -> p c t", c=16)).then_inc(k.dve_setup, 1)
                dve.wait_ge(k.dve_setup, 2)
                z = db[:, 0:8, :]
                dve.tensor_tensor(z, z, bc(dt_row[:, :], TT), ALU.add).then_inc(k.dve_setup, 1)
                dve.wait_ge(k.dve_setup, 3)
                z2 = db[:, :, :].rearrange("p c t -> p (c t)")
                m2 = mag[:, :, :].rearrange("p a b -> p (a b)")
                dve.tensor_scalar(m2, z2, -1.0, None, ALU.mult).then_inc(k.dve_setup, 1)
                dve.wait_ge(k.dve_setup, 4)
                dve.tensor_tensor(m2, m2, z2, ALU.max).then_inc(k.mag_ready, 1)
                dve.wait_ge(k.sp_step, 3)
                dve.scalar_tensor_tensor(out=g[:, :], in0=z2[:, 0:64], scalar=0.0, in1=sp[:, 0, :],
                                         op0=ALU.max, op1=ALU.add).then_inc(k.dve_setup, 1)
                dve.scalar_tensor_tensor(out=k.lnb[:, :, :].rearrange("p a b -> p (a b)"), in0=z2[:, 64:128], scalar=0.0,
                                         in1=sp[:, 1, :], op0=ALU.min, op1=ALU.subtract).then_inc(k.lnb_ready, 1)
                dve.wait_ge(k.dve_setup, 5)
                dve.tensor_scalar(g[:, :], g[:, :], -1.0, None, ALU.mult).then_inc(k.dve_setup, 1)
                dve.wait_ge(k.dve_setup, 6)
                dve.tensor_tensor(tiles(g[:, :], TT), tiles(g[:, :], TT), bc(a_row[:, :], TT), ALU.mult).then_inc(k.g_ready, 1)
                dve.wait_ge(k.gam_done, 1)
                dve.tensor_copy(k.gam[:, :, :].rearrange("p a b -> p (a b)"), ps[4][:, 0:64]).then_inc(k.gam_read, 1)
                dve.tensor_copy(k.gtot[:, :, :].rearrange("p a b -> p (a b)"), ps[5][:, 0:64]).then_inc(k.gam_read, 1)
                dve.wait_ge(k.gam_read, 2)
                dve.wait_ge(k.lnb_ready, 1)
                dve.tensor_tensor(k.gl[:, :, :], k.gam[:, :, :], k.lnb[:, :, :], ALU.add)
                dve.tensor_scalar(k.gs[:, :, :].rearrange("p a b -> p (a b)"), k.gam[:, :, :].rearrange("p a b -> p (a b)"),
                                  -0.5 * math.log(P), None, ALU.add)


def deltanet(nc, k, a):
    with ExitStack() as ctx:
        sb, sem = declare(nc, ctx, k)
        qT = [sb(f"qT{i}", [P, SEQ]) for i in range(2)]
        kTt = [sb(f"kT{i}", [P, SEQ]) for i in range(2)]
        vT = [sb(f"vT{i}", [P, SEQ]) for i in range(2)]
        zT = [sb(f"zT{i}", [P, SEQ]) for i in range(2)]
        qkv = (qT, kTt, vT)
        sqk = sb("sq_or_kbg", [P, SEQ])
        sqq = sb("sq_or_qd", [P, SEQ])
        kn = sb("kn", [P, SEQ])
        vb = sb("vb", [P, SEQ])
        x1 = sb("x1", [P, SEQ])
        x2 = sb("x2", [P, SEQ])
        nT = sb("nT", [P, SEQ])
        pd = sb("pd", [P, TT, 2, P])
        pw = sb("pw", [P, SEQ])
        no = sb("no", [P, SEQ])
        S = sb("state", [P, P])
        rbuf = sb("rbuf", [P, 2, P])
        vnew = sb("vnew", [P, 2, P])
        st = sb("stats", [P, 2, TT])
        rowA = sb("rowA", [P, TT])
        rowQ = sb("rowQ", [P, TT])
        colB = sb("colB", [P, TT])
        kde = sb("kde", [P, TT])
        orms = sb("orms", [P, TT])
        PP = ctx.enter_context(nc.psum_tensor("PP", [P, 1024], F32))
        DA = ctx.enter_context(nc.psum_tensor("DA", [P, 1024], F32))
        DB = ctx.enter_context(nc.psum_tensor("DB", [P, 1024], F32))
        DC = ctx.enter_context(nc.psum_tensor("DC", [P, 1024], F32))
        DD = (DA, DB)
        s = Names()
        s.half_done = sem("dn_half_done")
        s.proj_read = sem("dn_proj_read")
        s.conv_step = sem("dn_conv_step")
        s.conv_done = sem("dn_conv_done")
        s.silu_done = sem("dn_silu_done")
        s.turned = sem("dn_turned")
        s.squared = sem("dn_squared")
        s.ssq_done = sem("dn_ssq_done")
        s.kn_copied = sem("dn_kn_copied")
        s.vb_done = sem("dn_vb_done")
        s.ln_done = sem("dn_ln_done")
        s.rows_done = sem("dn_rows_done")
        s.kde_done = sem("dn_kde_done")
        s.kk_done = sem("dn_kk_done")
        s.qk_done = sem("dn_qk_done")
        s.an_rows = sem("dn_an_rows")
        s.aq_rows = sem("dn_aq_rows")
        s.an_exp = sem("dn_an_exp")
        s.aq_exp = sem("dn_aq_exp")
        s.x1_ready = sem("dn_x1_ready")
        s.x1_exp = sem("dn_x1_exp")
        s.x2_ready = sem("dn_x2_ready")
        s.x2_exp = sem("dn_x2_exp")
        s.nT_done = sem("dn_nT_done")
        s.qk_decayed = sem("dn_qk_decayed")
        s.kbg_done = sem("dn_kbg_done")
        s.qd_done = sem("dn_qd_done")
        s.kd_done = sem("dn_kd_done")
        s.n_turned = sem("dn_n_turned")
        s.p0_done = sem("dn_p0_done")
        s.off_copied = sem("dn_off_copied")
        s.off_done = sem("dn_off_done")
        s.dt_init = sem("dn_dt_init")
        s.pw_done = sem("dn_pw_done")
        s.pT_copied = sem("dn_pT_copied")
        s.dT_added = sem("dn_dT_added")
        s.p_copied = sem("dn_p_copied")
        s.d_turned = sem("dn_d_turned")
        s.d_copied = sem("dn_d_copied")
        s.z_done = sem("dn_z_done")
        s.z_copied = sem("dn_z_copied")
        s.w_done = sem("dn_w_done")
        s.t_done = sem("dn_t_done")
        s.r_done = sem("dn_r_done")
        s.r_read = sem("dn_r_read")
        s.v_done = sem("dn_v_done")
        s.v_copied = sem("dn_v_copied")
        s.ds_done = sem("dn_ds_done")
        s.s_done = sem("dn_s_done")
        s.o_done = sem("dn_o_done")
        s.o_copied = sem("dn_o_copied")
        s.o_squared = sem("dn_o_squared")
        s.o_ssq = sem("dn_o_ssq")
        s.o_ln = sem("dn_o_ln")
        s.o_rs = sem("dn_o_rs")
        s.o_scaled = sem("dn_o_scaled")
        s.o_turned = sem("dn_o_turned")
        s.o_gated = sem("dn_o_gated")
        s.o_stored = sem("dn_o_stored")
        with nc.Block() as block:
            @block.sync
            def _(sync):
                for q in k.phase_sems:
                    sync.sem_inc(q, 1)
        base = 1

        def unit(h, n):
            return base + 4 * h + n

        def unit_turn(h, n):
            return unit(h, n), 2 * h + (base + n) // RAW_SLOTS

        def piece(pe, h, i):
            n, f, kk = i // 8, (i // 4) % 2, i % 4
            slot = (base + n) % SPLIT_SLOTS
            if kk == 0:
                if f == 0:
                    pe.wait_ge(k.w_split, unit(h, n) + 1)
                pe.wait_ge(s.proj_read, 1 + 8 * h + 2 * n + f - 1) if not (isinstance(h, int) and 8 * h + 2 * n + f - 1 <= 0) else None
            for m in (2 * kk, 2 * kk + 1):
                last = three(pe, PP[:, f * HALF:(f + 1) * HALF],
                             k.whi[slot][:, m * P:(m + 1) * P], k.wlo[slot][:, m * P:(m + 1) * P],
                             k.xh[:, m, f * HALF:(f + 1) * HALF], k.xl[:, m, f * HALF:(f + 1) * HALF],
                             m == 0, m == KT - 1)
            if kk == 3:
                last.then_inc(s.half_done if f == 0 else k.w_used, 1)

        def pieces(pe, h, i0, i1):
            if h is not None:
                for i in range(i0, i1):
                    piece(pe, h, i)

        def ch(t, c):
            return t[:, c * P:(c + 1) * P]

        def pe_step(pe, h, g, b):
            if g is None:
                pieces(pe, h, 0, 32)
                return
            q, kk_, v = qT[b], kTt[b], vT[b]
            for i, (src, out) in enumerate(((q, DA), (kk_, DB), (v, DC))):
                pe.wait_ge(s.silu_done, 1 + 3 * g + i + 1)
                if i == 0:
                    pe.wait_ge(s.o_gated, 1 + g)
                    pe.wait_ge(s.s_done, 1 + 8 * g)
                    pe.wait_ge(s.o_copied, 1 + 8 * g)
                for c in range(TT):
                    last = pe.transpose(ch(out, c), ch(src, c), k.ident[:, :])
                last.then_inc(s.turned, 1)
            pieces(pe, h, 0, 4)
            pe.wait_ge(s.squared, 1 + 2 * g + 1)
            for c in range(TT):
                last = pe.matmul(ch(DA, c), ch(kk_, c), ch(kk_, c), start=True, stop=True)
            last.then_inc(s.kk_done, 1)
            pe.wait_ge(s.kn_copied, 1 + g + 1)
            pe.wait_ge(s.squared, 1 + 2 * g + 2)
            for c in range(TT):
                last = pe.matmul(ch(DB, c), ch(kk_, c), ch(q, c), start=True, stop=True)
            last.then_inc(s.qk_done, 1)
            pe.wait_ge(s.rows_done, 1 + g + 1)
            pe.wait_ge(s.vb_done, 1 + g + 1)
            for c in range(TT):
                last = pe.matmul(ch(DC, c), rowA[:, c:c + 1].broadcast_to([P, P]), k.ident[:, :], start=True, stop=True)
            last.then_inc(s.an_rows, 1)
            pieces(pe, h, 4, 6)
            pe.wait_ge(s.an_exp, 1 + g + 1)
            pe.wait_ge(s.x1_ready, 1 + g + 1)
            for c in range(TT):
                last = pe.matmul(ch(DC, c), rowQ[:, c:c + 1].broadcast_to([P, P]), k.ident[:, :], start=True, stop=True)
            last.then_inc(s.aq_rows, 1)
            pieces(pe, h, 6, 8)
            pe.wait_ge(s.nT_done, 1 + g + 1)
            for c in range(TT):
                last = pe.transpose(ch(DA, c), ch(nT, c), k.ident[:, :])
            last.then_inc(s.n_turned, 1)
            pieces(pe, h, 8, 9)
            for r in range(6):
                for j in range(2):
                    step = 12 * g + 2 * r + j
                    if r == 0:
                        pe.wait_ge(s.p0_done, 1 + 2 * g + 2)
                        pe.wait_ge(s.off_copied, 1 + g + 1)
                        pe.wait_ge(s.qk_decayed, 1 + g + 1)
                        pe.wait_ge(s.aq_exp, 1 + g + 1)
                        pe.wait_ge(s.x2_ready, 1 + g + 1)
                    else:
                        if r == 1:
                            pe.wait_ge(s.dt_init, 1 + g + 1)
                        else:
                            pe.wait_ge(s.dT_added, 1 + 10 * g + 2 * (r - 2) + j + 1)
                        if r < 5:
                            pe.wait_ge(s.pT_copied, 1 + 8 * g + 2 * (r - 1) + j + 1)
                        pe.wait_ge(s.p_copied, 1 + 10 * g + 2 * (r - 1) + j + 1)
                    for i in range(4):
                        c = 4 * j + i
                        out = DD[j][:, 2 * i * P:2 * (i + 1) * P]
                        if r == 0:
                            last = pe.matmul(out[:, 0:P], ch(pw, c), pd[:, c, 0, :], start=True, stop=True)
                        elif r < 4:
                            last = pe.matmul(out, ch(pw, c), pd[:, c, :, :].rearrange("p a b -> p (a b)"), start=True, stop=True)
                        else:
                            last = pe.matmul(out[:, P:2 * P], ch(pw, c), pd[:, c, 1, :], start=True, stop=True)
                    if r < 5:
                        for i in range(4):
                            c = 4 * j + i
                            last = pe.matmul(ch(DC, c), pd[:, c, 0, :], ch(pw, c), start=True, stop=True)
                    last.then_inc(s.pw_done, 1)
                if r < 4:
                    pieces(pe, h, 9 + r, 10 + r)
            for j in range(2):
                pe.wait_ge(s.dT_added, 1 + 10 * g + 8 + j + 1)
                for i in range(4):
                    c = 4 * j + i
                    last = pe.transpose(DD[j][:, i * P:(i + 1) * P], pd[:, c, 1, :], k.ident[:, :])
                last.then_inc(s.d_turned, 1)
            for j in range(2):
                pe.wait_ge(s.off_done, 1 + g + 1)
                for i in range(4):
                    c = 4 * j + i
                    last = pe.matmul(ch(DC, c), ch(no, c), pd[:, c, 1, :], start=True, stop=True)
                last.then_inc(s.z_done, 1)
            pieces(pe, h, 13, 14)
            for j in range(2):
                pe.wait_ge(s.z_copied, 1 + 2 * g + j + 1)
                pe.wait_ge(s.d_copied, 1 + 2 * g + j + 1)
                for i in range(4):
                    c = 4 * j + i
                    last = pe.matmul(DD[j][:, HALF + i * P:HALF + (i + 1) * P], ch(pw, c), ch(x1, c), start=True, stop=True)
                last.then_inc(s.w_done, 1)
            for c in range(TT):
                j = c % 2
                if c:
                    pe.wait_ge(s.s_done, 1 + 8 * g + c)
                if c == 0:
                    pe.wait_ge(k.s_zero, g + 1)
                    pe.wait_ge(s.kbg_done, 1 + g + 1)
                    pe.wait_ge(s.qd_done, 1 + g + 1)
                    pe.wait_ge(s.d_copied, 1 + 2 * g + 2)
                else:
                    pe.wait_ge(s.r_read, 1 + 8 * g + c)
                pe.matmul(DA[:, 0:P], ch(sqk, c), S[:, :], start=True, stop=True).then_inc(s.r_done, 1)
                if c == 0:
                    pe.wait_ge(s.z_copied, 1 + 2 * g + 2)
                elif c >= 2:
                    pe.wait_ge(s.o_copied, 1 + 8 * g + c - 1)
                pe.matmul(DC[:, j * HALF:j * HALF + P], ch(sqq, c), S[:, :], start=True, stop=False)
                pieces(pe, h, 14 + 2 * c, 15 + 2 * c)
                pe.wait_ge(s.r_read, 1 + 8 * g + c + 1)
                if c == 0:
                    pe.wait_ge(s.t_done, 1 + 2 * g + 2)
                else:
                    pe.wait_ge(s.v_copied, 1 + 8 * g + c)
                pe.matmul(DA[:, HALF:HALF + P], ch(nT, c), rbuf[:, j, :], start=True, stop=True).then_inc(s.v_done, 1)
                pieces(pe, h, 15 + 2 * c, 16 + 2 * c)
                pe.wait_ge(s.v_copied, 1 + 8 * g + c + 1)
                if c == 0:
                    pe.wait_ge(s.kd_done, 1 + g + 1)
                pe.matmul(DB[:, 0:P], ch(kn, c), vnew[:, j, :], start=True, stop=True).then_inc(s.ds_done, 1)
                pe.matmul(DC[:, j * HALF:j * HALF + P], ch(x2, c), vnew[:, j, :], start=False, stop=True).then_inc(s.o_done, 1)
            pieces(pe, h, 30, 32)
            pe.wait_ge(s.o_scaled, 1 + g + 1)
            for c in range(TT):
                last = pe.transpose(ch(DA, c), ch(x1, c), k.ident[:, :])
            last.then_inc(s.o_turned, 1)

        def wait_half(act, h, n, f):
            if f == 0:
                act.wait_ge(s.half_done, 1 + 4 * h + n + 1)
            else:
                act.wait_ge(k.w_used, unit(h, n) + 1)

        def copy_proj(act, h, n, f):
            wait_half(act, h, n, f)
            src = PP[:, f * HALF:(f + 1) * HALF]
            b = 0 if n != 1 else 1
            if n < 3:
                if f == 0:
                    done = {0: 3 * h, 1: 3 * h - 1, 2: 3 * h + 1}[n]
                    act.wait_ge(s.conv_done, 1 + done) if not (isinstance(h, int) and done <= 0) else None
                act.activation(k.xpad[b][:, CONV - 1 + f * HALF:CONV - 1 + (f + 1) * HALF], src, ACT.Copy).then_inc(s.proj_read, 1)

        def silu_z(act, h, hb, f):
            wait_half(act, h, 3, f)
            act.wait_ge(s.o_gated, 1 + h - 1) if not (isinstance(h, int) and h < 2) else None
            act.activation(zT[hb][:, f * HALF:(f + 1) * HALF], PP[:, f * HALF:(f + 1) * HALF], ACT.Silu).then_inc(s.proj_read, 1)

        def silu(act, h, hb, n):
            act.wait_ge(s.conv_done, 1 + 3 * h + n + 1)
            act.activation(qkv[n][hb][:, :], qkv[n][hb][:, :], ACT.Silu).then_inc(s.silu_done, 1)

        def conv_tap(dve, h, hb, n, j, tile):
            b = 0 if n != 1 else 1
            out = qkv[n][hb][:, :]
            w = k.cw[:, bass.ds(j * 24 + tile, 1)]
            if j == 0:
                dve.wait_ge(s.proj_read, 1 + 8 * h + 2 * n + 2)
                dve.tensor_scalar(out, k.xpad[b][:, 0:SEQ], w, None, ALU.mult).then_inc(s.conv_step, 1)
            else:
                dve.wait_ge(s.conv_step, 1 + 9 * h + 3 * n + j)
                dve.scalar_tensor_tensor(out=out, in0=k.xpad[b][:, j:j + SEQ], scalar=w, in1=out,
                                         op0=ALU.mult, op1=ALU.add).then_inc(s.conv_step if j < 3 else s.conv_done, 1)

        def act_step(act, h, hb, g, b):
            if g is None:
                for n in range(4):
                    round_unit(k, act, unit_turn(h, n + 1), (base + n + 1) % 4, (base + n + 1) % 2)
                    for f in range(2):
                        if n < 3:
                            copy_proj(act, h, n, f)
                        else:
                            silu_z(act, h, hb, f)
                    if n < 3:
                        silu(act, h, hb, n)
                return
            hh = h is not None
            for i, (src, out) in enumerate(((DA, sqk), (DB, sqq))):
                act.wait_ge(s.turned, 1 + 3 * g + i + 1)
                if i == 0:
                    act.wait_ge(s.r_done, 1 + 8 * g)
                    act.wait_ge(s.o_done, 1 + 8 * g)
                act.activation(out[:, :], src[:, :], ACT.Square).then_inc(s.squared, 1)
            if hh:
                copy_proj(act, h, 0, 0)
                round_unit(k, act, unit_turn(h, 1), (base + 1) % 4, (base + 1) % 2)
            act.wait_ge(s.ssq_done, 1 + 2 * g + 2)
            act.wait_ge(s.rows_done, 1 + g)
            act.activation(st[:, :, :], st[:, :, :], ACT.Ln, bias=k.eps_rms[:, :]).then_inc(s.ln_done, 1)
            act.wait_ge(s.rows_done, 1 + g + 1)
            act.activation(kde[:, :], kde[:, :], ACT.Exp).then_inc(s.kde_done, 1)
            act.wait_ge(s.an_rows, 1 + g + 1)
            act.activation(sqk[:, :], DC[:, :], ACT.Exp).then_inc(s.an_exp, 1)
            act.wait_ge(s.x1_ready, 1 + g + 1)
            act.activation(x1[:, :], x1[:, :], ACT.Exp).then_inc(s.x1_exp, 1)
            act.wait_ge(s.aq_rows, 1 + g + 1)
            act.activation(sqq[:, :], DC[:, :], ACT.Exp).then_inc(s.aq_exp, 1)
            act.wait_ge(s.x2_ready, 1 + g + 1)
            act.activation(x2[:, :], x2[:, :], ACT.Exp).then_inc(s.x2_exp, 1)
            if hh:
                copy_proj(act, h, 0, 1)
            act.wait_ge(s.n_turned, 1 + g + 1)
            act.activation(no[:, :], DA[:, :], ACT.Copy).then_inc(s.off_copied, 1)
            if hh:
                round_unit(k, act, unit_turn(h, 2), (base + 2) % 4, (base + 2) % 2)
            for r in range(5):
                for j in range(2):
                    act.wait_ge(s.pw_done, 1 + 12 * g + 2 * r + j + 1)
                    if r == 0:
                        act.wait_ge(s.dt_init, 1 + g + 1)
                    if r < 4:
                        act.activation(pd[:, 4 * j:4 * j + 4, 0, :],
                                       DD[j][:, :].rearrange("p (c a n) -> p c a n", a=2, n=P)[:, :, 0, :],
                                       ACT.Copy).then_inc(s.pT_copied, 1)
                    act.activation(pw[:, j * HALF:(j + 1) * HALF], DC[:, j * HALF:(j + 1) * HALF], ACT.Copy).then_inc(s.p_copied, 1)
                if hh and r == 3:
                    copy_proj(act, h, 1, 0)
            if hh:
                silu(act, h, hb, 0)
            for j in range(2):
                act.wait_ge(s.d_turned, 1 + 2 * g + j + 1)
                act.wait_ge(s.pw_done, 1 + 12 * g + 12)
                act.activation(pw[:, j * HALF:(j + 1) * HALF], DD[j][:, 0:HALF], ACT.Copy).then_inc(s.d_copied, 1)
            for c in range(TT):
                j = c % 2
                act.wait_ge(s.v_done, 1 + 8 * g + c + 1)
                if c >= 2:
                    act.wait_ge(s.o_done, 1 + 8 * g + c - 1)
                act.activation(vnew[:, j, :], DA[:, HALF:HALF + P], ACT.Copy).then_inc(s.v_copied, 1)
                act.wait_ge(s.o_done, 1 + 8 * g + c + 1)
                if c == 0:
                    act.wait_ge(s.w_done, 1 + 2 * g + 2)
                act.activation(ch(x1, c), DC[:, j * HALF:j * HALF + P], ACT.Copy).then_inc(s.o_copied, 1)
                if hh:
                    if c == 0:
                        copy_proj(act, h, 1, 1)
                        round_unit(k, act, unit_turn(h, 3), (base + 3) % 4, (base + 3) % 2)
                    if c == 2:
                        copy_proj(act, h, 2, 0)
                    if c == 4:
                        copy_proj(act, h, 2, 1)
                        silu(act, h, hb, 1)
                        round_unit(k, act, unit_turn(h, 4), base % 4, base % 2)
                    if c == 6:
                        silu_z(act, h, hb, 0)
            if hh:
                silu_z(act, h, hb, 1)
                silu(act, h, hb, 2)
            act.wait_ge(s.o_copied, 1 + 8 * g + 8)
            sq = pd[:, 0:4, :, :].rearrange("p c a n -> p (c a n)")
            act.wait_ge(s.t_done, 1 + 2 * g + 2)
            act.activation(sq, x1[:, :], ACT.Square).then_inc(s.o_squared, 1)
            act.wait_ge(s.o_ssq, 1 + g + 1)
            act.activation(orms[:, :], orms[:, :], ACT.Ln, scale=1.0 / P, bias=k.eps_rms[:, :]).then_inc(s.o_ln, 1)
            act.wait_ge(s.o_ln, 1 + g + 1)
            act.activation(orms[:, :], orms[:, :], ACT.Exp, scale=-0.5).then_inc(s.o_rs, 1)

        def dve_step(dve, h, hb, g, b, tq, tk, tv):
            if g is None:
                for n in range(4):
                    rest_unit(k, dve, unit(h, n + 1), (base + n + 1) % 4, (base + n + 1) % 2)
                    if n < 3:
                        for j in range(CONV):
                            conv_tap(dve, h, hb, n, j, (tq, tk, tv)[n])
                return
            hh = h is not None
            v3 = tiles
            dve.wait_ge(s.squared, 1 + 2 * g + 1)
            dve.wait_ge(s.ln_done, 1 + g)
            dve.reduce_sum(st[:, 0, :], v3(sqk[:, :]), AX_X).then_inc(s.ssq_done, 1)
            dve.wait_ge(s.squared, 1 + 2 * g + 2)
            dve.reduce_sum(st[:, 1, :], v3(sqq[:, :]), AX_X).then_inc(s.ssq_done, 1)
            dve.wait_ge(s.ds_done, 1 + 8 * g)
            dve.tensor_copy(kn[:, :], DB[:, :]).then_inc(s.kn_copied, 1)
            dve.wait_ge(s.turned, 1 + 3 * g + 3)
            dve.tensor_tensor(v3(vb[:, :]), v3(DC[:, :]), bc(k.beta[:, g, :] if isinstance(g, int) else k.beta[:, bass.ds(g, 1), :].rearrange("p a b -> p (a b)"), P), ALU.mult).then_inc(s.vb_done, 1)

            def row(t):
                return t[:, bass.ds(g, 1), :].rearrange("p a b -> p (a b)")
            dve.wait_ge(s.ln_done, 1 + g + 1)
            dve.scalar_tensor_tensor(out=rowA[:, :], in0=st[:, 1, :], scalar=-0.5, in1=row(k.gl), op0=ALU.mult, op1=ALU.add)
            dve.scalar_tensor_tensor(out=rowQ[:, :], in0=st[:, 0, :], scalar=-0.5, in1=row(k.gs), op0=ALU.mult, op1=ALU.add)
            dve.wait_ge(s.kd_done, 1 + g)
            dve.scalar_tensor_tensor(out=colB[:, :], in0=st[:, 1, :], scalar=-0.5, in1=row(k.gam), op0=ALU.mult, op1=ALU.subtract).then_inc(k.colb, 1)
            dve.wait_ge(k.colb, g + 1)
            dve.tensor_tensor(kde[:, :], colB[:, :], row(k.gtot), ALU.add).then_inc(s.rows_done, 1)
            if hh:
                rest_unit(k, dve, unit(h, 1), (base + 1) % 4, (base + 1) % 2)
            dve.wait_ge(s.an_exp, 1 + g + 1)
            dve.wait_ge(s.o_turned, 1 + g)
            for c in range(TT):
                last = dve.scalar_tensor_tensor(out=ch(x1, c), in0=ch(DC, c), scalar=colB[:, c:c + 1], in1=k.neg_strict[:, :],
                                                op0=ALU.add, op1=ALU.add)
            last.then_inc(s.x1_ready, 1)
            dve.wait_ge(s.x1_exp, 1 + g + 1)
            dve.wait_ge(s.kk_done, 1 + g + 1)
            dve.wait_ge(s.v_done, 1 + 8 * g)
            dve.scalar_tensor_tensor(out=nT[:, :], in0=DA[:, :], scalar=-1.0, in1=x1[:, :], op0=ALU.mult, op1=ALU.mult).then_inc(s.nT_done, 1)
            dve.wait_ge(s.aq_exp, 1 + g + 1)
            dve.wait_ge(s.o_done, 1 + 8 * g)
            for c in range(TT):
                last = dve.scalar_tensor_tensor(out=ch(x2, c), in0=ch(DC, c), scalar=colB[:, c:c + 1], in1=k.neg_incl[:, :],
                                                op0=ALU.add, op1=ALU.add)
            last.then_inc(s.x2_ready, 1)
            dve.wait_ge(s.nT_done, 1 + g + 1)
            dve.wait_ge(s.o_stored, 1 + 16 * g)
            dve.wait_ge(s.o_ssq, 1 + g)
            dve.tensor_tensor(pd[:, :, 0, :], v3(nT[:, :]), rep(k.same[:, :], TT), ALU.mult).then_inc(s.p0_done, 1)
            dve.wait_ge(s.off_copied, 1 + g + 1)
            dve.wait_ge(s.w_done, 1 + 2 * g)
            dve.tensor_tensor(v3(pw[:, :]), v3(DA[:, :]), rep(k.same[:, :], TT), ALU.mult).then_inc(s.p0_done, 1)
            dve.wait_ge(s.x2_exp, 1 + g + 1)
            dve.wait_ge(s.qk_done, 1 + g + 1)
            dve.tensor_tensor(x2[:, :], DB[:, :], x2[:, :], ALU.mult).then_inc(s.qk_decayed, 1)
            if hh:
                rest_unit(k, dve, unit(h, 2), (base + 2) % 4, (base + 2) % 2)
            for r in range(6):
                if hh and r < 4:
                    conv_tap(dve, h, hb, 0, r, tq)
                for j in range(2):
                    if r == 0:
                        continue
                    if r < 4:
                        dve.wait_ge(s.pT_copied, 1 + 8 * g + 2 * r + j + 1)
                    else:
                        dve.wait_ge(s.pw_done, 1 + 12 * g + 2 * r + j + 1)
                    dt = pd[:, 4 * j:4 * j + 4, 1, :]
                    if r == 1:
                        dve.wait_ge(s.dt_init, 1 + g + 1)
                    else:
                        dve.wait_ge(s.dT_added, 1 + 10 * g + 2 * (r - 2) + j + 1)
                    dve.tensor_tensor(dt, DD[j][:, :].rearrange("p (c a n) -> p c a n", a=2, n=P)[:, :, 1, :], dt,
                                      ALU.add).then_inc(s.dT_added, 1)
            for j in range(2):
                dve.wait_ge(s.z_done, 1 + 2 * g + j + 1)
                dve.tensor_copy(x1[:, j * HALF:(j + 1) * HALF], DC[:, j * HALF:(j + 1) * HALF]).then_inc(s.z_copied, 1)
            for j in range(2):
                dve.wait_ge(s.w_done, 1 + 2 * g + j + 1)
                dve.tensor_tensor(v3(nT[:, j * HALF:(j + 1) * HALF]), v3(DD[j][:, HALF:2 * HALF]), pd[:, 4 * j:4 * j + 4, 1, :],
                                  ALU.add).then_inc(s.t_done, 1)
            for c in range(TT):
                j = c % 2
                dve.wait_ge(s.r_done, 1 + 8 * g + c + 1)
                if c >= 2:
                    dve.wait_ge(s.v_done, 1 + 8 * g + c - 1)
                dve.scalar_tensor_tensor(out=rbuf[:, j, :], in0=DA[:, 0:P], scalar=-1.0, in1=ch(vb, c), op0=ALU.mult,
                                         op1=ALU.add).then_inc(s.r_read, 1)
                dve.wait_ge(s.ds_done, 1 + 8 * g + c + 1)
                dve.wait_ge(s.o_done, 1 + 8 * g + c + 1)
                if c == 0:
                    dve.wait_ge(k.s_zero, g + 1)
                else:
                    dve.wait_ge(s.s_done, 1 + 8 * g + c)
                dve.scalar_tensor_tensor(out=S[:, :], in0=S[:, :], scalar=k.gtot_e[:, bass.ds(g, 1), c:c + 1].rearrange("p a b -> p (a b)"),
                                         in1=DB[:, 0:P], op0=ALU.mult, op1=ALU.add).then_inc(s.s_done, 1)
                if hh:
                    if c == 0:
                        rest_unit(k, dve, unit(h, 3), (base + 3) % 4, (base + 3) % 2)
                    if 1 <= c <= 4:
                        conv_tap(dve, h, hb, 1, c - 1, tk)
                    if c == 5:
                        rest_unit(k, dve, unit(h, 4), base % 4, base % 2)
                    if c >= 5:
                        conv_tap(dve, h, hb, 2, c - 5, tv)
            if hh:
                conv_tap(dve, h, hb, 2, 3, tv)
            dve.wait_ge(s.s_done, 1 + 8 * g + 8)
            dve.memset(S[:, :], 0.0).then_inc(k.s_zero, 1)
            dve.wait_ge(s.o_squared, 1 + g + 1)
            sq = pd[:, 0:4, :, :].rearrange("p c a n -> p (c a) n")
            dve.reduce_sum(orms[:, :], sq, AX_X).then_inc(s.o_ssq, 1)
            dve.wait_ge(s.o_rs, 1 + g + 1)
            dve.tensor_tensor(v3(x1[:, :]), v3(x1[:, :]), bc(orms[:, :], P), ALU.mult).then_inc(s.o_scaled, 1)
            dve.wait_ge(s.o_turned, 1 + g + 1)
            dve.scalar_tensor_tensor(out=pd[:, 4:8, :, :].rearrange("p c a n -> p (c a n)"), in0=DA[:, :], scalar=k.dn_g[:, :],
                                     in1=zT[b][:, :], op0=ALU.mult, op1=ALU.mult).then_inc(s.o_gated, 1)

        def pool_step(pool, g, b):
            pool.wait_ge(s.kn_copied, 1 + g + 1)
            pool.wait_ge(s.kde_done, 1 + g + 1)
            pool.tensor_tensor(tiles(kn[:, :]), tiles(kn[:, :]), bc(kde[:, :], P), ALU.mult).then_inc(s.kd_done, 1)
            pool.wait_ge(s.p0_done, 1 + 2 * g + 1)
            pool.tensor_tensor(pd[:, :, 1, :], pd[:, :, 0, :], rep(k.ident[:, :], TT), ALU.add).then_inc(s.dt_init, 1)
            pool.wait_ge(s.off_copied, 1 + g + 1)
            pool.tensor_tensor(tiles(no[:, :]), tiles(no[:, :]), rep(k.other[:, :], TT), ALU.mult).then_inc(s.off_done, 1)
            pool.wait_ge(s.an_exp, 1 + g + 1)
            pool.tensor_tensor(sqk[:, :], sqk[:, :], kTt[b][:, :], ALU.mult).then_inc(s.kbg_done, 1)
            pool.wait_ge(s.aq_exp, 1 + g + 1)
            pool.tensor_tensor(sqq[:, :], sqq[:, :], qT[b][:, :], ALU.mult).then_inc(s.qd_done, 1)

        oa = pd[:, 4:8, :, :].rearrange("p c a n -> p (c a n)")
        w_in = a["w_in"][0]

        with nc.Block() as block:
            @block.sync
            def _(sync):
                for h in range(HEADS):
                    for n, col in enumerate((COL_K, COL_V, COL_Z, COL_Q)):
                        if n < 3:
                            load_unit(k, sync, unit(h, n + 1), columns(w_in, col + h * P))
                        elif h + 1 < HEADS:
                            load_unit(k, sync, unit(h, n + 1), columns(w_in, col + (h + 1) * P))
                        else:
                            load_unit(k, sync, unit(h, n + 1), k.next_unit)
                    if h:
                        sync.wait_ge(s.o_gated, 1 + h)
                        sync.dma_start(k.oaT[h - 1], oa).then_inc(s.o_stored, 16)
                sync.wait_ge(s.o_gated, 1 + HEADS)
                sync.dma_start(k.oaT[HEADS - 1], oa).then_inc(s.o_stored, 16)
                sync.wait_ge(s.o_stored, 1 + 16 * HEADS)

            @block.tensor
            def _(pe):
                pe_step(pe, 0, None, None)
                with pe.Fori(0, (HEADS - 2) // 2) as i:
                    for j in range(2):
                        pe_step(pe, 2 * i + 1 + j, 2 * i + j, j)
                pe_step(pe, HEADS - 1, HEADS - 2, 0)
                pe_step(pe, None, HEADS - 1, 1)

            @block.scalar
            def _(act):
                act_step(act, 0, 0, None, None)
                with act.Fori(0, (HEADS - 2) // 2) as i:
                    for j in range(2):
                        act_step(act, 2 * i + 1 + j, 1 - j, 2 * i + j, j)
                act_step(act, HEADS - 1, 1, HEADS - 2, 0)
                act_step(act, None, None, HEADS - 1, 1)

            @block.vector
            def _(dve):
                dve.memset(S[:, :], 0.0).then_inc(k.s_zero, 1)
                dve_step(dve, 0, 0, None, None, 0, 8, 16)
                with dve.Fori(0, (HEADS - 2) // 2) as i:
                    for j in range(2):
                        h = 2 * i + 1 + j
                        dve_step(dve, h, 1 - j, 2 * i + j, j, h, h + 8, h + 16)
                dve_step(dve, HEADS - 1, 1, HEADS - 2, 0, 7, 15, 23)
                dve_step(dve, None, None, HEADS - 1, 1, 0, 0, 0)

            @block.gpsimd
            def _(pool):
                with pool.Fori(0, HEADS // 2) as i:
                    for j in range(2):
                        pool_step(pool, 2 * i + j, j)
        clear_semaphores(nc, k)



def load(k, queue, u, ap):
    load_unit(k, queue, u, ap)


def split_act(k, act, u):
    round_unit(k, act, u, u % SPLIT_SLOTS, u % RAW_SLOTS)


def split_dve(k, dve, u):
    rest_unit(k, dve, u, u % SPLIT_SLOTS, u % RAW_SLOTS)


def product_half(k, pe, u, out, xh, xl, f, kt=KT, col=0, width=P, x0=None, n=HALF, part=None):
    x0 = f * HALF if x0 is None else x0
    slot = u % SPLIT_SLOTS
    ks = range(kt) if part is None else range(part * kt // 2, (part + 1) * kt // 2)
    for m in ks:
        c = m * width + col
        last = three(pe, out, k.whi[slot][:, c:c + P], k.wlo[slot][:, c:c + P],
                     xh[:, m, x0:x0 + n], xl[:, m, x0:x0 + n], m == 0, m == kt - 1)
    return last


def natural_unit(k, pe, u, banks, xh, xl, k0, k_last, done, rows=TT):
    slot = u % SPLIT_SLOTS
    for t in range(rows):
        for kk in range(2):
            m = k0 + kk
            lh, ll = xh[:, m, t * P:(t + 1) * P], xl[:, m, t * P:(t + 1) * P]
            wh, wl = k.whi[slot][:, kk * 512:(kk + 1) * 512], k.wlo[slot][:, kk * 512:(kk + 1) * 512]
            pe.matmul(banks[t], lh, wh, start=(m == 0), stop=False)
            pe.matmul(banks[t], lh, wl, start=False, stop=False)
            last = pe.matmul(banks[t], ll, wh, start=False, stop=(m == k_last))
        if done is not None and t < rows - 1:
            last.then_inc(done, 1)
    last.then_inc(k.w_used, 1)


def pair_columns(w, k0, c0):
    return w[k0 * P:(k0 + 2) * P, c0:c0 + 512].rearrange("(k p) n -> p k n", p=P)


def branch_a(nc, k, a, base):
    with ExitStack() as ctx:
        sb, sem = declare(nc, ctx, k)
        oah = sb("oah", [P, HEADS, SEQ], F32R)
        oal = sb("oal", [P, HEADS, SEQ], F32R)
        stage = [sb(f"oa_stage{i}", [P, SEQ]) for i in range(2)]
        ga = [sb(f"ga{i}", [P, SEQ]) for i in range(2)]
        gb = [sb(f"gb{i}", [P, SEQ]) for i in range(2)]
        ps = [ctx.enter_context(nc.psum_tensor(f"ba_ps{i}", [P, 1024], F32)) for i in range(4)]
        s = Names()
        s.oa_rounded = sem("ba_oa_rounded")
        s.oa_split = sem("ba_oa_split")
        s.ga_done = sem("ba_ga_done")
        s.gb_done = sem("ba_gb_done")
        s.gated = sem("ba_gated")
        oa_loaded = [sem(f"oa_loaded{i}") for i in range(2)]
        ga_stored = [sem(f"ga_stored{i}") for i in range(2)]
        gb_stored = [sem(f"gb_stored{i}") for i in range(2)]
        w_in, w_br = a["w_in"][0], a["w_br_a"][0]
        last_m = KT - 1

        def source(m, n):
            if n == 2:
                return w_br[:, bass.ds(m * P, P)].rearrange("(k p) n -> p k n", p=P)
            return w_in[:, bass.ds((COL_GA, COL_GB)[n] + m * P, P)].rearrange("(k p) n -> p k n", p=P)

        with nc.Block() as block:
            @block.sync
            def _(sync):
                for u in range(1, 3 * KT):
                    load_unit(k, sync, base + u, source(u // 3, u % 3))
                load_unit(k, sync, base + 3 * KT, k.next_unit)

            @block.gpsimd
            def _(pool):
                for h in range(HEADS):
                    if h >= 2:
                        pool.wait_ge(s.oa_split, h - 1)
                    pool.dma_start(stage[h % 2][:, :], k.oaT[h]).then_inc(oa_loaded[h % 2], 16)
                for m in range(KT):
                    pool.wait_ge(s.gb_done, m + 1)
                    pool.dma_start(k.gateB[m], gb[m % 2][:, :]).then_inc(gb_stored[m % 2], 16)
                    pool.wait_ge(s.gated, m + 1)
                    pool.dma_start(k.hA[m], ga[m % 2][:, :]).then_inc(ga_stored[m % 2], 16)
                for q in (*ga_stored, *gb_stored):
                    pool.wait_ge(q, 16 * (KT // 2))

            @block.tensor
            def _(pe):
                for u in range(3 * KT):
                    m, n = u // 3, u % 3
                    out = ps[u % 4]
                    pe.wait_ge(k.w_split, base + u + 1)
                    if u >= 4:
                        mm, nn = (u - 4) // 3, (u - 4) % 3
                        pe.wait_ge((s.ga_done, s.gb_done, s.gated)[nn], mm + 1)
                    if n == 2:
                        pe.wait_ge(s.oa_split, HEADS)
                    xh, xl = (oah, oal) if n == 2 else (k.xh, k.xl)
                    for f in range(2):
                        last = product_half(k, pe, base + u, out[:, f * HALF:(f + 1) * HALF], xh, xl, f)
                    last.then_inc(k.w_used, 1)

            @block.scalar
            def _(act):
                for h in range(HEADS):
                    if h == 4:
                        split_act(k, act, base + 1)
                    act.wait_ge(oa_loaded[h % 2], 16 * (h // 2 + 1))
                    act.activation(oah[:, h, :], stage[h % 2][:, :], ACT.Copy).then_inc(s.oa_rounded, 1)
                for u in range(3 * KT):
                    m, n = u // 3, u % 3
                    if u:
                        split_act(k, act, base + u + 1)
                    if n < 2:
                        act.wait_ge(k.w_used, base + u + 1)
                        if m >= 2:
                            act.wait_ge((ga_stored, gb_stored)[n][m % 2], 16 * (m // 2))
                        act.activation((ga, gb)[n][m % 2][:, :], ps[u % 4][:, :], ACT.Sigmoid).then_inc((s.ga_done, s.gb_done)[n], 1)

            @block.vector
            def _(dve):
                for h in range(HEADS):
                    if h == 4:
                        split_dve(k, dve, base + 1)
                    dve.wait_ge(s.oa_rounded, h + 1)
                    dve.tensor_tensor(oal[:, h, :], stage[h % 2][:, :], oah[:, h, :].bitcast(F32), ALU.subtract).then_inc(s.oa_split, 1)
                for u in range(3 * KT):
                    m, n = u // 3, u % 3
                    if u:
                        split_dve(k, dve, base + u + 1)
                    if n == 2:
                        dve.wait_ge(k.w_used, base + u + 1)
                        dve.wait_ge(s.ga_done, m + 1)
                        dve.tensor_tensor(ga[m % 2][:, :], ps[u % 4][:, :], ga[m % 2][:, :], ALU.mult).then_inc(s.gated, 1)
        clear_semaphores(nc, k)


TWO_PI = 2.0 * math.pi
PI_1 = 6.28125
PI_2 = float(np.float32(TWO_PI - PI_1))
PI_3 = TWO_PI - PI_1 - PI_2
ROUND = 1.5 * 2.0 ** 23
PI_MAX = 3.1415925


def by_residue(ap, g):
    r = DILATIONS[g]
    return ap.rearrange("p (l r) -> p r l", r=r)


def attention(nc, k, a, base):
    with ExitStack() as ctx:
        sb, sem = declare(nc, ctx, k)
        cosT, sinT = sb("cosT", [P, SEQ]), sb("sinT", [P, SEQ])
        V = [sb(f"V{g}", [P, TT, P]) for g in range(GROUPS)]
        pr = [sb("pr0", [P, TT, 2 * P]), sb("pr1", [P, TT, 2 * P]), sb("pr2", [P, TT, P])]
        q = sb("q", [P, SEQ])
        kk = sb("k", [P, P + SEQ])
        A = sb("turn", [P, SEQ])
        SW = sb("swap", [P, SEQ])
        pT = sb("pT", [P, 2, HALF])
        OT = sb("OT", [P, SEQ])
        mask = sb("mask", [P, 2, 2 * P])
        mask2 = sb("mask2", [P, P])
        freq, sign = sb("freq", [P, 1]), sb("sign", [P, 1])
        mx = sb("mx", [P, 4])
        st = sb("st", [P, GROUPS, TT, 2])
        R = sb("R", [P, GROUPS * TT, GROUPS, 2])
        low = sb("low", [P, GROUPS * TT])
        ex = sb("ex", [P, GROUPS * TT, GROUPS])
        lw = sb("lw", [P, GROUPS * TT, GROUPS])
        coef = sb("coef", [P, GROUPS * TT])
        PA = [ctx.enter_context(nc.psum_tensor(f"at_p{i}", [P, 1024], F32)) for i in range(2)]
        SA = ctx.enter_context(nc.psum_tensor("SA", [P, 1024], F32))
        SB = ctx.enter_context(nc.psum_tensor("SB", [P, 1024], F32))
        s = Names()
        s.masks = sem("at_masks")
        s.pos_loaded = sem("at_pos_loaded")
        s.trig = sem("at_trig")
        s.sin_done = sem("at_sin_done")
        s.swapped = sem("at_swapped")
        s.a_done = sem("at_a_done")
        s.sw_done = sem("at_sw_done")
        s.roped = sem("at_roped")
        s.v_read = sem("at_v_read")
        s.v_turned = sem("at_v_turned")
        s.v_copied = sem("at_v_copied")
        s.s_scores = sem("at_s_scores")
        s.s_masked = sem("at_s_masked")
        s.mx_done = sem("at_mx_done")
        s.nm_done = sem("at_nm_done")
        s.exp_done = sem("at_exp_done")
        s.stat_stored = sem("at_stat_stored")
        s.stat_loaded = sem("at_stat_loaded")
        s.stat_step = sem("at_stat_step")
        s.ex_done = sem("at_ex_done")
        s.coef_done = sem("at_coef_done")
        s.scaled = sem("at_scaled")
        s.p_turned = sem("at_p_turned")
        s.own_copied = sem("at_own_copied")
        s.prev_copied = sem("at_prev_copied")
        s.pv_done = sem("at_pv_done")
        s.o_added = sem("at_o_added")
        s.ob_rounded = sem("at_ob_rounded")
        s.ob_split = sem("at_ob_split")
        stat_put = [sem(f"stat_put{g}") for g in range(GROUPS)]
        w_in = a["w_in"][0]
        scale = float(P) ** -0.5
        UN = 3 * GROUPS

        def source(u):
            hh, g, n = u // UN, (u % UN) // 3, u % 3
            return columns(w_in, (COL_BQ, COL_BK, COL_BV)[n] + (g * HG + hh) * P)

        def rope_no(hh, g, n):
            return 6 * hh + 2 * g + n

        def it(hh, g):
            return 3 * hh + g

        with nc.Block() as block:
            @block.sync
            def _(sync):
                sync.dma_start(OT[:, :].bitcast(I32), a["positions"].partition_broadcast(P)).then_inc(s.pos_loaded, 16)
                sync.dma_start(freq[:, :], a["rope_freq"]).then_inc(s.pos_loaded, 16)
                for u in range(1, UN * HG):
                    load_unit(k, sync, base + u, source(u))
                load_unit(k, sync, base + UN * HG, k.next_unit)

            @block.gpsimd
            def _(pool):
                pool.memset(mask[:, :, :], 0.0).then_inc(s.masks, 1)
                pool.memset(mask2[:, :], 0.0).then_inc(s.masks, 1)
                pool.memset(kk[:, 0:P], 0.0).then_inc(s.masks, 1)
                pool.memset(sign[:, :], 1.0).then_inc(s.masks, 1)
                pool.wait_ge(s.masks, 4)
                pool.memset(sign[0:64, :], -1.0).then_inc(s.masks, 1)
                pool.wait_ge(s.masks, 5)
                pool.memset(mask[:, 0, 0:P], NEG).then_inc(s.masks, 1)
                pool.affine_select(out=mask[:, 1, 0:P], in_=mask[:, 1, 0:P], compare_op=ALU.is_ge, fill=NEG,
                                   base=0, pattern=[[1, P]], channel_multiplier=-1).then_inc(s.masks, 1)
                for m in (mask[:, 0, P:2 * P], mask[:, 1, P:2 * P], mask2[:, :]):
                    pool.affine_select(out=m, in_=m, compare_op=ALU.is_ge, fill=NEG,
                                       base=0, pattern=[[-1, P]], channel_multiplier=1).then_inc(s.masks, 1)
                pool.wait_ge(s.masks, 10)
                pool.memset(mask2[64:P, 0:64], NEG).then_inc(s.masks, 1)

                for hh in range(HG):
                    for g in range(GROUPS):
                        for n in range(2):
                            i = rope_no(hh, g, n)
                            pool.wait_ge(s.swapped, 2 * (i + 1))
                            if i == 0:
                                pool.wait_ge(s.masks, 11)
                                pool.wait_ge(s.sin_done, 2)
                            pool.tensor_tensor(SW[:, :], SW[:, :], sinT[:, :], ALU.mult).then_inc(s.sw_done, 1)
                        pool.wait_ge(s.exp_done, 8 * (it(hh, g) + 1))
                        dst = k.stats[hh]
                        if g == 0:
                            pool.dma_start(dst.rearrange("(b p) g c -> p b g c", p=P)[:, :, 0, :], st[:, 0, :, :]).then_inc(stat_put[g], 16)
                        elif g == 1:
                            v = dst.rearrange("(h p r) g c -> p r h g c", h=2, r=4)
                            for r in range(4):
                                pool.dma_start(v[:, r, :, 1, :], st[:, 1, 2 * r:2 * r + 2, :]).then_inc(stat_put[g], 16)
                        else:
                            v = dst.rearrange("(l b s) g c -> s l b g c", b=8, s=2)
                            for half in range(2):
                                pool.dma_start(v[half, :, :, 2, :], st[64 * half:64 * half + 64, 2, :, :]).then_inc(stat_put[g], 16)
                    pool.wait_ge(stat_put[0], 16 * (hh + 1))
                    pool.wait_ge(stat_put[1], 64 * (hh + 1))
                    pool.wait_ge(stat_put[2], 32 * (hh + 1))
                    if hh:
                        pool.wait_ge(s.coef_done, 2 * hh)
                    src = k.stats[hh]
                    Rv = R[:, :, :, :].rearrange("p n g c -> p n (g c)")
                    pool.dma_start(Rv[:, 0:8, :], src.rearrange("(b p) g c -> p b (g c)", p=P)).then_inc(s.stat_loaded, 16)
                    v = src.rearrange("(h p r) g c -> p r h (g c)", h=2, r=4)
                    for r in range(4):
                        pool.dma_start(Rv[:, 8 + 2 * r:10 + 2 * r, :], v[:, r, :, :]).then_inc(s.stat_loaded, 16)
                    v = src.rearrange("(l b s) g c -> s l b (g c)", b=8, s=2)
                    for half in range(2):
                        pool.dma_start(Rv[64 * half:64 * half + 64, 16:24, :], v[half]).then_inc(s.stat_loaded, 16)

            @block.tensor
            def _(pe):
                def half(u, f):
                    out = PA[u % 2]
                    if f == 0:
                        pe.wait_ge(k.w_split, base + u + 1)
                        if u >= 2:
                            hh, g, n = (u - 2) // UN, ((u - 2) % UN) // 3, (u - 2) % 3
                            if n < 2:
                                pe.wait_ge(s.a_done, rope_no(hh, g, n) + 1)
                            else:
                                pe.wait_ge(s.v_read, it(hh, g) + 1)
                    last = product_half(k, pe, base + u, out[:, f * HALF:(f + 1) * HALF], k.xh, k.xl, f)
                    if f == 1:
                        last.then_inc(k.w_used, 1)

                def scores(hh, g, j):
                    out = (SA, SB)[j]
                    if j == 0:
                        pe.wait_ge(s.roped, rope_no(hh, g, 1) + 1)
                        if hh:
                            pe.wait_ge(s.o_added, it(hh - 1, g) + 1)
                    else:
                        if hh:
                            pe.wait_ge(s.prev_copied, 6 * (hh - 1) + 2 * g + 2)
                            pe.wait_ge(s.own_copied, 6 * (hh - 1) + 2 * g + 2)
                    i = it(hh, g)
                    if i:
                        pe.wait_ge(s.s_masked, 2 * (i - 1) + j + 1)
                        if j == 0:
                            pe.wait_ge(s.v_copied, i)
                    for i in range(4):
                        b = 4 * j + i
                        if g < 2:
                            last = pe.matmul(out[:, i * 256:(i + 1) * 256], q[:, b * P:(b + 1) * P],
                                             kk[:, b * P:(b + 2) * P], start=True, stop=True)
                        else:
                            last = pe.matmul(out[:, i * P:(i + 1) * P], q[:, b * P:(b + 1) * P],
                                             kk[:, (b + 1) * P:(b + 2) * P], start=True, stop=True)
                    last.then_inc(s.s_scores, 1)

                def turn_v(hh, g):
                    pe.wait_ge(s.v_read, it(hh, g) + 1)
                    pe.wait_ge(s.s_masked, 2 * it(hh, g) + 1)
                    for b in range(TT):
                        last = pe.transpose(SA[:, b * P:(b + 1) * P], A[:, b * P:(b + 1) * P], k.ident[:, :])
                    last.then_inc(s.v_turned, 1)

                def turn_p(hh, g, j):
                    if j == 0:
                        pe.wait_ge(s.scaled, it(hh, g) + 1)
                        pe.wait_ge(s.s_masked, 2 * min(it(hh + 1, g), 3 * HG))
                    if 6 * hh + 2 * g + j:
                        pe.wait_ge(s.own_copied, 6 * hh + 2 * g + j)
                        pe.wait_ge(s.prev_copied, 6 * hh + 2 * g + j)
                    for i in range(4):
                        b = 4 * j + i
                        own = pr[g][:, b, P:2 * P] if g < 2 else pr[g][:, b, :]
                        last = pe.transpose(SB[:, i * P:(i + 1) * P], own, k.ident[:, :])
                    if g < 2:
                        for i in range(4):
                            last = pe.transpose(SB[:, HALF + i * P:HALF + (i + 1) * P], pr[g][:, 4 * j + i, 0:P], k.ident[:, :])
                    last.then_inc(s.p_turned, 1)

                def has_prev(g, b):
                    return (g == 0 and b > 0) or (g == 1 and b % 2 == 1)

                def pv(hh, g, j):
                    n = 6 * hh + 2 * g + j + 1
                    pe.wait_ge(s.own_copied, n)
                    pe.wait_ge(s.prev_copied, n)
                    pe.wait_ge(s.v_copied, it(hh + 1, g) if hh + 1 < HG else 3 * HG)
                    if j == 0 and it(hh, g):
                        pe.wait_ge(s.o_added, it(hh, g))
                    for i in range(4):
                        b = 4 * j + i
                        out = SA[:, b * P:(b + 1) * P]
                        last = pe.matmul(out, V[g][:, b, :], pT[:, 0, i * P:(i + 1) * P], start=True, stop=not has_prev(g, b))
                        if has_prev(g, b):
                            last = pe.matmul(out, V[g][:, b - 1, :], pT[:, 1, i * P:(i + 1) * P], start=False, stop=True)
                    last.then_inc(s.pv_done, 1)

                for hh in range(HG):
                    for g in range(GROUPS):
                        u = UN * hh + 3 * g
                        half(u, 0)
                        if u:
                            turn_v(*((hh, g - 1) if g else (hh - 1, 2)))
                        half(u, 1)
                        if hh:
                            turn_p(hh - 1, g, 0)
                        half(u + 1, 0)
                        if hh:
                            pv(hh - 1, g, 0)
                            turn_p(hh - 1, g, 1)
                        half(u + 1, 1)
                        if hh:
                            pv(hh - 1, g, 1)
                        half(u + 2, 0)
                        scores(hh, g, 0)
                        half(u + 2, 1)
                        scores(hh, g, 1)
                turn_v(HG - 1, 2)
                for g in range(GROUPS):
                    for j in range(2):
                        turn_p(HG - 1, g, j)
                        pv(HG - 1, g, j)

            @block.scalar
            def _(act):
                def copy_p(hh, g, j):
                    n = 6 * hh + 2 * g + j
                    act.wait_ge(s.p_turned, n + 1)
                    if n:
                        act.wait_ge(s.pv_done, n)
                    act.activation(pT[:, 0, :], SB[:, 0:HALF], ACT.Copy).then_inc(s.own_copied, 1)

                def read_v(hh, g, u):
                    act.wait_ge(k.w_used, base + u + 1)
                    i = rope_no(hh, g, 1) + 1
                    act.wait_ge(s.roped, i)
                    act.activation(A[:, :].rearrange("p (r l) -> p r l", r=DILATIONS[g]), by_residue(PA[u % 2][:, :], g),
                                   ACT.Copy).then_inc(s.v_read, 1)

                act.wait_ge(s.trig, 17)
                act.wait_ge(s.masks, 5)
                act.activation(sinT[:, :], sinT[:, :], ACT.Sin, scale=sign[:, :]).then_inc(s.sin_done, 1)
                act.activation(cosT[:, :], cosT[:, :], ACT.Sin).then_inc(s.sin_done, 1)
                for hh in range(HG):
                    for g in range(GROUPS):
                        u0 = UN * hh + 3 * g
                        for n in range(2):
                            u = u0 + n
                            split_act(k, act, base + u + 1)
                            if hh and n == 1:
                                copy_p(hh - 1, g, 0)
                            act.wait_ge(k.w_used, base + u + 1)
                            if rope_no(hh, g, n):
                                act.wait_ge(s.roped, rope_no(hh, g, n))
                            act.activation(SW[0:64, :], PA[u % 2][64:P, :], ACT.Copy).then_inc(s.swapped, 1)
                            act.activation(SW[64:P, :], PA[u % 2][0:64, :], ACT.Copy).then_inc(s.swapped, 1)
                            if n == 0 and hh and g == 0:
                                act.wait_ge(s.stat_step, 3 * hh)
                                act.activation(ex[:, :, :], ex[:, :, :], ACT.Exp).then_inc(s.ex_done, 1)
                            if hh and n == 1:
                                copy_p(hh - 1, g, 1)
                        split_act(k, act, base + u0 + 3)
                        read_v(hh, g, u0 + 2)
                        if hh:
                            pass
                        for j in range(2):
                            act.wait_ge(s.nm_done, 2 * it(hh, g) + j + 1)
                            if hh and j == 0:
                                act.wait_ge(stat_put[g], (16, 64, 32)[g] * hh)
                            for b in range(4 * j, 4 * j + 4):
                                w = pr[g][:, b, :]
                                act.activation(w, w, ACT.Exp, scale=scale, bias=st[:, g, b, 0:1],
                                               accum_out=st[:, g, b, 1:2]).then_inc(s.exp_done, 1)
                        if hh:
                            if g == 2:
                                act.wait_ge(s.o_added, 3 * hh)
                                act.activation(k.obh[:, hh - 1, :], OT[:, :], ACT.Copy).then_inc(s.ob_rounded, 1)
                act.wait_ge(s.stat_step, 3 * HG)
                act.activation(ex[:, :, :], ex[:, :, :], ACT.Exp).then_inc(s.ex_done, 1)
                for g in range(GROUPS):
                    copy_p(HG - 1, g, 0)
                    copy_p(HG - 1, g, 1)
                act.wait_ge(s.o_added, 3 * HG)
                act.activation(k.obh[:, HG - 1, :], OT[:, :], ACT.Copy).then_inc(s.ob_rounded, 1)

            @block.vector
            def _(dve):
                count = [0]

                def trig(ins):
                    ins.then_inc(s.trig, 1)
                    count[0] += 1
                    dve.wait_ge(s.trig, count[0])

                dve.wait_ge(s.pos_loaded, 32)
                trig(dve.tensor_copy(A[:, :], OT[:, :].bitcast(I32)))
                trig(dve.tensor_scalar(A[:, :], A[:, :], freq[:, :], None, ALU.mult))
                for out, turn, off in ((sinT, 0.0, 0.0), (cosT, 0.25, 0.5 * math.pi)):
                    trig(dve.tensor_scalar(OT[:, :], A[:, :], 1.0 / TWO_PI, turn, ALU.mult, ALU.add))
                    trig(dve.tensor_scalar(OT[:, :], OT[:, :], ROUND, None, ALU.add))
                    trig(dve.tensor_scalar(OT[:, :], OT[:, :], -ROUND, None, ALU.add))
                    trig(dve.scalar_tensor_tensor(out=out[:, :], in0=OT[:, :], scalar=-PI_1, in1=A[:, :], op0=ALU.mult, op1=ALU.add))
                    trig(dve.scalar_tensor_tensor(out=out[:, :], in0=OT[:, :], scalar=-PI_2, in1=out[:, :], op0=ALU.mult, op1=ALU.add))
                    trig(dve.scalar_tensor_tensor(out=out[:, :], in0=OT[:, :], scalar=-PI_3, in1=out[:, :], op0=ALU.mult, op1=ALU.add))
                    if off:
                        trig(dve.tensor_scalar(out[:, :], out[:, :], off, None, ALU.add))
                for out in (sinT, cosT):
                    dve.tensor_scalar(out[:, :], out[:, :], PI_MAX, -PI_MAX, ALU.min, ALU.max).then_inc(s.trig, 1)

                def coefs(hh):
                    dve.wait_ge(s.stat_loaded, 112 * (hh + 1))
                    nm = [R[:, :, g, 0] for g in range(GROUPS)]
                    dve.tensor_tensor(low[:, :], nm[0], nm[1], ALU.min).then_inc(s.stat_step, 1)
                    dve.wait_ge(s.stat_step, 3 * hh + 1)
                    dve.tensor_tensor(low[:, :], low[:, :], nm[2], ALU.min).then_inc(s.stat_step, 1)
                    dve.wait_ge(s.stat_step, 3 * hh + 2)
                    dve.tensor_tensor(ex[:, :, :], bc(low[:, :], GROUPS), R[:, :, :, 0], ALU.subtract).then_inc(s.stat_step, 1)
                    dve.wait_ge(s.ex_done, hh + 1)
                    dve.tensor_tensor(lw[:, :, :], ex[:, :, :], R[:, :, :, 1], ALU.mult).then_inc(s.coef_done, 1)
                    dve.wait_ge(s.coef_done, 2 * hh + 1)
                    dve.reduce_sum(low[:, :], lw[:, :, :], AX_X).then_inc(k.chain, 1)
                    dve.wait_ge(k.chain, 2 * hh + 1)
                    dve.reciprocal(low[:, :], low[:, :]).then_inc(k.chain, 1)
                    dve.wait_ge(k.chain, 2 * hh + 2)
                    for g in range(GROUPS):
                        last = dve.tensor_tensor(coef[:, g * TT:(g + 1) * TT], ex[:, g * TT:(g + 1) * TT, g],
                                                 low[:, g * TT:(g + 1) * TT], ALU.mult)
                    last.then_inc(s.coef_done, 1)

                def scale_p(hh, g):
                    if g == 0:
                        dve.wait_ge(s.coef_done, 2 * hh + 2)
                    p = pr[g][:, :, :]
                    dve.tensor_tensor(p, p, bc(coef[:, g * TT:(g + 1) * TT], p.shape[2]), ALU.mult).then_inc(s.scaled, 1)

                def copy_prev(hh, g, j):
                    n = 6 * hh + 2 * g + j
                    dve.wait_ge(s.p_turned, n + 1)
                    if n:
                        dve.wait_ge(s.pv_done, n)
                    if g < 2:
                        dve.tensor_copy(pT[:, 1, :], SB[:, HALF:2 * HALF]).then_inc(s.prev_copied, 1)
                    else:
                        dve.nop().then_inc(s.prev_copied, 1)

                def add_o(hh, g):
                    dve.wait_ge(s.pv_done, 6 * hh + 2 * g + 2)
                    src = SA[:, :].rearrange("p (r l) -> p r l", r=DILATIONS[g])
                    if g == 0:
                        if hh:
                            dve.wait_ge(s.ob_rounded, hh)
                            dve.wait_ge(s.ob_split, hh)
                        dve.tensor_copy(OT[:, :], SA[:, :]).then_inc(s.o_added, 1)
                    else:
                        dve.wait_ge(s.o_added, it(hh, g))
                        o = by_residue(OT[:, :], g)
                        dve.tensor_tensor(o, src, o, ALU.add).then_inc(s.o_added, 1)

                def rest_o(hh):
                    dve.wait_ge(s.ob_rounded, hh + 1)
                    dve.tensor_tensor(k.obl[:, hh, :], OT[:, :], k.obh[:, hh, :].bitcast(F32), ALU.subtract).then_inc(s.ob_split, 1)

                def copy_v(hh, g):
                    dve.wait_ge(s.v_turned, it(hh, g) + 1)
                    if hh:
                        dve.wait_ge(s.pv_done, 6 * (hh - 1) + 2 * g + 2)
                    dve.tensor_copy(V[g][:, :, :], tiles(SA[:, :])).then_inc(s.v_copied, 1)

                for hh in range(HG):
                    for g in range(GROUPS):
                        u0 = UN * hh + 3 * g
                        for n in range(2):
                            u, i = u0 + n, rope_no(hh, g, n)
                            split_dve(k, dve, base + u + 1)
                            if n == 0 and u:
                                copy_v(*((hh, g - 1) if g else (hh - 1, 2)))
                            if hh and n == 0:
                                if g == 0:
                                    coefs(hh - 1)
                                scale_p(hh - 1, g)
                            if hh and n == 1:
                                copy_prev(hh - 1, g, 0)
                            dve.wait_ge(s.swapped, 2 * (i + 1))
                            if i == 0:
                                dve.wait_ge(s.sin_done, 2)
                            else:
                                dve.wait_ge(s.roped, i)
                                if n == 0:
                                    dve.wait_ge(s.v_turned, it(hh, g))
                            dve.tensor_tensor(A[:, :], PA[u % 2][:, :], cosT[:, :], ALU.mult).then_inc(s.a_done, 1)
                            dve.wait_ge(s.sw_done, i + 1)
                            dve.wait_ge(s.a_done, i + 1)
                            if it(hh, g):
                                dve.wait_ge(s.s_scores, 2 * it(hh, g))
                            if i == 0:
                                dve.wait_ge(s.masks, 11)
                            dst = (q[:, :], kk[:, P:P + SEQ])[n].rearrange("p (r l) -> p r l", r=DILATIONS[g])
                            dve.tensor_tensor(dst, by_residue(A[:, :], g), by_residue(SW[:, :], g), ALU.add).then_inc(s.roped, 1)
                            if hh and n == 1:
                                copy_prev(hh - 1, g, 1)
                        split_dve(k, dve, base + u0 + 3)
                        if hh:
                            add_o(hh - 1, g)
                        for j in range(2):
                            n = 2 * it(hh, g) + j
                            dve.wait_ge(s.s_scores, n + 1)
                            S = (SA, SB)[j]
                            if g == 2:
                                p = pr[g][:, 4 * j:4 * j + 4, :]
                                dve.tensor_tensor(p, tiles(S[:, 0:HALF]), rep(mask2[:, :], 4), ALU.add).then_inc(s.s_masked, 1)
                            elif g == 1:
                                p = pr[g][:, 4 * j:4 * j + 4, :]
                                p4 = p.rearrange("p (a b) n -> p a (b n)", b=2)
                                dve.tensor_tensor(p4, S[:, :].rearrange("p (a n) -> p a n", a=2),
                                                  rep(mask[:, :, :].rearrange("p b n -> p (b n)"), 2), ALU.add).then_inc(s.s_masked, 1)
                            else:
                                p = pr[g][:, 4 * j:4 * j + 4, :]
                                kind = 0 if j == 0 else 1
                                dve.tensor_tensor(p[:, 0, :], S[:, 0:256], mask[:, kind, :], ALU.add)
                                dve.tensor_tensor(p[:, 1:4, :], tiles(S[:, 256:1024], 256), rep(mask[:, 1, :], 3), ALU.add).then_inc(s.s_masked, 1)
                            dve.wait_ge(s.s_masked, n + 1)
                            if n:
                                dve.wait_ge(s.nm_done, n)
                            dve.reduce_max(mx[:, :], p, AX_X).then_inc(s.mx_done, 1)
                            dve.wait_ge(s.mx_done, n + 1)
                            if hh and j == 0:
                                dve.wait_ge(stat_put[g], (16, 64, 32)[g] * hh)
                            dve.tensor_scalar(st[:, g, 4 * j:4 * j + 4, 0], mx[:, :], -scale, None, ALU.mult).then_inc(s.nm_done, 1)
                        if hh and g == 2:
                            rest_o(hh - 1)
                copy_v(HG - 1, 2)
                coefs(HG - 1)
                for g in range(GROUPS):
                    scale_p(HG - 1, g)
                    copy_prev(HG - 1, g, 0)
                    copy_prev(HG - 1, g, 1)
                    add_o(HG - 1, g)
                rest_o(HG - 1)
        clear_semaphores(nc, k)


def merge(nc, k, a, base):
    with ExitStack() as ctx:
        sb, sem = declare(nc, ctx, k)
        ha = [sb(f"ha{i}", [P, SEQ]) for i in range(2)]
        gb = [sb(f"gbl{i}", [P, SEQ]) for i in range(2)]
        ps = [ctx.enter_context(nc.psum_tensor(f"mg_ps{i}", [P, 1024], F32)) for i in range(4)]
        s = Names()
        s.yb_done = sem("mg_yb_done")
        s.yb_gated = sem("mg_yb_gated")
        s.h_added = sem("mg_h_added")
        s.h_rounded = sem("mg_h_rounded")
        s.h_split = sem("mg_h_split")
        loaded = [sem(f"mg_loaded{i}") for i in range(2)]
        w = a["w_br_b"][0]

        with nc.Block() as block:
            @block.sync
            def _(sync):
                for i in range(1, 4):
                    load_unit(k, sync, base + i, w[:, 2 * i * P:2 * (i + 1) * P].rearrange("(k p) n -> p k n", p=P))
                load_unit(k, sync, base + 4, k.next_unit)

            @block.gpsimd
            def _(pool):
                for m in range(KT):
                    if m >= 2:
                        pool.wait_ge(s.h_split, m - 1)
                    pool.dma_start(ha[m % 2][:, :], k.hA[m]).then_inc(loaded[m % 2], 16)
                    pool.dma_start(gb[m % 2][:, :], k.gateB[m]).then_inc(loaded[m % 2], 16)

            @block.tensor
            def _(pe):
                for m in range(KT):
                    u = base + m // 2
                    if m % 2 == 0:
                        pe.wait_ge(k.w_split, u + 1)
                    if m >= 4:
                        pe.wait_ge(s.yb_gated, m - 3)
                    for f in range(2):
                        last = product_half(k, pe, u, ps[m % 4][:, f * HALF:(f + 1) * HALF], k.obh, k.obl, f,
                                            kt=HG, col=(m % 2) * P, width=2 * P)
                    last.then_inc(s.yb_done if m % 2 == 0 else k.w_used, 1)

            @block.scalar
            def _(act):
                for m in range(KT):
                    if m % 2 == 0:
                        split_act(k, act, base + m // 2 + 1)
                    act.wait_ge(s.h_added, m + 1)
                    act.activation(k.xh[:, m, :], gb[m % 2][:, :], ACT.Copy).then_inc(s.h_rounded, 1)

            @block.vector
            def _(dve):
                for m in range(KT):
                    if m % 2 == 0:
                        split_dve(k, dve, base + m // 2 + 1)
                        dve.wait_ge(s.yb_done, m // 2 + 1)
                    else:
                        dve.wait_ge(k.w_used, base + m // 2 + 1)
                    dve.wait_ge(loaded[m % 2], 32 * (m // 2 + 1))
                    g = gb[m % 2][:, :]
                    dve.tensor_tensor(g, ps[m % 4][:, :], g, ALU.mult).then_inc(s.yb_gated, 1)
                    dve.wait_ge(s.yb_gated, m + 1)
                    dve.tensor_tensor(g, g, ha[m % 2][:, :], ALU.add).then_inc(s.h_added, 1)
                    dve.wait_ge(s.h_rounded, m + 1)
                    dve.tensor_tensor(k.xl[:, m, :], g, k.xh[:, m, :].bitcast(F32), ALU.subtract).then_inc(s.h_split, 1)
        clear_semaphores(nc, k)


def project_and_norm(nc, k, name, base, w, inh, inl, residual, gain, bias, outh, outl, y_dram, gained):
    with ExitStack() as ctx:
        sb0, sem0 = declare(nc, ctx, k)

        def sb(n, *r):
            return sb0(name + n, *r)

        def sem(n):
            return sem0(name + n)
        X = sb("X", [P, TT, D_MODEL])
        if gained:
            g_row, b_row = sb("g_row", [P, D_MODEL]), sb("b_row", [P, D_MODEL])
            y = sb("y", [P, D_MODEL])
        gT, bT = sb("gT", [P, KT]), sb("bT", [P, KT])
        rows = sb("rows", [2 * KT, P])
        tmp = [sb(f"tmp{i}", [P, HALF]) for i in range(2)]
        bst, mv = sb("bst", [P, TT, 12]), sb("mv", [P, TT, 2])
        rs = sb("rs", [P, TT])
        ps = [ctx.enter_context(nc.psum_tensor(f"{name}ps{i}", [P, 512], F32)) for i in range(8)]
        s = Names()
        s.loaded = sem("loaded")
        s.rows_loaded = sem("rows_loaded")
        s.gain_loaded = sem("gain_loaded")
        s.bank_done = sem("bank_done")
        s.summed = sem("summed")
        s.sums_done = sem("sums_done")
        s.stats_done = sem("stats_done")
        s.rs_step = sem("rs_step")
        s.rs_done = sem("rs_done")
        s.normed = sem("normed")
        s.turned = sem("turned")
        s.gain_applied = sem("gain_applied")
        s.rounded = sem("rounded")
        s.split = sem("split")
        s.gT_turned = sem("gT_turned")
        s.gT_copied = sem("gT_copied")
        s.y_scaled = sem("y_scaled")
        s.y_done = sem("y_done")
        s.y_stored = sem("y_stored")
        NU = 8

        def wait_bank(eng, n, t):
            if t < TT - 1:
                eng.wait_ge(s.bank_done, (TT - 1) * n + t + 1)
            else:
                eng.wait_ge(k.w_used, base + 4 * n + 4)

        with nc.Block() as block:
            @block.sync
            def _(sync):
                for t in range(TT):
                    sync.dma_start(X[:, t, :], residual[t * P:(t + 1) * P, :]).then_inc(s.loaded, 16)
                if gained:
                    sync.dma_start(g_row[:, :], gain.partition_broadcast(P)).then_inc(s.gain_loaded, 16)
                    sync.dma_start(b_row[:, :], bias.partition_broadcast(P)).then_inc(s.gain_loaded, 16)
                sync.dma_start(rows[0:KT, :], gain.rearrange("l (m p) -> (l m) p", p=P)).then_inc(s.rows_loaded, 16)
                sync.dma_start(rows[KT:2 * KT, :], bias.rearrange("l (m p) -> (l m) p", p=P)).then_inc(s.rows_loaded, 16)
                for i in range(1, NU):
                    load_unit(k, sync, base + i, pair_columns(w, 2 * (i % 4), 512 * (i // 4)))
                load_unit(k, sync, base + NU, k.next_unit)
                for t in range(TT):
                    if gained:
                        sync.wait_ge(s.y_done, t + 1)
                    else:
                        sync.wait_ge(s.normed, t + 1)
                    sync.dma_start(y_dram[t * P:(t + 1) * P, :], y[:, :] if gained else X[:, t, :]).then_inc(s.y_stored, 16)
                sync.wait_ge(s.y_stored, 16 * TT)

            @block.tensor
            def _(pe):
                for n in range(2):
                    for i in range(4):
                        u = base + 4 * n + i
                        pe.wait_ge(k.w_split, u + 1)
                        if n == 1 and i == 0:
                            pe.wait_ge(s.summed, TT)
                        natural_unit(k, pe, u, [b[:, :] for b in ps], inh, inl, 2 * i, KT - 1, s.bank_done if i == 3 else None)
                pe.wait_ge(s.rows_loaded, 32)
                pe.wait_ge(s.summed, TT + 1)
                pe.transpose(ps[0][:, 0:2 * KT], rows[:, :], k.ident[0:2 * KT, 0:2 * KT]).then_inc(s.gT_turned, 1)
                n = 0
                for G in range(2):
                    pe.wait_ge(s.normed, 4 * (G + 1))
                    if G == 0:
                        pe.wait_ge(s.gT_copied, 1)
                        pe.wait_ge(s.summed, 2 * TT)
                    for m in range(KT):
                        if n >= 8:
                            pe.wait_ge(s.gain_applied, n - 7)
                        for t in range(4):
                            last = pe.transpose(ps[n % 8][:, t * P:(t + 1) * P], X[:, 4 * G + t, m * P:(m + 1) * P], k.ident[:, :])
                        last.then_inc(s.turned, 1)
                        n += 1

            @block.scalar
            def _(act):
                for i in range(NU):
                    split_act(k, act, base + i + 1)
                act.wait_ge(s.gT_turned, 1)
                act.activation(gT[:, :], ps[0][:, 0:KT], ACT.Copy)
                act.activation(bT[:, :], ps[0][:, KT:2 * KT], ACT.Copy).then_inc(s.gT_copied, 1)
                for t in range(TT):
                    act.wait_ge(s.stats_done, t + 1)
                    act.activation(rs[:, t:t + 1], mv[:, t, 1:2], ACT.Ln, bias=k.eps_ln[:, :]).then_inc(s.rs_step, 1)
                    act.wait_ge(s.rs_step, t + 1)
                    act.activation(rs[:, t:t + 1], rs[:, t:t + 1], ACT.Exp, scale=-0.5).then_inc(s.rs_done, 1)
                act.wait_ge(s.gT_copied, 1)
                for n in range(16):
                    G, m = n // 8, n % 8
                    act.wait_ge(s.turned, n + 1)
                    if n >= 2:
                        act.wait_ge(s.split, n - 1)
                    act.activation(tmp[n % 2][:, :], ps[n % 8][:, :], ACT.Identity, scale=gT[:, m:m + 1], bias=bT[:, m:m + 1]).then_inc(s.gain_applied, 1)
                    act.wait_ge(s.gain_applied, n + 1)
                    act.activation(outh[:, m, G * HALF:(G + 1) * HALF], tmp[n % 2][:, :], ACT.Copy).then_inc(s.rounded, 1)

            def norm(dve, t):
                dve.wait_ge(s.rs_done, t + 1)
                dve.tensor_scalar(X[:, t, :], X[:, t, :], mv[:, t, 0:1], rs[:, t:t + 1], ALU.subtract, ALU.mult).then_inc(s.normed, 1)

            @block.vector
            def _(dve):
                for i in range(NU):
                    split_dve(k, dve, base + i + 1)
                    if i % 4 == 3:
                        n = i // 4
                        for t in range(TT):
                            wait_bank(dve, n, t)
                            if n == 0 and t == 0:
                                dve.wait_ge(s.loaded, 16 * TT)
                            v = X[:, t, n * 512:(n + 1) * 512]
                            dve.scalar_tensor_tensor(out=v, in0=v, scalar=ALPHA, in1=ps[t][:, :], op0=ALU.mult, op1=ALU.add).then_inc(s.summed, 1)
                            if n == 1:
                                dve.wait_ge(s.summed, TT + t + 1)
                                for hn in range(2):
                                    dve.bn_stats(bst[:, t, 6 * hn:6 * hn + 6], X[:, t, hn * 512:(hn + 1) * 512]).then_inc(s.sums_done, 1)
                                dve.wait_ge(s.sums_done, 2 * t + 2)
                                dve.bn_aggr(mv[:, t, :], bst[:, t, :]).then_inc(s.stats_done, 1)
                                if t:
                                    norm(dve, t - 1)
                norm(dve, TT - 1)
                for n in range(16):
                    G, m = n // 8, n % 8
                    dve.wait_ge(s.rounded, n + 1)
                    dve.tensor_tensor(outl[:, m, G * HALF:(G + 1) * HALF], tmp[n % 2][:, :],
                                      outh[:, m, G * HALF:(G + 1) * HALF].bitcast(F32), ALU.subtract).then_inc(s.split, 1)

            @block.gpsimd
            def _(pool):
                if not gained:
                    return
                pool.wait_ge(s.gain_loaded, 32)
                for t in range(TT):
                    pool.wait_ge(s.normed, t + 1)
                    if t:
                        pool.wait_ge(s.y_stored, 16 * t)
                    pool.tensor_tensor(y[:, :], X[:, t, :], g_row[:, :], ALU.mult).then_inc(s.y_scaled, 1)
                    pool.wait_ge(s.y_scaled, t + 1)
                    pool.tensor_tensor(y[:, :], y[:, :], b_row[:, :], ALU.add).then_inc(s.y_done, 1)
        clear_semaphores(nc, k)


def cross_attention(nc, k, a, base, oh, ol):
    with ExitStack() as ctx:
        sb, sem = declare(nc, ctx, k)
        kT = sb("xkT", [P, KT, MEM])
        v = sb("xv", [P, 2, D_MODEL])
        pr = sb("xp", [P, 4, MEM])
        with ExitStack() as early:
            mh = early.enter_context(nc.sbuf_tensor("memh", [P, KT, MEM], F32R))
            ml = early.enter_context(nc.sbuf_tensor("meml", [P, KT, MEM], F32R))
        qT = sb("xqT", [P, 2, SEQ])
        pT = sb("xpT", [P, 2, HALF])
        mn = pr[:, :, :].rearrange("p a n -> p (a n)")
        mx, nm, l = sb("xmx", [P, 4]), sb("xnm", [P, 4]), sb("xl_", [P, 4])
        ps = [ctx.enter_context(nc.psum_tensor(f"x_ps{i}", [P, 1024], F32)) for i in range(4)]
        s = Names()
        s.m_turned = sem("ca_m_turned")
        s.m_rounded = sem("ca_m_rounded")
        s.m_split = sem("ca_m_split")
        s.k_copied = sem("ca_k_copied")
        s.v_bank = sem("ca_v_bank")
        s.v_copied = sem("ca_v_copied")
        s.q_copied = sem("ca_q_copied")
        s.x_scores = sem("ca_x_scores")
        s.x_max = sem("ca_x_max")
        s.x_nm = sem("ca_x_nm")
        s.x_exp = sem("ca_x_exp")
        s.x_rec = sem("ca_x_rec")
        s.x_norm = sem("ca_x_norm")
        s.x_turned = sem("ca_x_turned")
        s.x_copied = sem("ca_x_copied")
        s.x_pv = sem("ca_x_pv")
        s.x_rounded = sem("ca_x_rounded")
        s.x_split_o = sem("ca_x_split_o")
        m_loaded = sem("m_loaded")
        w_kv, w_q = a["w_xkv"][0], a["w_xq"][0]
        scale = float(XD) ** -0.5

        def source(i):
            if i < 8:
                return columns(w_kv, i * P)
            if i < 16:
                return pair_columns(w_kv, 2 * (i % 4), D_MODEL + 512 * ((i - 8) // 4))
            return columns(w_q, (i - 16) * P)

        with nc.Block() as block:
            @block.sync
            def _(sync):
                for t in range(2):
                    if t:
                        sync.wait_ge(s.m_turned, 2)
                    sync.dma_start(mn, a["mem"][0, t * P:(t + 1) * P, :]).then_inc(m_loaded, 16)
                for i in range(1, 24):
                    load_unit(k, sync, base + i, source(i))
                load_unit(k, sync, base + 24, k.next_unit)

            @block.tensor
            def _(pe):
                for t in range(2):
                    pe.wait_ge(m_loaded, 16 * (t + 1))
                    for f in range(2):
                        for i in range(4):
                            last = pe.transpose(ps[t][:, f * HALF + i * P:f * HALF + (i + 1) * P],
                                                mn[:, (4 * f + i) * P:(4 * f + i + 1) * P], k.ident[:, :])
                        last.then_inc(s.m_turned, 1)
                for i in range(8):
                    u = base + i
                    pe.wait_ge(k.w_split, u + 1)
                    if i == 0:
                        pe.wait_ge(s.m_split, 4)
                    if i >= 2:
                        pe.wait_ge(s.k_copied, i - 1)
                    product_half(k, pe, u, ps[2 + i % 2][:, 0:MEM], mh, ml, 0, x0=0, n=MEM).then_inc(k.w_used, 1)
                for n in range(2):
                    banks = [ps[n][:, 0:512], ps[n][:, 512:1024]]
                    for i in range(4):
                        u = base + 8 + 4 * n + i
                        pe.wait_ge(k.w_split, u + 1)
                        natural_unit(k, pe, u, banks, mh, ml, 2 * i, KT - 1, s.v_bank if i == 3 else None, rows=2)

                def query(h, d):
                    i = 2 * h + d
                    u = base + 16 + i
                    pe.wait_ge(k.w_split, u + 1)
                    if i >= 1:
                        pe.wait_ge(s.q_copied, 2 * i)
                    if i == 0:
                        pe.wait_ge(s.k_copied, 8)
                    for f in range(2):
                        last = product_half(k, pe, u, ps[3][:, f * HALF:(f + 1) * HALF], k.xh, k.xl, f)
                    last.then_inc(k.w_used, 1)

                def scores(h, j):
                    n = 2 * h + j
                    pe.wait_ge(s.q_copied, 4 * h + 4)
                    if n == 0:
                        pe.wait_ge(s.v_copied, 4)
                    if n:
                        pe.wait_ge(s.x_exp, 4 * n)
                    for i in range(4):
                        for d in range(2):
                            last = pe.matmul(ps[0][:, i * MEM:(i + 1) * MEM], qT[:, d, (4 * j + i) * P:(4 * j + i + 1) * P],
                                             kT[:, 2 * h + d, :], start=(d == 0), stop=(d == 1))
                    last.then_inc(s.x_scores, 1)

                def turn(h, j):
                    n = 2 * h + j
                    pe.wait_ge(s.x_norm, n + 1)
                    if n:
                        pe.wait_ge(s.x_copied, n)
                    for m in range(2):
                        for i in range(4):
                            last = pe.transpose(ps[1][:, m * HALF + i * P:m * HALF + (i + 1) * P], pr[:, i, m * P:(m + 1) * P], k.ident[:, :])
                    last.then_inc(s.x_turned, 1)

                def pv(h, j):
                    n = 2 * h + j
                    pe.wait_ge(s.x_copied, n + 1)
                    if n:
                        pe.wait_ge(s.x_split_o, n)
                    for d in range(2):
                        for m in range(2):
                            last = pe.matmul(ps[2][:, d * HALF:(d + 1) * HALF], v[:, m, (2 * h + d) * P:(2 * h + d + 1) * P],
                                             pT[:, m, :], start=(m == 0), stop=(m == 1))
                    last.then_inc(s.x_pv, 1)

                query(0, 0)
                query(0, 1)
                for h in range(XH):
                    scores(h, 0)
                    nxt = h + 1 < XH
                    pe.wait_ge(s.x_exp, 8 * h + 4)
                    turn(h, 0)
                    scores(h, 1)
                    if nxt:
                        pe.wait_ge(s.x_scores, 2 * h + 2)
                        query(h + 1, 0)
                    pv(h, 0)
                    turn(h, 1)
                    if nxt:
                        query(h + 1, 1)
                    pv(h, 1)

            @block.scalar
            def _(act):
                for n in range(4):
                    t, f = n // 2, n % 2
                    act.wait_ge(s.m_turned, n + 1)
                    act.activation(mh[:, 4 * f:4 * f + 4, t * P:(t + 1) * P], tiles(ps[t][:, f * HALF:(f + 1) * HALF]), ACT.Copy).then_inc(s.m_rounded, 1)
                for i in range(16):
                    split_act(k, act, base + i + 1)
                    if i < 8:
                        act.wait_ge(k.w_used, base + i + 1)
                        act.activation(kT[:, i, :], ps[2 + i % 2][:, 0:MEM], ACT.Copy).then_inc(s.k_copied, 1)
                    elif i % 4 == 3:
                        n = (i - 8) // 4
                        for t in range(2):
                            if t == 0:
                                act.wait_ge(s.v_bank, n + 1)
                            else:
                                act.wait_ge(k.w_used, base + i + 1)
                            act.activation(v[:, t, n * 512:(n + 1) * 512], ps[n][:, t * 512:(t + 1) * 512], ACT.Copy).then_inc(s.v_copied, 1)

                def copy_q(h, d):
                    i = 2 * h + d
                    if h:
                        act.wait_ge(s.x_scores, 2 * h)
                    act.wait_ge(k.w_used, base + 16 + i + 1)
                    for f in range(2):
                        act.activation(qT[:, d, f * HALF:(f + 1) * HALF], ps[3][:, f * HALF:(f + 1) * HALF], ACT.Copy).then_inc(s.q_copied, 1)

                def exps(h, j):
                    n = 2 * h + j
                    act.wait_ge(s.x_nm, n + 1)
                    if n:
                        act.wait_ge(s.x_turned, n)
                        act.wait_ge(s.x_norm, n)
                    for i in range(4):
                        act.activation(pr[:, i, :], ps[0][:, i * MEM:(i + 1) * MEM], ACT.Exp, scale=scale, bias=nm[:, i:i + 1],
                                       accum_out=l[:, i:i + 1]).then_inc(s.x_exp, 1)

                def round_o(h, j):
                    n = 2 * h + j
                    act.wait_ge(s.x_pv, n + 1)
                    act.activation(oh[:, 2 * h:2 * h + 2, j * HALF:(j + 1) * HALF], tiles(ps[2][:, :], HALF), ACT.Copy).then_inc(s.x_rounded, 1)

                split_act(k, act, base + 17)
                copy_q(0, 0)
                split_act(k, act, base + 18)
                copy_q(0, 1)
                for h in range(XH):
                    nxt = h + 1 < XH
                    exps(h, 0)
                    exps(h, 1)
                    if nxt:
                        split_act(k, act, base + 16 + 2 * h + 3)
                        copy_q(h + 1, 0)
                    round_o(h, 0)
                    if nxt:
                        split_act(k, act, base + 16 + 2 * h + 4)
                        copy_q(h + 1, 1)
                    round_o(h, 1)

            @block.vector
            def _(dve):
                for n in range(4):
                    t, f = n // 2, n % 2
                    dve.wait_ge(s.m_rounded, n + 1)
                    o = slice(4 * f, 4 * f + 4)
                    dve.tensor_tensor(ml[:, o, t * P:(t + 1) * P], tiles(ps[t][:, f * HALF:(f + 1) * HALF]),
                                      mh[:, o, t * P:(t + 1) * P].bitcast(F32), ALU.subtract).then_inc(s.m_split, 1)
                for i in range(16):
                    split_dve(k, dve, base + i + 1)

                def soft(h, j):
                    n = 2 * h + j
                    dve.wait_ge(s.x_scores, n + 1)
                    if n:
                        dve.wait_ge(s.x_nm, n)
                    dve.reduce_max(mx[:, :], tiles(ps[0][:, :], MEM), AX_X).then_inc(s.x_max, 1)
                    dve.wait_ge(s.x_max, n + 1)
                    if n:
                        dve.wait_ge(s.x_exp, 4 * n)
                    dve.tensor_scalar(nm[:, :], mx[:, :], -scale, None, ALU.mult).then_inc(s.x_nm, 1)
                    dve.wait_ge(s.x_exp, 4 * n + 4)
                    dve.reciprocal(l[:, :], l[:, :]).then_inc(s.x_rec, 1)
                    dve.wait_ge(s.x_rec, n + 1)
                    dve.tensor_tensor(pr[:, :, :], pr[:, :, :], bc(l[:, :], MEM), ALU.mult).then_inc(s.x_norm, 1)

                def copy_p(h, j):
                    n = 2 * h + j
                    dve.wait_ge(s.x_turned, n + 1)
                    if n:
                        dve.wait_ge(s.x_pv, n)
                    dve.tensor_copy(pT[:, :, :].rearrange("p a n -> p (a n)"), ps[1][:, :]).then_inc(s.x_copied, 1)

                def rest_o(h, j):
                    n = 2 * h + j
                    dve.wait_ge(s.x_rounded, n + 1)
                    o = slice(2 * h, 2 * h + 2)
                    dve.tensor_tensor(ol[:, o, j * HALF:(j + 1) * HALF], tiles(ps[2][:, :], HALF),
                                      oh[:, o, j * HALF:(j + 1) * HALF].bitcast(F32), ALU.subtract).then_inc(s.x_split_o, 1)

                split_dve(k, dve, base + 17)
                split_dve(k, dve, base + 18)
                for h in range(XH):
                    nxt = h + 1 < XH
                    soft(h, 0)
                    copy_p(h, 0)
                    soft(h, 1)
                    if nxt:
                        split_dve(k, dve, base + 16 + 2 * h + 3)
                    rest_o(h, 0)
                    copy_p(h, 1)
                    if nxt:
                        split_dve(k, dve, base + 16 + 2 * h + 4)
                    rest_o(h, 1)
        clear_semaphores(nc, k)


def feed_forward(nc, k, a, base, xh, xl, gh, gl, out):
    parts = (6, 6, 6, 4)
    with ExitStack() as ctx:
        sb, sem = declare(nc, ctx, k)
        X = sb("fX", [P, TT, D_MODEL])
        sa = sb("sa", [P, 2, HALF])
        row = sb("row", [P, HALF])
        bst, mv, rs = sb("fbst", [P, TT, 12]), sb("fmv", [P, TT, 2]), sb("frs", [P, TT])
        psall = [ctx.enter_context(nc.psum_tensor(f"f_ps{i}", [P, 1024], F32)) for i in range(4)]
        banks = [psall[i // 2][:, (i % 2) * 512:(i % 2 + 1) * 512] for i in range(8)]
        s = Names()
        s.f_loaded = sem("ff_f_loaded")
        s.f_res = sem("ff_f_res")
        s.silu_a = sem("ff_silu_a")
        s.prod = sem("ff_prod")
        s.rnd = sem("ff_rnd")
        s.rest = sem("ff_rest")
        s.bank_done = sem("ff_bank_done")
        s.y_added = sem("ff_y_added")
        s.f_stat = sem("ff_f_stat")
        s.f_stats = sem("ff_f_stats")
        s.f_ln = sem("ff_f_ln")
        s.f_rs = sem("ff_f_rs")
        s.f_norm = sem("ff_f_norm")
        s.f_gain = sem("ff_f_gain")
        s.f_out = sem("ff_f_out")
        rows_loaded = sem("f_rows")
        row_loaded = sem("f_row")
        stored = sem("f_stored")
        w13, w2 = a["w_ffn13"][0], a["w_ffn2"][0]

        plan = []
        f0 = 0
        for p, n in enumerate(parts):
            for f in range(n):
                plan += [("a", p, f0 + f, f), ("b", p, f0 + f, f)]
            for half in range(2):
                plan += [("y", p, f0 + 2 * i, (half, i)) for i in range(n // 2)]
            f0 += n
        NU = len(plan)

        def source(i):
            kind, p, f, x = plan[i]
            if kind == "y":
                return pair_columns(w2, f, 512 * x[0])
            return columns(w13, (0 if kind == "a" else D_FF) + f * P)

        ab_no = {i: f for i, (kind, p, f, x) in enumerate(plan) if kind != "y"}
        with nc.Block() as block:
            @block.sync
            def _(sync):
                for t in range(TT):
                    sync.dma_start(X[:, t, :], k.x2[t * P:(t + 1) * P, :]).then_inc(s.f_loaded, 16)
                for i in range(1, NU):
                    load_unit(k, sync, base + i, source(i))

            @block.tensor
            def _(pe):
                for i, (kind, p, f, x) in enumerate(plan):
                    u = base + i
                    pe.wait_ge(k.w_split, u + 1)
                    if kind != "y":
                        o = psall[2 * (f % 2) + (kind == "b")]
                        if x < 2:
                            if p:
                                pe.wait_ge(s.y_added, 16 * p)
                        else:
                            pe.wait_ge(s.silu_a if kind == "a" else s.prod, 2 * (f - 1))
                        for h in range(2):
                            last = product_half(k, pe, u, o[:, h * HALF:(h + 1) * HALF], xh, xl, h)
                        last.then_inc(k.w_used, 1)
                    else:
                        half, j = x
                        n = parts[p]
                        if j == 0:
                            if half == 0:
                                pe.wait_ge(s.rest, 2 * sum(parts[:p + 1]))
                            else:
                                pe.wait_ge(s.y_added, 16 * p + 8)
                        natural_unit(k, pe, u, banks, gh, gl, 2 * j, n - 1, s.bank_done if j == n // 2 - 1 else None)

            @block.scalar
            def _(act):
                for i, (kind, p, f, x) in enumerate(plan):
                    if i + 1 < NU:
                        split_act(k, act, base + i + 1)
                    if kind == "a":
                        act.wait_ge(k.w_used, base + i + 1)
                        for h in range(2):
                            if f:
                                act.wait_ge(s.rest, 2 * f + h - 1)
                            act.activation(sa[:, h, :], psall[2 * (f % 2)][:, h * HALF:(h + 1) * HALF], ACT.Silu).then_inc(s.silu_a, 1)
                    if kind == "b":
                        for h in range(2):
                            act.wait_ge(s.prod, 2 * f + h + 1)
                            act.activation(gh[:, x, h * HALF:(h + 1) * HALF], sa[:, h, :], ACT.Copy).then_inc(s.rnd, 1)
                for t in range(TT):
                    act.wait_ge(s.f_stats, t + 1)
                    act.activation(rs[:, t:t + 1], mv[:, t, 1:2], ACT.Ln, bias=k.eps_ln[:, :]).then_inc(s.f_ln, 1)
                    act.wait_ge(s.f_ln, t + 1)
                    act.activation(rs[:, t:t + 1], rs[:, t:t + 1], ACT.Exp, scale=-0.5).then_inc(s.f_rs, 1)

            def finish(dve, t):
                dve.wait_ge(s.f_rs, t + 1)
                dve.tensor_scalar(X[:, t, :], X[:, t, :], mv[:, t, 0:1], rs[:, t:t + 1], ALU.subtract, ALU.mult).then_inc(s.f_norm, 1)
                dve.wait_ge(s.f_norm, t + 1)
                if t == 0:
                    dve.wait_ge(rows_loaded, 32)
                dve.tensor_tensor(X[:, t, :], X[:, t, :], k.raw[0][:, :], ALU.mult).then_inc(s.f_gain, 1)

            @block.vector
            def _(dve):
                for i, (kind, p, f, x) in enumerate(plan):
                    if i + 1 < NU:
                        split_dve(k, dve, base + i + 1)
                    if kind == "b":
                        dve.wait_ge(k.w_used, base + i + 1)
                        for h in range(2):
                            dve.wait_ge(s.silu_a, 2 * f + h + 1)
                            dve.tensor_tensor(sa[:, h, :], psall[2 * (f % 2) + 1][:, h * HALF:(h + 1) * HALF], sa[:, h, :],
                                              ALU.mult).then_inc(s.prod, 1)
                        for h in range(2):
                            o = slice(h * HALF, (h + 1) * HALF)
                            dve.wait_ge(s.rnd, 2 * f + h + 1)
                            dve.tensor_tensor(gl[:, x, o], sa[:, h, :], gh[:, x, o].bitcast(F32), ALU.subtract).then_inc(s.rest, 1)
                    if kind == "y" and x[1] == parts[p] // 2 - 1:
                        half = x[0]
                        for t in range(TT):
                            if t < TT - 1:
                                dve.wait_ge(s.bank_done, (TT - 1) * (2 * p + half) + t + 1)
                            else:
                                dve.wait_ge(k.w_used, base + i + 1)
                            v = X[:, t, half * 512:(half + 1) * 512]
                            if p:
                                if t == 0:
                                    dve.wait_ge(s.y_added, 16 * p)
                                dve.tensor_tensor(v, banks[t], v, ALU.add).then_inc(s.y_added, 1)
                            else:
                                if t == 0:
                                    dve.wait_ge(s.f_res, 4 * TT)
                                dve.scalar_tensor_tensor(out=v, in0=v, scalar=ALPHA, in1=banks[t], op0=ALU.mult, op1=ALU.add).then_inc(s.y_added, 1)
                            if p == len(parts) - 1 and half == 1:
                                dve.wait_ge(s.y_added, 16 * p + 8 + t + 1)
                                for hn in range(2):
                                    dve.bn_stats(bst[:, t, 6 * hn:6 * hn + 6], X[:, t, hn * 512:(hn + 1) * 512]).then_inc(s.f_stat, 1)
                                dve.wait_ge(s.f_stat, 2 * t + 2)
                                dve.bn_aggr(mv[:, t, :], bst[:, t, :]).then_inc(s.f_stats, 1)
                                if t:
                                    finish(dve, t - 1)
                finish(dve, TT - 1)

            @block.gpsimd
            def _(pool):
                pool.wait_ge(s.f_loaded, 16 * TT)
                for i in range(4):
                    h, what = i // 2, (a["ln2_g"], a["ln2_b"])[i % 2]
                    if i:
                        pool.wait_ge(s.f_res, TT * i)
                    pool.dma_start(row[:, :], what[:, h * HALF:(h + 1) * HALF].partition_broadcast(P)).then_inc(row_loaded, 16)
                    pool.wait_ge(row_loaded, 16 * (i + 1))
                    for t in range(TT):
                        v = X[:, t, h * HALF:(h + 1) * HALF]
                        pool.tensor_tensor(v, v, row[:, :], (ALU.mult, ALU.add)[i % 2]).then_inc(s.f_res, 1)
                pool.wait_ge(k.w_split, base + NU)
                pool.dma_start(k.raw[0][:, :], a["ln3_g"].partition_broadcast(P)).then_inc(rows_loaded, 16)
                pool.dma_start(k.raw[1][:, :], a["ln3_b"].partition_broadcast(P)).then_inc(rows_loaded, 16)
                pool.wait_ge(rows_loaded, 32)
                for t in range(TT):
                    pool.wait_ge(s.f_gain, t + 1)
                    pool.tensor_tensor(X[:, t, :], X[:, t, :], k.raw[1][:, :], ALU.add).then_inc(s.f_out, 1)
                    pool.wait_ge(s.f_out, t + 1)
                    pool.dma_start(out[0, t * P:(t + 1) * P, :], X[:, t, :]).then_inc(stored, 16)
                pool.wait_ge(stored, 16 * TT)


def hybrid_layer(nc, a, out, scratch):
    k = Names()
    k.oaT, k.hA, k.gateB, k.stats, k.x1, k.x2 = scratch
    with ExitStack() as ctx:
        def sb(name, shape, dt=F32):
            return ctx.enter_context(nc.sbuf_tensor(name, shape, dt))
        k.phase_sems = []
        def sem(name):
            return ctx.enter_context(nc.semaphore(name))
        k.x_loaded = sem("x_loaded")
        k.small_loaded = sem("small_loaded")
        k.const = sem("const")
        k.x_turned = sem("x_turned")
        k.x_rounded = sem("x_rounded")
        k.x_split = sem("x_split")
        k.w_rounded = sem("w_rounded")
        k.w_split = sem("w_split")
        k.w_used = sem("w_used")
        k.db_copied = sem("db_copied")
        k.db_turned = sem("db_turned")
        k.conv_turned = sem("conv_turned")
        k.mag_ready = sem("mag_ready")
        k.sp_step = sem("sp_step")
        k.lnb_ready = sem("lnb_ready")
        k.g_ready = sem("g_ready")
        k.gam_done = sem("gam_done")
        k.gam_read = sem("gam_read")
        k.dve_setup = sem("dve_setup")
        k.s_zero = sem("s_zero")
        k.colb = sem("colb")
        k.chain = sem("chain")
        k.w_loaded = [ctx.enter_context(nc.semaphore(f"w_loaded{i}")) for i in range(RAW_SLOTS)]
        k.raw = [sb(f"raw{i}", [P, UNIT]) for i in range(RAW_SLOTS)]
        k.whi = [sb(f"whi{i}", [P, UNIT], F32R) for i in range(SPLIT_SLOTS)]
        k.wlo = [sb(f"wlo{i}", [P, UNIT], F32R) for i in range(SPLIT_SLOTS)]
        k.ident = sb("ident", [P, P])
        k.eps_rms = sb("eps_rms", [P, 1])
        k.eps_ln = sb("eps_ln", [P, 1])
        k.one_col = sb("one_col", [P, 1])
        k.dn_g = sb("dn_g", [P, 1])
        k.xh = sb("xh", [P, KT, SEQ], F32R)
        k.xl = sb("xl", [P, KT, SEQ], F32R)
        with ExitStack() as dn:
            def sbd(name, shape, dt=F32):
                return dn.enter_context(nc.sbuf_tensor(name, shape, dt))
            k.ones = sbd("ones", [P, P])
            k.upto = sbd("upto", [P, P])
            k.neg_strict = sbd("neg_strict", [P, P])
            k.neg_incl = sbd("neg_incl", [P, P])
            k.same = sbd("same", [P, P])
            k.other = sbd("other", [P, P])
            k.beta = sbd("beta", [P, HEADS, TT])
            k.lnb = sbd("lnb", [P, HEADS, TT])
            k.gam = sbd("gam", [P, HEADS, TT])
            k.gtot = sbd("gtot", [P, HEADS, TT])
            k.gtot_e = sbd("gtot_e", [P, HEADS, TT])
            k.gl = sbd("gl", [P, HEADS, TT])
            k.gs = sbd("gs", [P, HEADS, TT])
            k.cw = sbd("cw", [P, 96])
            k.xpad = [sbd(f"xpad{i}", [P, CONV - 1 + SEQ]) for i in range(2)]
            setup(nc, k, a)
            k.next_unit = columns(a["w_in"][0], COL_GA)
            deltanet(nc, k, a)
        base = 1 + 4 * HEADS
        k.next_unit = columns(a["w_in"][0], COL_BQ)
        branch_a(nc, k, a, base)
        base += 3 * KT
        with ExitStack() as ob:
            k.obh = ob.enter_context(nc.sbuf_tensor("obh", [P, HG, SEQ], F32R))
            k.obl = ob.enter_context(nc.sbuf_tensor("obl", [P, HG, SEQ], F32R))
            k.next_unit = a["w_br_b"][0][:, 0:2 * P].rearrange("(k p) n -> p k n", p=P)
            attention(nc, k, a, base)
            base += 3 * GROUPS * HG
            k.next_unit = pair_columns(a["w_mix_out"][0], 0, 0)
            merge(nc, k, a, base)
            base += 4
        k.next_unit = columns(a["w_xkv"][0], 0)
        project_and_norm(nc, k, "mix_", base, a["w_mix_out"][0], k.xh, k.xl, a["x"][0], a["ln1_g"], a["ln1_b"],
                         k.xh, k.xl, k.x1, True)
        base += 8
        oh = sb("oh", [P, KT, SEQ], F32R)
        ol = sb("ol", [P, KT, SEQ], F32R)
        k.next_unit = pair_columns(a["w_xo"][0], 0, 0)
        cross_attention(nc, k, a, base, oh, ol)
        base += 24
        k.next_unit = columns(a["w_ffn13"][0], 0)
        project_and_norm(nc, k, "xo_", base, a["w_xo"][0], oh, ol, k.x1, a["ln2_g"], a["ln2_b"],
                         k.xh, k.xl, k.x2, False)
        base += 8
        feed_forward(nc, k, a, base, k.xh, k.xl, oh, ol, out)


INPUTS = ("x", "mem", "positions", "w_in", "conv_w", "a_log", "dt_bias", "dn_norm_g", "w_br_a", "w_br_b",
          "w_mix_out", "ln1_g", "ln1_b", "w_xq", "w_xkv", "w_xo", "ln2_g", "ln2_b", "w_ffn13", "w_ffn2",
          "ln3_g", "ln3_b")
SCRATCH = {"oaT": (HEADS, P, SEQ), "hA": (KT, P, SEQ), "gateB": (KT, P, SEQ), "stats": (HG, SEQ, GROUPS, 2),
           "x1": (SEQ, D_MODEL), "x2": (SEQ, D_MODEL)}


def rope_frequencies():
    f = np.float32(10000.0) ** (-np.arange(0, P, 2, dtype=np.float32) / np.float32(P))
    return np.concatenate([f, f]).astype(np.float32).reshape(P, 1)


def kernel(**inputs):
    import concourse.bacc as bacc
    from concourse.bass_utils import run_bass_kernel_spmd

    nc = bacc.Bacc("TRN2", target_bir_lowering=False, num_devices=1)
    arrays = {n: np.ascontiguousarray(inputs[n]) for n in INPUTS}
    arrays["rope_freq"] = rope_frequencies()
    a = {n: nc.dram_tensor(f"in_{n}", v.shape, mybir.dt.from_np(v.dtype), kind="ExternalInput").ap()
         for n, v in arrays.items()}
    out = nc.dram_tensor("out", (1, SEQ, D_MODEL), F32, kind="ExternalOutput").ap()
    scratch = [nc.dram_tensor(f"scratch_{n}", shape, F32, kind="Internal").ap() for n, shape in SCRATCH.items()]
    hybrid_layer(nc, a, out, scratch)
    r = run_bass_kernel_spmd(nc, [{f"in_{n}": v for n, v in arrays.items()}], core_ids=[0])
    return r.results[0]["out"]
```

```python
import math
from contextlib import ExitStack

import concourse.bass as bass
import numpy as np
from concourse import mybir

F32 = mybir.dt.float32
F32R = mybir.dt.float32r
I32 = mybir.dt.int32
ALU = mybir.AluOpType
ACT = mybir.ActivationFunctionType
AX_X = mybir.AxisListType.X

P = 128
D_MODEL = 1024
SEQ = 1024
KT = D_MODEL // P
TT = SEQ // P
HALF = SEQ // 2
HEADS = 8
CHUNK = 64
CONV = 4
HG = 4
DILATIONS = (1, 4, 16)
GROUPS = len(DILATIONS)
DIL_W = GROUPS * HG * P
MEM = 256
XH = 4
XD = 256
D_FF = 2816
FT = D_FF // P
ALPHA = 2.0 ** 0.25
LN_EPS = 1e-5
RMS_EPS = 1e-6
NEG = -1e30

COL_Q, COL_K, COL_V = 0, HEADS * P, 2 * HEADS * P
COL_Z = 3 * HEADS * P
COL_DB = COL_Z + HEADS * P
COL_BQ = COL_DB + 2 * HEADS
COL_BK = COL_BQ + DIL_W
COL_BV = COL_BK + DIL_W
COL_GA = COL_BV + DIL_W
COL_GB = COL_GA + D_MODEL

RAW_SLOTS = 2
FIRST_GATE = 3
GATES_LATER = FIRST_GATE
GATES_ELSEWHERE = FIRST_GATE + 4
SPLIT_SLOTS = 4
UNIT = 1024


class Names:
    pass


def bc(ap, n):
    m = ap.shape[1]
    return ap.rearrange("p (m a) -> p m a", a=1).broadcast_to([P, m, n])


def rep(ap, n):
    m = ap.shape[1]
    return ap.rearrange("p (a m) -> p a m", a=1).broadcast_to([P, n, m])


def tiles(ap, n=P):
    return ap.rearrange("p (t n) -> p t n", n=n)



def load_unit(k, sync, u, ap):
    slot = k.raw[u % RAW_SLOTS]
    if u >= RAW_SLOTS:
        sync.wait_ge(k.w_split, u - RAW_SLOTS + 1)
    sync.dma_start(slot[:, :].rearrange("p (k n) -> p k n", k=ap.shape[1]), ap).then_inc(k.w_loaded[u % RAW_SLOTS], 16)


def round_unit(k, act, u, slot, raw):
    u, turn = u if isinstance(u, tuple) else (u, u // RAW_SLOTS)
    act.wait_ge(k.w_loaded[raw], 16 * (turn + 1))
    if not isinstance(u, int) or u >= SPLIT_SLOTS:
        act.wait_ge(k.w_used, u - SPLIT_SLOTS + 1)
    act.activation(k.whi[slot][:, :], k.raw[raw][:, :], ACT.Copy).then_inc(k.w_rounded, 1)


def rest_unit(k, dve, u, slot, raw):
    dve.wait_ge(k.w_rounded, u + 1)
    dve.tensor_tensor(k.wlo[slot][:, :], k.raw[raw][:, :], k.whi[slot][:, :].bitcast(F32),
                      ALU.subtract).then_inc(k.w_split, 1)


def columns(w, c0, n=P):
    return w[:, c0:c0 + n].rearrange("(k p) n -> p k n", p=P)


def three(pe, out, w_hi, w_lo, x_hi, x_lo, first, last):
    pe.matmul(out, w_hi, x_hi, start=first, stop=False)
    pe.matmul(out, w_hi, x_lo, start=False, stop=False)
    return pe.matmul(out, w_lo, x_hi, start=False, stop=last)


def clear_semaphores(nc, k):
    with nc.Block() as block:
        @block.sync
        def _(sync):
            for q in k.phase_sems:
                sync.sem_clear(q)
    k.phase_sems = []


def queue_sem(nc, k, name):
    return k.whole_program.enter_context(nc.semaphore(name))


def declare(nc, ctx, k):
    def sb(name, shape, dt=F32):
        t = ctx.enter_context(nc.sbuf_tensor(name, shape, dt))
        return t

    def sem(name):
        q = ctx.enter_context(nc.semaphore(name))
        k.phase_sems.append(q)
        return q
    return sb, sem


def setup(nc, k, a):
    with ExitStack() as ctx:
        sb, sem = declare(nc, ctx, k)
        xn = sb("xn", [P, TT, D_MODEL])
        wrows = sb("conv_rows", [96, P])
        dbT = sb("dbT", [16, SEQ])
        db = sb("db", [P, 16, TT])
        a_row = sb("a_row", [P, HEADS])
        dt_row = sb("dt_row", [P, HEADS])
        sp = sb("sp", [P, 2, 64])
        mag = sb("mag", [P, 2, 64])
        g = sb("g", [P, 64])
        ps = [ctx.enter_context(nc.psum_tensor(f"p0_{i}", [P, 512], F32)) for i in range(8)]
        with nc.Block() as block:
            @block.sync
            def _(sync):
                for f in range(2):
                    for half in range(2):
                        c = slice(half * D_MODEL // 2, (half + 1) * D_MODEL // 2)
                        sync.dma_start(xn[:, 4 * f:4 * f + 4, c], a["x"][0, f * HALF:(f + 1) * HALF, c].rearrange("(t p) d -> p t d", p=P)
                                       ).then_inc(k.x_loaded[2 * f + half], 16)
                sync.dma_start(wrows[:, :], a["conv_w"].rearrange("l j (t c) -> (l j t) c", c=P)).then_inc(k.small_loaded, 16)
                sync.dma_start(a_row[:, :], a["a_log"].partition_broadcast(P)).then_inc(k.small_loaded, 16)
                sync.dma_start(dt_row[:, :], a["dt_bias"].partition_broadcast(P)).then_inc(k.small_loaded, 16)
                sync.dma_start(k.dn_g[:, :], a["dn_norm_g"].rearrange("l (d o) -> (l d) o", o=1)).then_inc(k.small_loaded, 16)
                load_unit(k, sync, 0, columns(a["w_in"][0], COL_DB))
                load_unit(k, sync, 1, columns(a["w_in"][0], COL_Q))

            @block.gpsimd
            def _(pool):
                pool.memset(k.ident[:, :], 0.0).then_inc(k.const, 1)
                pool.memset(k.ones[:, :], 1.0).then_inc(k.const, 1)
                pool.memset(k.upto[:, :], 1.0).then_inc(k.const, 1)
                pool.memset(k.neg_strict[:, :], 0.0).then_inc(k.const, 1)
                pool.memset(k.neg_incl[:, :], 0.0).then_inc(k.const, 1)
                pool.memset(k.same[:, :], 0.0).then_inc(k.const, 1)
                pool.memset(k.other[:, :], 1.0).then_inc(k.const, 1)
                pool.wait_ge(k.const, 7)
                pool.affine_select(out=k.ident[:, :], in_=k.ident[:, :], compare_op=ALU.not_equal, fill=1.0,
                                   base=0, pattern=[[-1, P]], channel_multiplier=1).then_inc(k.const, 1)
                pool.affine_select(out=k.upto[:, :], in_=k.upto[:, :], compare_op=ALU.is_ge, fill=0.0,
                                   base=0, pattern=[[1, P]], channel_multiplier=-1).then_inc(k.const, 1)
                pool.affine_select(out=k.neg_incl[:, :], in_=k.neg_incl[:, :], compare_op=ALU.is_ge, fill=NEG,
                                   base=0, pattern=[[1, P]], channel_multiplier=-1).then_inc(k.const, 1)
                pool.affine_select(out=k.neg_strict[:, :], in_=k.neg_strict[:, :], compare_op=ALU.is_ge, fill=NEG,
                                   base=-1, pattern=[[1, P]], channel_multiplier=-1).then_inc(k.const, 1)
                for n, (m, v) in enumerate(((k.same, 1.0), (k.other, 0.0))):
                    pool.wait_ge(k.const, 11 + 2 * n)
                    pool.memset(m[0:CHUNK, 0:CHUNK], v).then_inc(k.const, 1)
                    pool.wait_ge(k.const, 12 + 2 * n)
                    pool.memset(m[CHUNK:P, CHUNK:P], v).then_inc(k.const, 1)
                pool.wait_ge(k.const, 15)
                pool.memset(k.xpad[0][:, 0:CONV - 1], 0.0).then_inc(k.const, 1)
                pool.memset(k.xpad[1][:, 0:CONV - 1], 0.0).then_inc(k.const, 1)
                for col, v in ((k.eps_rms, RMS_EPS), (k.eps_ln, LN_EPS), (k.one_col, 1.0)):
                    pool.memset(col[:, :], v).then_inc(k.const, 1)

            @block.tensor
            def _(pe):
                pe.wait_ge(k.const, 20)
                n = 0
                for f in range(2):
                    for m in range(KT):
                        if m % (KT // 2) == 0:
                            pe.wait_ge(k.x_loaded[2 * f + m // (KT // 2)], 16)
                        if n >= 8:
                            pe.wait_ge(k.x_split, n - 7)
                        for t in range(4):
                            last = pe.transpose(ps[n % 8][:, t * P:(t + 1) * P],
                                                xn[:, 4 * f + t, m * P:(m + 1) * P], k.ident[:, :])
                        last.then_inc(k.x_turned, 1)
                        n += 1
                pe.wait_ge(k.w_split, 1)
                pe.wait_ge(k.x_split, 16)
                for f in range(2):
                    for m in range(KT):
                        last = three(pe, ps[f][:, :], k.whi[0][:, m * P:(m + 1) * P], k.wlo[0][:, m * P:(m + 1) * P],
                                     k.xh[:, m, f * HALF:(f + 1) * HALF], k.xl[:, m, f * HALF:(f + 1) * HALF],
                                     m == 0, m == KT - 1)
                last.then_inc(k.w_used, 1)
                pe.wait_ge(k.db_copied, 2)
                for t in range(TT):
                    last = pe.transpose(ps[2][:, t * 16:(t + 1) * 16], dbT[:, t * P:(t + 1) * P], k.ident[0:16, 0:16])
                last.then_inc(k.db_turned, 1)
                pe.wait_ge(k.small_loaded, 64)
                pe.transpose(ps[3][:, 0:96], wrows[:, :], k.ident[0:96, 0:96]).then_inc(k.conv_turned, 1)
                pe.wait_ge(k.g_ready, 1)
                pe.matmul(ps[4][:, 0:64], k.upto[:, :], g[:, :], start=True, stop=True)
                pe.matmul(ps[5][:, 0:64], k.ones[:, :], g[:, :], start=True, stop=True).then_inc(k.gam_done, 1)

            @block.scalar
            def _(act):
                for n in range(16):
                    m, f = n % KT, n // KT
                    act.wait_ge(k.x_turned, n + 1)
                    act.activation(k.xh[:, m, f * HALF:(f + 1) * HALF], ps[n % 8][:, :], ACT.Copy).then_inc(k.x_rounded, 1)
                round_unit(k, act, 0, 0, 0)
                round_unit(k, act, 1, 1, 1)
                act.wait_ge(k.w_used, 1)
                for f in range(2):
                    act.activation(dbT[:, f * HALF:(f + 1) * HALF], ps[f][0:16, :], ACT.Copy).then_inc(k.db_copied, 1)
                act.wait_ge(k.mag_ready, 1)
                act.activation(sp[:, :, :], mag[:, :, :], ACT.Exp, scale=-1.0).then_inc(k.sp_step, 1)
                act.wait_ge(k.sp_step, 1)
                act.activation(sp[:, :, :], sp[:, :, :], ACT.Ln, bias=k.one_col[:, :]).then_inc(k.sp_step, 1)
                act.activation(a_row[:, :], a_row[:, :], ACT.Exp).then_inc(k.sp_step, 1)
                act.wait_ge(k.lnb_ready, 1)
                act.activation(k.beta[:, :, :], k.lnb[:, :, :], ACT.Exp).then_inc(k.sp_step, 1)
                act.wait_ge(k.gam_read, 2)
                act.activation(k.gtot_e[:, :, :], k.gtot[:, :, :], ACT.Exp).then_inc(k.sp_step, 1)

            @block.vector
            def _(dve):
                for n in range(16):
                    m, f = n % KT, n // KT
                    dve.wait_ge(k.x_rounded, n + 1)
                    dve.tensor_tensor(k.xl[:, m, f * HALF:(f + 1) * HALF], ps[n % 8][:, :],
                                      k.xh[:, m, f * HALF:(f + 1) * HALF].bitcast(F32), ALU.subtract).then_inc(k.x_split, 1)
                rest_unit(k, dve, 0, 0, 0)
                rest_unit(k, dve, 1, 1, 1)
                dve.wait_ge(k.conv_turned, 1)
                dve.tensor_copy(k.cw[:, :], ps[3][:, 0:96]).then_inc(k.dve_setup, 1)
                dve.wait_ge(k.db_turned, 1)
                dve.tensor_copy(db[:, :, :], ps[2][:, 0:128].rearrange("p (t c) -> p c t", c=16)).then_inc(k.dve_setup, 1)
                dve.wait_ge(k.dve_setup, 2)
                z = db[:, 0:8, :]
                dve.tensor_tensor(z, z, bc(dt_row[:, :], TT), ALU.add).then_inc(k.dve_setup, 1)
                dve.wait_ge(k.dve_setup, 3)
                z2 = db[:, :, :].rearrange("p c t -> p (c t)")
                m2 = mag[:, :, :].rearrange("p a b -> p (a b)")
                dve.tensor_scalar(m2, z2, -1.0, None, ALU.mult).then_inc(k.dve_setup, 1)
                dve.wait_ge(k.dve_setup, 4)
                dve.tensor_tensor(m2, m2, z2, ALU.max).then_inc(k.mag_ready, 1)
                dve.wait_ge(k.sp_step, 3)
                dve.scalar_tensor_tensor(out=g[:, :], in0=z2[:, 0:64], scalar=0.0, in1=sp[:, 0, :],
                                         op0=ALU.max, op1=ALU.add).then_inc(k.dve_setup, 1)
                dve.scalar_tensor_tensor(out=k.lnb[:, :, :].rearrange("p a b -> p (a b)"), in0=z2[:, 64:128], scalar=0.0,
                                         in1=sp[:, 1, :], op0=ALU.min, op1=ALU.subtract).then_inc(k.lnb_ready, 1)
                dve.wait_ge(k.dve_setup, 5)
                dve.tensor_scalar(g[:, :], g[:, :], -1.0, None, ALU.mult).then_inc(k.dve_setup, 1)
                dve.wait_ge(k.dve_setup, 6)
                dve.tensor_tensor(tiles(g[:, :], TT), tiles(g[:, :], TT), bc(a_row[:, :], TT), ALU.mult).then_inc(k.g_ready, 1)
                dve.wait_ge(k.gam_done, 1)
                dve.tensor_copy(k.gam[:, :, :].rearrange("p a b -> p (a b)"), ps[4][:, 0:64]).then_inc(k.gam_read, 1)
                dve.tensor_copy(k.gtot[:, :, :].rearrange("p a b -> p (a b)"), ps[5][:, 0:64]).then_inc(k.gam_read, 1)
                dve.wait_ge(k.gam_read, 2)
                dve.wait_ge(k.lnb_ready, 1)
                dve.tensor_tensor(k.gl[:, :, :], k.gam[:, :, :], k.lnb[:, :, :], ALU.add)
                dve.tensor_scalar(k.gs[:, :, :].rearrange("p a b -> p (a b)"), k.gam[:, :, :].rearrange("p a b -> p (a b)"),
                                  -0.5 * math.log(P), None, ALU.add)


def deltanet(nc, k, a):
    with ExitStack() as ctx:
        sb, sem = declare(nc, ctx, k)
        qT = [sb(f"qT{i}", [P, SEQ]) for i in range(2)]
        kTt = [sb(f"kT{i}", [P, SEQ]) for i in range(2)]
        vT = [sb(f"vT{i}", [P, SEQ]) for i in range(2)]
        zT = [sb(f"zT{i}", [P, SEQ]) for i in range(2)]
        qkv = (qT, kTt, vT)
        sqk = sb("sq_or_kbg", [P, SEQ])
        sqq = sb("sq_or_qd", [P, SEQ])
        kn = sb("kn", [P, SEQ])
        vb = sb("vb", [P, SEQ])
        x1 = sb("x1", [P, SEQ])
        x2 = sb("x2", [P, SEQ])
        nT = sb("nT", [P, SEQ])
        pd = sb("pd", [P, TT, 2, P])
        pw = sb("pw", [P, SEQ])
        no = sb("no", [P, SEQ])
        S = sb("state", [P, P])
        rbuf = sb("rbuf", [P, 2, P])
        vnew = sb("vnew", [P, 2, P])
        st = sb("stats", [P, 2, TT])
        rowA = sb("rowA", [P, TT])
        rowQ = sb("rowQ", [P, TT])
        colB = sb("colB", [P, TT])
        kde = sb("kde", [P, TT])
        orms = sb("orms", [P, TT])
        PP = ctx.enter_context(nc.psum_tensor("PP", [P, 1024], F32))
        DA = ctx.enter_context(nc.psum_tensor("DA", [P, 1024], F32))
        DB = ctx.enter_context(nc.psum_tensor("DB", [P, 1024], F32))
        DC = ctx.enter_context(nc.psum_tensor("DC", [P, 1024], F32))
        DD = (DA, DB)
        s = Names()
        s.half_done = sem("dn_half_done")
        s.proj_read = sem("dn_proj_read")
        s.conv_step = sem("dn_conv_step")
        s.conv_done = sem("dn_conv_done")
        s.silu_done = sem("dn_silu_done")
        s.turned = sem("dn_turned")
        s.squared = sem("dn_squared")
        s.ssq_done = sem("dn_ssq_done")
        s.kn_copied = sem("dn_kn_copied")
        s.vb_done = sem("dn_vb_done")
        s.ln_done = sem("dn_ln_done")
        s.rows_done = sem("dn_rows_done")
        s.kde_done = sem("dn_kde_done")
        s.kk_done = sem("dn_kk_done")
        s.qk_done = sem("dn_qk_done")
        s.an_rows = sem("dn_an_rows")
        s.aq_rows = sem("dn_aq_rows")
        s.an_exp = sem("dn_an_exp")
        s.aq_exp = sem("dn_aq_exp")
        s.x1_ready = sem("dn_x1_ready")
        s.x1_exp = sem("dn_x1_exp")
        s.x2_ready = sem("dn_x2_ready")
        s.x2_exp = sem("dn_x2_exp")
        s.nT_done = sem("dn_nT_done")
        s.qk_decayed = sem("dn_qk_decayed")
        s.kbg_done = sem("dn_kbg_done")
        s.qd_done = sem("dn_qd_done")
        s.kd_done = sem("dn_kd_done")
        s.n_turned = sem("dn_n_turned")
        s.p0_done = sem("dn_p0_done")
        s.p0T_done = sem("dn_p0T_done")
        s.off_copied = sem("dn_off_copied")
        s.off_done = sem("dn_off_done")
        s.dt_init = sem("dn_dt_init")
        s.pw_done = sem("dn_pw_done")
        s.pT_copied = sem("dn_pT_copied")
        s.dT_added = sem("dn_dT_added")
        s.p_copied = sem("dn_p_copied")
        s.d_turned = sem("dn_d_turned")
        s.d_copied = sem("dn_d_copied")
        s.z_done = sem("dn_z_done")
        s.z_copied = sem("dn_z_copied")
        s.w_done = sem("dn_w_done")
        s.t_done = sem("dn_t_done")
        s.r_done = sem("dn_r_done")
        s.r_read = sem("dn_r_read")
        s.v_done = sem("dn_v_done")
        s.v_copied = sem("dn_v_copied")
        s.ds_done = sem("dn_ds_done")
        s.s_done = sem("dn_s_done")
        s.o_done = sem("dn_o_done")
        s.o_copied = sem("dn_o_copied")
        s.o_rms = sem("dn_o_rms")
        s.o_rs = sem("dn_o_rs")
        s.o_scaled = sem("dn_o_scaled")
        s.o_turned = sem("dn_o_turned")
        s.o_gated = sem("dn_o_gated")
        s.o_stored = sem("dn_o_stored")
        s.gates_stored = sem("dn_gates_stored")
        with nc.Block() as block:
            @block.sync
            def _(sync):
                for q in k.phase_sems:
                    sync.sem_inc(q, 1)
        base = 1

        def unit(h, n):
            return base + 4 * h + n

        def unit_turn(h, n):
            return unit(h, n), 2 * h + (base + n) // RAW_SLOTS

        def piece(pe, h, i):
            n, f, m = i // (2 * KT), (i // KT) % 2, i % KT
            slot = (base + n) % SPLIT_SLOTS
            if m == 0:
                if f == 0:
                    pe.wait_ge(k.w_split, unit(h, n) + 1)
                read = 8 * h + 2 * n + f - 1
                if not isinstance(h, int) or read > 0:
                    pe.wait_ge(s.proj_read, 1 + read)
            last = three(pe, PP[:, f * HALF:(f + 1) * HALF],
                         k.whi[slot][:, m * P:(m + 1) * P], k.wlo[slot][:, m * P:(m + 1) * P],
                         k.xh[:, m, f * HALF:(f + 1) * HALF], k.xl[:, m, f * HALF:(f + 1) * HALF],
                         m == 0, m == KT - 1)
            if m == KT - 1:
                last.then_inc(s.half_done if f == 0 else k.w_used, 1)

        def pieces(pe, h, i0, i1):
            for i in range(i0, i1):
                piece(pe, h, i)

        def ch(t, c):
            return t[:, c * P:(c + 1) * P]

        sq = pd[:, 0:4, :, :].rearrange("p c a n -> p (c a n)")

        def pe_step(pe, h, g, b):
            if g is None:
                pieces(pe, h, 0, 4 * 2 * KT)
                return
            q, kk_, v = qT[b], kTt[b], vT[b]
            for i, (src, out) in enumerate(((kk_, DB), (v, DC), (q, DA))):
                if i == 0:
                    pe.wait_ge(s.silu_done, 1 + 3 * g + 3)
                    pe.wait_ge(s.s_done, 1 + 8 * g)
                    pe.wait_ge(s.o_copied, 1 + 8 * g)
                elif i == 2:
                    pe.wait_ge(s.o_gated, 1 + g)
                for c in range(TT):
                    last = pe.transpose(ch(out, c), ch(src, c), k.ident[:, :])
                last.then_inc(s.turned, 1)
            pieces(pe, h, 0, 3)
            pe.wait_ge(s.squared, 1 + 2 * g + 2)
            for c in range(TT):
                last = pe.matmul(ch(DA, c), ch(kk_, c), ch(kk_, c), start=True, stop=True)
            last.then_inc(s.kk_done, 1)
            pe.wait_ge(s.kn_copied, 1 + g + 1)
            for c in range(TT):
                last = pe.matmul(ch(DB, c), ch(kk_, c), ch(q, c), start=True, stop=True)
            last.then_inc(s.qk_done, 1)
            pe.wait_ge(s.rows_done, 1 + g + 1)
            pe.wait_ge(s.vb_done, 1 + g + 1)
            for c in range(TT):
                last = pe.matmul(ch(DC, c), rowA[:, c:c + 1].broadcast_to([P, P]), k.ident[:, :], start=True, stop=True)
            last.then_inc(s.an_rows, 1)
            pieces(pe, h, 3, 9)
            pe.wait_ge(s.an_exp, 1 + g + 1)
            pe.wait_ge(s.x1_ready, 1 + g + 1)
            for c in range(TT):
                last = pe.matmul(ch(DC, c), rowQ[:, c:c + 1].broadcast_to([P, P]), k.ident[:, :], start=True, stop=True)
            last.then_inc(s.aq_rows, 1)
            pieces(pe, h, 9, 13)
            pe.wait_ge(s.nT_done, 1 + g + 1)
            for c in range(TT):
                last = pe.transpose(ch(DA, c), ch(nT, c), k.ident[:, :])
            last.then_inc(s.n_turned, 1)
            pieces(pe, h, 13, 18)
            for r in range(6):
                for j in range(2):
                    if r == 0:
                        pe.wait_ge(s.p0_done, 1 + g + 1)
                        pe.wait_ge(s.p0T_done, 1 + g + 1)
                        pe.wait_ge(s.off_copied, 1 + g + 1)
                        pe.wait_ge(s.qk_decayed, 1 + g + 1)
                        pe.wait_ge(s.aq_exp, 1 + g + 1)
                        pe.wait_ge(s.x2_ready, 1 + g + 1)
                    else:
                        if r == 1:
                            pe.wait_ge(s.dt_init, 1 + g + 1)
                        else:
                            pe.wait_ge(s.dT_added, 1 + 10 * g + 2 * (r - 2) + j + 1)
                        if r < 5:
                            pe.wait_ge(s.pT_copied, 1 + 8 * g + 2 * (r - 1) + j + 1)
                        pe.wait_ge(s.p_copied, 1 + 10 * g + 2 * (r - 1) + j + 1)
                    for i in range(4):
                        c = 4 * j + i
                        out = DD[j][:, 2 * i * P:2 * (i + 1) * P]
                        if r == 0:
                            last = pe.matmul(out[:, 0:P], ch(pw, c), pd[:, c, 0, :], start=True, stop=True)
                        elif r < 4:
                            last = pe.matmul(out, ch(pw, c), pd[:, c, :, :].rearrange("p a b -> p (a b)"), start=True, stop=True)
                        else:
                            last = pe.matmul(out[:, P:2 * P], ch(pw, c), pd[:, c, 1, :], start=True, stop=True)
                    if r < 5:
                        for i in range(4):
                            c = 4 * j + i
                            last = pe.matmul(ch(DC, c), pd[:, c, 0, :], ch(pw, c), start=True, stop=True)
                    last.then_inc(s.pw_done, 1)
            for j in range(2):
                if j:
                    pieces(pe, h, 18, 19)
                pe.wait_ge(s.dT_added, 1 + 10 * g + 8 + j + 1)
                for i in range(4):
                    c = 4 * j + i
                    last = pe.transpose(DD[j][:, i * P:(i + 1) * P], pd[:, c, 1, :], k.ident[:, :])
                last.then_inc(s.d_turned, 1)
            for j in range(2):
                pe.wait_ge(s.off_done, 1 + g + 1)
                for i in range(4):
                    c = 4 * j + i
                    last = pe.matmul(ch(DC, c), ch(no, c), pd[:, c, 1, :], start=True, stop=True)
                last.then_inc(s.z_done, 1)
            pieces(pe, h, 19, 20)
            for j in range(2):
                pe.wait_ge(s.z_copied, 1 + 2 * g + j + 1)
                pe.wait_ge(s.d_copied, 1 + 2 * g + j + 1)
                for i in range(4):
                    c = 4 * j + i
                    last = pe.matmul(DD[j][:, HALF + i * P:HALF + (i + 1) * P], ch(pw, c), ch(x1, c), start=True, stop=True)
                last.then_inc(s.w_done, 1)
            for c in range(TT):
                j = c % 2
                if c:
                    pe.wait_ge(s.s_done, 1 + 8 * g + c)
                if c == 0:
                    pe.wait_ge(k.s_zero, g + 1)
                    pe.wait_ge(s.kbg_done, 1 + g + 1)
                    pe.wait_ge(s.qd_done, 1 + g + 1)
                    pe.wait_ge(s.d_copied, 1 + 2 * g + 2)
                else:
                    pe.wait_ge(s.r_read, 1 + 8 * g + c)
                pe.matmul(DA[:, 0:P], ch(sqk, c), S[:, :], start=True, stop=True).then_inc(s.r_done, 1)
                if c == 0:
                    pe.wait_ge(s.z_copied, 1 + 2 * g + 2)
                elif c >= 2:
                    pe.wait_ge(s.o_copied, 1 + 8 * g + c - 1)
                pe.matmul(DC[:, j * HALF:j * HALF + P], ch(sqq, c), S[:, :], start=True, stop=False)
                pieces(pe, h, 20 + 5 * c, 22 + 5 * c)
                pe.wait_ge(s.r_read, 1 + 8 * g + c + 1)
                if c % 4 == 0:
                    pe.wait_ge(s.t_done, 1 + 2 * g + c // 4 + 1)
                if c:
                    pe.wait_ge(s.v_copied, 1 + 8 * g + c)
                pe.matmul(DA[:, HALF:HALF + P], ch(nT, c), rbuf[:, j, :], start=True, stop=True).then_inc(s.v_done, 1)
                pieces(pe, h, 22 + 5 * c, 24 + 5 * c)
                pe.wait_ge(s.v_copied, 1 + 8 * g + c + 1)
                if c == 0:
                    pe.wait_ge(s.kd_done, 1 + g + 1)
                pe.matmul(DB[:, 0:P], ch(kn, c), vnew[:, j, :], start=True, stop=True).then_inc(s.ds_done, 1)
                pe.matmul(DC[:, j * HALF:j * HALF + P], ch(x2, c), vnew[:, j, :], start=False, stop=True).then_inc(s.o_done, 1)
                pieces(pe, h, 24 + 5 * c, 25 + 5 * c)
            pieces(pe, h, 60, 64)
            pe.wait_ge(s.o_scaled, 1 + g + 1)
            for c in range(TT):
                last = pe.transpose(ch(DA, c), ch(x1, c), k.ident[:, :])
            last.then_inc(s.o_turned, 1)

        def is_gates(h):
            return isinstance(h, int) and h == HEADS

        def wait_half(act, h, n, f):
            if f == 0:
                act.wait_ge(s.half_done, 1 + 4 * h + n + 1)
            else:
                act.wait_ge(k.w_used, unit(h, n) + 1)

        def copy_proj(act, h, n, f):
            wait_half(act, h, n, f)
            src = PP[:, f * HALF:(f + 1) * HALF]
            b = 0 if n != 1 else 1
            if is_gates(h):
                act.activation(qkv[n][0][:, f * HALF:(f + 1) * HALF], src, ACT.Sigmoid).then_inc(s.proj_read, 1)
            else:
                if f == 0:
                    done = {0: 3 * h, 1: 3 * h - 1, 2: 3 * h + 1}[n]
                    if not isinstance(h, int) or done > 0:
                        act.wait_ge(s.conv_done, 1 + done)
                act.activation(k.xpad[b][:, CONV - 1 + f * HALF:CONV - 1 + (f + 1) * HALF], src, ACT.Copy).then_inc(s.proj_read, 1)

        def silu_z(act, h, hb, f):
            wait_half(act, h, 3, f)
            if not isinstance(h, int) or h > 1:
                act.wait_ge(s.o_gated, 1 + h - 1)
            act.activation(zT[hb][:, f * HALF:(f + 1) * HALF], PP[:, f * HALF:(f + 1) * HALF],
                           ACT.Sigmoid if is_gates(h) else ACT.Silu).then_inc(s.proj_read, 1)

        def silu(act, h, hb, n):
            if is_gates(h):
                return
            act.wait_ge(s.conv_done, 1 + 3 * h + n + 1)
            act.activation(qkv[n][hb][:, :], qkv[n][hb][:, :], ACT.Silu).then_inc(s.silu_done, 1)

        def conv_tap(dve, h, hb, n, j):
            if is_gates(h):
                return
            b = 0 if n != 1 else 1
            out = qkv[n][hb][:, :]
            w = k.cw[:, bass.ds(h + HEADS * (3 * j + n), 1)]
            if j == 0:
                dve.wait_ge(s.proj_read, 1 + 8 * h + 2 * n + 2)
                dve.tensor_scalar(out, k.xpad[b][:, 0:SEQ], w, None, ALU.mult).then_inc(s.conv_step, 1)
            else:
                dve.wait_ge(s.conv_step, 1 + 9 * h + 3 * n + j)
                dve.scalar_tensor_tensor(out=out, in0=k.xpad[b][:, j:j + SEQ], scalar=w, in1=out,
                                         op0=ALU.mult, op1=ALU.add).then_inc(s.conv_step if j < 3 else s.conv_done, 1)

        def act_step(act, h, hb, g):
            if g is None:
                for n in range(4):
                    round_unit(k, act, unit_turn(h, n + 1), (base + n + 1) % 4, (base + n + 1) % 2)
                    for f in range(2):
                        if n < 3:
                            copy_proj(act, h, n, f)
                        else:
                            silu_z(act, h, hb, f)
                    if n < 3:
                        silu(act, h, hb, n)
                return
            for i, (src, out) in enumerate(((DB, sqq), (DA, sqk))):
                act.wait_ge(s.turned, 1 + 3 * g + 2 * i + 1)
                if i == 0:
                    act.wait_ge(s.r_done, 1 + 8 * g)
                    act.wait_ge(s.o_done, 1 + 8 * g)
                act.activation(out[:, :], src[:, :], ACT.Square).then_inc(s.squared, 1)
            act.wait_ge(s.ssq_done, 1 + 2 * g + 2)
            act.wait_ge(s.rows_done, 1 + g)
            act.activation(st[:, :, :], st[:, :, :], ACT.Ln, bias=k.eps_rms[:, :]).then_inc(s.ln_done, 1)
            act.wait_ge(s.rows_done, 1 + g + 1)
            act.activation(kde[:, :], kde[:, :], ACT.Exp).then_inc(s.kde_done, 1)
            act.wait_ge(s.an_rows, 1 + g + 1)
            act.activation(sqk[:, :], DC[:, :], ACT.Exp).then_inc(s.an_exp, 1)
            copy_proj(act, h, 0, 0)
            round_unit(k, act, unit_turn(h, 1), (base + 1) % 4, (base + 1) % 2)
            act.wait_ge(s.x1_ready, 1 + g + 1)
            act.activation(x1[:, :], x1[:, :], ACT.Exp).then_inc(s.x1_exp, 1)
            act.wait_ge(s.aq_rows, 1 + g + 1)
            act.activation(sqq[:, :], DC[:, :], ACT.Exp).then_inc(s.aq_exp, 1)
            act.wait_ge(s.n_turned, 1 + g + 1)
            act.activation(no[:, :], DA[:, :], ACT.Copy).then_inc(s.off_copied, 1)
            act.wait_ge(s.x2_ready, 1 + g + 1)
            act.activation(x2[:, :], x2[:, :], ACT.Exp).then_inc(s.x2_exp, 1)
            copy_proj(act, h, 0, 1)
            round_unit(k, act, unit_turn(h, 2), (base + 2) % 4, (base + 2) % 2)
            for r in range(5):
                for j in range(2):
                    act.wait_ge(s.pw_done, 1 + 12 * g + 2 * r + j + 1)
                    if r == 0:
                        act.wait_ge(s.dt_init, 1 + g + 1)
                    if r < 4:
                        act.activation(pd[:, 4 * j:4 * j + 4, 0, :],
                                       DD[j][:, :].rearrange("p (c a n) -> p c a n", a=2, n=P)[:, :, 0, :],
                                       ACT.Copy).then_inc(s.pT_copied, 1)
                    act.activation(pw[:, j * HALF:(j + 1) * HALF], DC[:, j * HALF:(j + 1) * HALF], ACT.Copy).then_inc(s.p_copied, 1)
            for j in range(2):
                act.wait_ge(s.d_turned, 1 + 2 * g + j + 1)
                act.wait_ge(s.pw_done, 1 + 12 * g + 12)
                act.activation(pw[:, j * HALF:(j + 1) * HALF], DD[j][:, 0:HALF], ACT.Copy).then_inc(s.d_copied, 1)
            for c in range(TT):
                j = c % 2
                act.wait_ge(s.v_done, 1 + 8 * g + c + 1)
                if c >= 2:
                    act.wait_ge(s.o_done, 1 + 8 * g + c - 1)
                act.activation(vnew[:, j, :], DA[:, HALF:HALF + P], ACT.Copy).then_inc(s.v_copied, 1)
                act.wait_ge(s.o_done, 1 + 8 * g + c + 1)
                if c == 0:
                    act.wait_ge(s.w_done, 1 + 2 * g + 2)
                    act.wait_ge(s.t_done, 1 + 2 * g + 2)
                    act.wait_ge(s.o_scaled, 1 + g)
                act.activation(ch(x1, c), DC[:, j * HALF:j * HALF + P], ACT.Copy)
                act.activation(ch(sq, c), DC[:, j * HALF:j * HALF + P], ACT.Square,
                               accum_out=orms[:, c:c + 1]).then_inc(s.o_copied, 1)
                if c == 0:
                    copy_proj(act, h, 1, 0)
                    round_unit(k, act, unit_turn(h, 3), (base + 3) % 4, (base + 3) % 2)
                if c == 2:
                    copy_proj(act, h, 1, 1)
                if c == 4:
                    copy_proj(act, h, 2, 0)
                    round_unit(k, act, unit_turn(h, 4), base % 4, base % 2)
                if c == 5:
                    copy_proj(act, h, 2, 1)
                    silu(act, h, hb, 0)
                if c == 6:
                    silu(act, h, hb, 1)
            act.wait_ge(s.o_copied, 1 + 8 * g + 8)
            act.activation(orms[:, :], orms[:, :], ACT.Sqrt, scale=1.0 / P, bias=k.eps_rms[:, :]).then_inc(s.o_rms, 1)
            silu_z(act, h, hb, 0)
            silu(act, h, hb, 2)
            silu_z(act, h, hb, 1)

        def row(t, g):
            return t[:, bass.ds(g, 1), :].rearrange("p a b -> p (a b)")

        def dve_step(dve, h, hb, g, b):
            if g is None:
                for n in range(4):
                    rest_unit(k, dve, unit(h, n + 1), (base + n + 1) % 4, (base + n + 1) % 2)
                    if n < 3:
                        for j in range(CONV):
                            conv_tap(dve, h, hb, n, j)
                return
            v3 = tiles
            dve.wait_ge(s.squared, 1 + 2 * g + 1)
            dve.wait_ge(s.ln_done, 1 + g)
            dve.reduce_sum(st[:, 1, :], v3(sqq[:, :]), AX_X).then_inc(s.ssq_done, 1)
            dve.wait_ge(s.ds_done, 1 + 8 * g)
            dve.tensor_copy(kn[:, :], DB[:, :]).then_inc(s.kn_copied, 1)
            dve.wait_ge(s.squared, 1 + 2 * g + 2)
            dve.reduce_sum(st[:, 0, :], v3(sqk[:, :]), AX_X).then_inc(s.ssq_done, 1)
            dve.wait_ge(s.turned, 1 + 3 * g + 2)
            dve.tensor_tensor(v3(vb[:, :]), v3(DC[:, :]), bc(row(k.beta, g), P), ALU.mult).then_inc(s.vb_done, 1)

            dve.wait_ge(s.ln_done, 1 + g + 1)
            dve.scalar_tensor_tensor(out=rowA[:, :], in0=st[:, 1, :], scalar=-0.5, in1=row(k.gl, g), op0=ALU.mult, op1=ALU.add)
            dve.scalar_tensor_tensor(out=rowQ[:, :], in0=st[:, 0, :], scalar=-0.5, in1=row(k.gs, g), op0=ALU.mult, op1=ALU.add)
            dve.wait_ge(s.kd_done, 1 + g)
            dve.scalar_tensor_tensor(out=colB[:, :], in0=st[:, 1, :], scalar=-0.5, in1=row(k.gam, g), op0=ALU.mult, op1=ALU.subtract).then_inc(k.colb, 1)
            dve.wait_ge(k.colb, g + 1)
            dve.tensor_tensor(kde[:, :], colB[:, :], row(k.gtot, g), ALU.add).then_inc(s.rows_done, 1)
            dve.wait_ge(s.an_exp, 1 + g + 1)
            dve.wait_ge(s.o_turned, 1 + g)
            for c in range(TT):
                last = dve.scalar_tensor_tensor(out=ch(x1, c), in0=ch(DC, c), scalar=colB[:, c:c + 1], in1=k.neg_strict[:, :],
                                                op0=ALU.add, op1=ALU.add)
            last.then_inc(s.x1_ready, 1)
            rest_unit(k, dve, unit(h, 1), (base + 1) % 4, (base + 1) % 2)
            dve.wait_ge(s.x1_exp, 1 + g + 1)
            dve.wait_ge(s.kk_done, 1 + g + 1)
            dve.wait_ge(s.v_done, 1 + 8 * g)
            dve.scalar_tensor_tensor(out=nT[:, :], in0=DA[:, :], scalar=-1.0, in1=x1[:, :], op0=ALU.mult, op1=ALU.mult).then_inc(s.nT_done, 1)
            dve.wait_ge(s.aq_exp, 1 + g + 1)
            dve.wait_ge(s.o_done, 1 + 8 * g)
            for c in range(TT):
                last = dve.scalar_tensor_tensor(out=ch(x2, c), in0=ch(DC, c), scalar=colB[:, c:c + 1], in1=k.neg_incl[:, :],
                                                op0=ALU.add, op1=ALU.add)
            last.then_inc(s.x2_ready, 1)
            dve.wait_ge(s.off_copied, 1 + g + 1)
            dve.wait_ge(s.w_done, 1 + 2 * g)
            dve.tensor_tensor(v3(pw[:, :]), v3(DA[:, :]), rep(k.same[:, :], TT), ALU.mult).then_inc(s.p0_done, 1)
            dve.wait_ge(s.x2_exp, 1 + g + 1)
            dve.wait_ge(s.qk_done, 1 + g + 1)
            dve.tensor_tensor(x2[:, :], DB[:, :], x2[:, :], ALU.mult).then_inc(s.qk_decayed, 1)
            rest_unit(k, dve, unit(h, 2), (base + 2) % 4, (base + 2) % 2)
            for r in range(6):
                if r < 4:
                    conv_tap(dve, h, hb, 0, r)
                for j in range(2):
                    if r == 0:
                        continue
                    if r < 4:
                        dve.wait_ge(s.pT_copied, 1 + 8 * g + 2 * r + j + 1)
                    else:
                        dve.wait_ge(s.pw_done, 1 + 12 * g + 2 * r + j + 1)
                    dt = pd[:, 4 * j:4 * j + 4, 1, :]
                    if r == 1:
                        dve.wait_ge(s.dt_init, 1 + g + 1)
                    else:
                        dve.wait_ge(s.dT_added, 1 + 10 * g + 2 * (r - 2) + j + 1)
                    dve.tensor_tensor(dt, DD[j][:, :].rearrange("p (c a n) -> p c a n", a=2, n=P)[:, :, 1, :], dt,
                                      ALU.add).then_inc(s.dT_added, 1)
            for j in range(2):
                dve.wait_ge(s.z_done, 1 + 2 * g + j + 1)
                dve.tensor_copy(x1[:, j * HALF:(j + 1) * HALF], DC[:, j * HALF:(j + 1) * HALF]).then_inc(s.z_copied, 1)

            def add_w(j):
                dve.wait_ge(s.w_done, 1 + 2 * g + j + 1)
                dve.tensor_tensor(v3(nT[:, j * HALF:(j + 1) * HALF]), v3(DD[j][:, HALF:2 * HALF]), pd[:, 4 * j:4 * j + 4, 1, :],
                                  ALU.add).then_inc(s.t_done, 1)
            add_w(0)
            for c in range(TT):
                j = c % 2
                dve.wait_ge(s.r_done, 1 + 8 * g + c + 1)
                if c >= 2:
                    dve.wait_ge(s.v_done, 1 + 8 * g + c - 1)
                dve.scalar_tensor_tensor(out=rbuf[:, j, :], in0=DA[:, 0:P], scalar=-1.0, in1=ch(vb, c), op0=ALU.mult,
                                         op1=ALU.add).then_inc(s.r_read, 1)
                if c == 0:
                    add_w(1)
                if c == 1:
                    rest_unit(k, dve, unit(h, 3), (base + 3) % 4, (base + 3) % 2)
                if c == 5:
                    rest_unit(k, dve, unit(h, 4), base % 4, base % 2)
                if c in (3, 4):
                    conv_tap(dve, h, hb, 1, 2 * c - 6)
                if c in (6, 7):
                    conv_tap(dve, h, hb, 2, 2 * c - 12)
                dve.wait_ge(s.ds_done, 1 + 8 * g + c + 1)
                if c == 0:
                    dve.wait_ge(k.s_zero, g + 1)
                else:
                    dve.wait_ge(s.s_done, 1 + 8 * g + c)
                dve.scalar_tensor_tensor(out=S[:, :], in0=S[:, :], scalar=k.gtot_e[:, bass.ds(g, 1), c:c + 1].rearrange("p a b -> p (a b)"),
                                         in1=DB[:, 0:P], op0=ALU.mult, op1=ALU.add).then_inc(s.s_done, 1)
                if c in (3, 4):
                    conv_tap(dve, h, hb, 1, 2 * c - 5)
                if c in (6, 7):
                    conv_tap(dve, h, hb, 2, 2 * c - 11)
            dve.wait_ge(s.s_done, 1 + 8 * g + 8)
            dve.memset(S[:, :], 0.0).then_inc(k.s_zero, 1)
            dve.wait_ge(s.o_rms, 1 + g + 1)
            dve.reciprocal(orms[:, :], orms[:, :]).then_inc(s.o_rs, 1)
            dve.wait_ge(s.o_rs, 1 + g + 1)
            dve.tensor_tensor(v3(x1[:, :]), v3(x1[:, :]), bc(orms[:, :], P), ALU.mult).then_inc(s.o_scaled, 1)
            dve.wait_ge(s.o_turned, 1 + g + 1)
            dve.scalar_tensor_tensor(out=pd[:, 4:8, :, :].rearrange("p c a n -> p (c a n)"), in0=DA[:, :], scalar=k.dn_g[:, :],
                                     in1=zT[b][:, :], op0=ALU.mult, op1=ALU.mult).then_inc(s.o_gated, 1)

        def pool_step(pool, g, b):
            pool.wait_ge(s.kn_copied, 1 + g + 1)
            pool.wait_ge(s.kde_done, 1 + g + 1)
            pool.tensor_tensor(tiles(kn[:, :]), tiles(kn[:, :]), bc(kde[:, :], P), ALU.mult).then_inc(s.kd_done, 1)
            pool.wait_ge(s.nT_done, 1 + g + 1)
            pool.wait_ge(s.o_stored, 1 + 16 * g)
            pool.wait_ge(s.o_copied, 1 + 8 * g)
            pool.tensor_tensor(pd[:, :, 0, :], tiles(nT[:, :]), rep(k.same[:, :], TT), ALU.mult).then_inc(s.p0T_done, 1)
            pool.wait_ge(s.p0T_done, 1 + g + 1)
            pool.tensor_tensor(pd[:, :, 1, :], pd[:, :, 0, :], rep(k.ident[:, :], TT), ALU.add).then_inc(s.dt_init, 1)
            pool.wait_ge(s.off_copied, 1 + g + 1)
            pool.tensor_tensor(tiles(no[:, :]), tiles(no[:, :]), rep(k.other[:, :], TT), ALU.mult).then_inc(s.off_done, 1)
            pool.wait_ge(s.an_exp, 1 + g + 1)
            pool.tensor_tensor(sqk[:, :], sqk[:, :], kTt[b][:, :], ALU.mult).then_inc(s.kbg_done, 1)
            pool.wait_ge(s.aq_exp, 1 + g + 1)
            pool.tensor_tensor(sqq[:, :], sqq[:, :], qT[b][:, :], ALU.mult).then_inc(s.qd_done, 1)

        oa = pd[:, 4:8, :, :].rearrange("p c a n -> p (c a n)")
        w_in = a["w_in"][0]

        def gate_columns(n):
            return columns(w_in, COL_GB + (FIRST_GATE + n) * P)

        with nc.Block() as block:
            @block.sync
            def _(sync):
                for h in range(HEADS):
                    for n, col in enumerate((COL_K, COL_V, COL_Z, COL_Q)):
                        if n < 3:
                            load_unit(k, sync, unit(h, n + 1), columns(w_in, col + h * P))
                        elif h + 1 < HEADS:
                            load_unit(k, sync, unit(h, n + 1), columns(w_in, col + (h + 1) * P))
                        else:
                            load_unit(k, sync, unit(h, n + 1), gate_columns(0))
                    if h:
                        sync.wait_ge(s.o_gated, 1 + h)
                        sync.dma_start(k.oaT[h - 1], oa).then_inc(s.o_stored, 16)
                for n in range(1, 4):
                    load_unit(k, sync, unit(HEADS, n), gate_columns(n))
                load_unit(k, sync, unit(HEADS, 4), k.next_unit)
                for n, gate in enumerate((qT[0], kTt[0], vT[0], zT[0])):
                    sync.wait_ge(s.proj_read, 1 + 8 * HEADS + 2 * n + 2)
                    sync.dma_start(k.gateB[FIRST_GATE + n], gate[:, :]).then_inc(s.gates_stored, 16)
                sync.wait_ge(s.o_gated, 1 + HEADS)
                sync.dma_start(k.oaT[HEADS - 1], oa).then_inc(s.o_stored, 16)
                sync.wait_ge(s.gates_stored, 1 + 16 * 4)
                sync.wait_ge(s.o_stored, 1 + 16 * HEADS)

            @block.tensor
            def _(pe):
                pe_step(pe, 0, None, None)
                with pe.Fori(0, (HEADS - 2) // 2) as i:
                    for j in range(2):
                        pe_step(pe, 2 * i + 1 + j, 2 * i + j, j)
                pe_step(pe, HEADS - 1, HEADS - 2, 0)
                pe_step(pe, HEADS, HEADS - 1, 1)

            @block.scalar
            def _(act):
                act_step(act, 0, 0, None)
                with act.Fori(0, (HEADS - 2) // 2) as i:
                    for j in range(2):
                        act_step(act, 2 * i + 1 + j, 1 - j, 2 * i + j)
                act_step(act, HEADS - 1, 1, HEADS - 2)
                act_step(act, HEADS, 0, HEADS - 1)

            @block.vector
            def _(dve):
                dve.memset(S[:, :], 0.0).then_inc(k.s_zero, 1)
                dve_step(dve, 0, 0, None, None)
                with dve.Fori(0, (HEADS - 2) // 2) as i:
                    for j in range(2):
                        dve_step(dve, 2 * i + 1 + j, 1 - j, 2 * i + j, j)
                dve_step(dve, HEADS - 1, 1, HEADS - 2, 0)
                dve_step(dve, HEADS, 0, HEADS - 1, 1)

            @block.gpsimd
            def _(pool):
                with pool.Fori(0, HEADS // 2) as i:
                    for j in range(2):
                        pool_step(pool, 2 * i + j, j)
        clear_semaphores(nc, k)



def split_act(k, act, u):
    round_unit(k, act, u, u % SPLIT_SLOTS, u % RAW_SLOTS)


def split_dve(k, dve, u):
    rest_unit(k, dve, u, u % SPLIT_SLOTS, u % RAW_SLOTS)


def product_half(k, pe, u, out, xh, xl, f, kt=KT, col=0, width=P, x0=None, n=HALF, part=None):
    x0 = f * HALF if x0 is None else x0
    slot = u % SPLIT_SLOTS
    ks = range(kt) if part is None else range(part * kt // 2, (part + 1) * kt // 2)
    for m in ks:
        c = m * width + col
        last = three(pe, out, k.whi[slot][:, c:c + P], k.wlo[slot][:, c:c + P],
                     xh[:, m, x0:x0 + n], xl[:, m, x0:x0 + n], m == 0, m == kt - 1)
    return last


def natural_unit(k, pe, u, banks, xh, xl, k0, k_last, done, rows=TT, read=None, first=0, final=True):
    slot = u % SPLIT_SLOTS
    for t in range(first, rows):
        if read is not None:
            pe.wait_ge(read[0], read[1] + t)
        for kk in range(2):
            m = k0 + kk
            lh, ll = xh[:, m, t * P:(t + 1) * P], xl[:, m, t * P:(t + 1) * P]
            wh, wl = k.whi[slot][:, kk * 512:(kk + 1) * 512], k.wlo[slot][:, kk * 512:(kk + 1) * 512]
            pe.matmul(banks[t], lh, wh, start=(m == 0), stop=False)
            pe.matmul(banks[t], lh, wl, start=False, stop=False)
            last = pe.matmul(banks[t], ll, wh, start=False, stop=(m == k_last))
        if done is not None and (t < rows - 1 or not final):
            last.then_inc(done, 1)
    if final:
        last.then_inc(k.w_used, 1)


def pair_columns(w, k0, c0):
    return w[k0 * P:(k0 + 2) * P, c0:c0 + 512].rearrange("(k p) n -> p k n", p=P)


def branch_a(nc, k, a, base):
    with ExitStack() as ctx:
        sb, sem = declare(nc, ctx, k)
        oah = sb("oah", [P, HEADS, SEQ], F32R)
        oal = sb("oal", [P, HEADS, SEQ], F32R)
        stage = [sb(f"oa_stage{i}", [P, SEQ]) for i in range(2)]
        ga = [sb(f"ga{i}", [P, SEQ]) for i in range(2)]
        gb = [sb(f"gb{i}", [P, SEQ]) for i in range(2)]
        ps = [ctx.enter_context(nc.psum_tensor(f"ba_ps{i}", [P, 1024], F32)) for i in range(4)]
        s = Names()
        s.oa_rounded = sem("ba_oa_rounded")
        s.oa_split = sem("ba_oa_split")
        s.ga_done = sem("ba_ga_done")
        s.gb_done = sem("ba_gb_done")
        s.gated = sem("ba_gated")
        oa_loaded = [queue_sem(nc, k, f"oa_loaded{i}") for i in range(2)]
        ga_stored = [queue_sem(nc, k, f"ga_stored{i}") for i in range(2)]
        gb_stored = [queue_sem(nc, k, f"gb_stored{i}") for i in range(2)]
        w_in, w_br = a["w_in"][0], a["w_br_a"][0]
        plan = [(0, 0), (1, 0), *((m, 1) for m in range(GATES_ELSEWHERE, KT))]
        for m in range(KT):
            plan += [(m, 2)] + ([(m + 2, 0)] if m + 2 < KT else [])

        def gates_stored(m):
            return len(range(m - 2, GATES_ELSEWHERE - 1, -2))

        def source(m, n):
            if n == 2:
                return w_br[:, bass.ds(m * P, P)].rearrange("(k p) n -> p k n", p=P)
            return w_in[:, bass.ds((COL_GA, COL_GB)[n] + m * P, P)].rearrange("(k p) n -> p k n", p=P)

        with nc.Block() as block:
            @block.sync
            def _(sync):
                for u in range(1, len(plan)):
                    load_unit(k, sync, base + u, source(*plan[u]))
                load_unit(k, sync, base + len(plan), k.next_unit)

            @block.gpsimd
            def _(pool):
                for h in range(HEADS):
                    if h >= 2:
                        pool.wait_ge(s.oa_split, h - 1)
                    pool.dma_start(stage[h % 2][:, :], k.oaT[h]).then_inc(oa_loaded[h % 2], 16)
                for m in range(KT):
                    if m >= GATES_ELSEWHERE:
                        pool.wait_ge(s.gb_done, m - GATES_ELSEWHERE + 1)
                        pool.dma_start(k.gateB[m], gb[m % 2][:, :]).then_inc(gb_stored[m % 2], 16)
                    pool.wait_ge(s.gated, m + 1)
                    pool.dma_start(k.hA[m], ga[m % 2][:, :]).then_inc(ga_stored[m % 2], 16)
                for i in range(2):
                    pool.wait_ge(ga_stored[i], 16 * (KT // 2))
                    pool.wait_ge(gb_stored[i], 16 * gates_stored(KT + i))

            @block.tensor
            def _(pe):
                for u, (m, n) in enumerate(plan):
                    out = ps[u % 4]
                    pe.wait_ge(k.w_split, base + u + 1)
                    if u >= 4:
                        mm, nn = plan[u - 4]
                        pe.wait_ge((s.ga_done, s.gb_done, s.gated)[nn], mm + 1 - (GATES_ELSEWHERE if nn == 1 else 0))
                    if n == 2:
                        pe.wait_ge(s.oa_split, HEADS)
                    xh, xl = (oah, oal) if n == 2 else (k.xh, k.xl)
                    for f in range(2):
                        last = product_half(k, pe, base + u, out[:, f * HALF:(f + 1) * HALF], xh, xl, f)
                    last.then_inc(k.w_used, 1)

            @block.scalar
            def _(act):
                for h in range(HEADS):
                    if h in (0, 4):
                        split_act(k, act, base + 1 + h // 4)
                    act.wait_ge(oa_loaded[h % 2], 16 * (h // 2 + 1))
                    act.activation(oah[:, h, :], stage[h % 2][:, :], ACT.Copy).then_inc(s.oa_rounded, 1)
                for u, (m, n) in enumerate(plan):
                    if 1 <= u <= len(plan) - 2:
                        split_act(k, act, base + u + 2)
                    if n < 2:
                        act.wait_ge(k.w_used, base + u + 1)
                        stored = m // 2 if n == 0 else gates_stored(m)
                        if stored:
                            act.wait_ge((ga_stored, gb_stored)[n][m % 2], 16 * stored)
                        act.activation((ga, gb)[n][m % 2][:, :], ps[u % 4][:, :], ACT.Sigmoid).then_inc((s.ga_done, s.gb_done)[n], 1)

            @block.vector
            def _(dve):
                for h in range(HEADS):
                    if h in (0, 4):
                        split_dve(k, dve, base + 1 + h // 4)
                    dve.wait_ge(s.oa_rounded, h + 1)
                    dve.tensor_tensor(oal[:, h, :], stage[h % 2][:, :], oah[:, h, :].bitcast(F32), ALU.subtract).then_inc(s.oa_split, 1)
                for u, (m, n) in enumerate(plan):
                    if 1 <= u <= len(plan) - 2:
                        split_dve(k, dve, base + u + 2)
                    if n == 2:
                        dve.wait_ge(k.w_used, base + u + 1)
                        dve.wait_ge(s.ga_done, m + 1)
                        dve.tensor_tensor(ga[m % 2][:, :], ps[u % 4][:, :], ga[m % 2][:, :], ALU.mult).then_inc(s.gated, 1)
        clear_semaphores(nc, k)


TWO_PI = 2.0 * math.pi
PI_1 = 6.28125
PI_2 = float(np.float32(TWO_PI - PI_1))
PI_3 = TWO_PI - PI_1 - PI_2
ROUND = 1.5 * 2.0 ** 23
PI_MAX = 3.1415925


def by_residue(ap, g):
    r = DILATIONS[g]
    return ap.rearrange("p (l r) -> p r l", r=r)


def attention(nc, k, a, base):
    with ExitStack() as ctx:
        sb, sem = declare(nc, ctx, k)
        cosT, sinT = sb("cosT", [P, SEQ]), sb("sinT", [P, SEQ])
        V = [sb(f"V{g}", [P, TT, P]) for g in range(GROUPS)]
        pr = [sb("pr0", [P, TT, 2 * P]), sb("pr1", [P, TT, 2 * P]), sb("pr2", [P, TT, P])]
        q = sb("q", [P, SEQ])
        kk = sb("k", [P, P + SEQ])
        A = sb("turn", [P, SEQ])
        SW = sb("swap", [P, SEQ])
        pT = sb("pT", [P, 2, HALF])
        OT = sb("OT", [P, SEQ])
        mask = sb("mask", [P, 2, 2 * P])
        mask2 = sb("mask2", [P, P])
        freq, sign = sb("freq", [P, 1]), sb("sign", [P, 1])
        mx = sb("mx", [P, 4])
        st = sb("st", [P, GROUPS, TT, 2])
        R = sb("R", [P, GROUPS * TT, GROUPS, 2])
        low = sb("low", [P, GROUPS * TT])
        ex = sb("ex", [P, GROUPS * TT, GROUPS])
        lw = sb("lw", [P, GROUPS * TT, GROUPS])
        coef = sb("coef", [P, GROUPS * TT])
        PA = [ctx.enter_context(nc.psum_tensor(f"at_p{i}", [P, 1024], F32)) for i in range(2)]
        SA = ctx.enter_context(nc.psum_tensor("SA", [P, 1024], F32))
        SB = ctx.enter_context(nc.psum_tensor("SB", [P, 1024], F32))
        s = Names()
        s.masks = sem("at_masks")
        s.gate_done = sem("at_gate_done")
        s.gate_stored = sem("at_gate_stored")
        s.pos_loaded = sem("at_pos_loaded")
        s.trig = sem("at_trig")
        s.sin_done = sem("at_sin_done")
        s.swapped = sem("at_swapped")
        s.a_done = sem("at_a_done")
        s.sw_done = sem("at_sw_done")
        s.roped = sem("at_roped")
        s.v_read = sem("at_v_read")
        s.v_turned = sem("at_v_turned")
        s.v_copied = sem("at_v_copied")
        s.s_scores = sem("at_s_scores")
        s.s_masked = sem("at_s_masked")
        s.mx_done = sem("at_mx_done")
        s.nm_done = sem("at_nm_done")
        s.exp_done = sem("at_exp_done")
        s.stat_loaded = sem("at_stat_loaded")
        s.stat_step = sem("at_stat_step")
        s.ex_done = sem("at_ex_done")
        s.coef_done = sem("at_coef_done")
        s.scaled = sem("at_scaled")
        s.p_turned = sem("at_p_turned")
        s.own_copied = sem("at_own_copied")
        s.prev_copied = sem("at_prev_copied")
        s.pv_done = sem("at_pv_done")
        s.o_added = sem("at_o_added")
        s.ob_rounded = sem("at_ob_rounded")
        s.ob_split = sem("at_ob_split")
        stat_put = [sem(f"stat_put{g}") for g in range(GROUPS)]
        gate = (q[:, :], SW[:, :], kk[:, P:P + SEQ])
        w_in = a["w_in"][0]
        scale = float(P) ** -0.5
        UN = 3 * GROUPS

        LAST = UN * HG

        def source(u):
            if u >= LAST:
                return columns(w_in, COL_GB + (u - LAST) * P)
            hh, g, n = u // UN, (u % UN) // 3, u % 3
            return columns(w_in, (COL_BQ, COL_BK, COL_BV)[n] + (g * HG + hh) * P)

        def rope_no(hh, g, n):
            return 6 * hh + 2 * g + n

        def it(hh, g):
            return 3 * hh + g

        with nc.Block() as block:
            @block.sync
            def _(sync):
                sync.dma_start(OT[:, :].bitcast(I32), a["positions"].partition_broadcast(P)).then_inc(s.pos_loaded, 16)
                sync.dma_start(freq[:, :], a["rope_freq"]).then_inc(s.pos_loaded, 16)
                for u in range(1, LAST + GATES_LATER):
                    load_unit(k, sync, base + u, source(u))
                load_unit(k, sync, base + LAST + GATES_LATER, k.next_unit)
                for e in range(GATES_LATER):
                    sync.wait_ge(s.gate_done, e + 1)
                    sync.dma_start(k.gateB[e], gate[e]).then_inc(s.gate_stored, 16)
                sync.wait_ge(s.gate_stored, 16 * GATES_LATER)

            @block.gpsimd
            def _(pool):
                pool.memset(mask[:, :, :], 0.0).then_inc(s.masks, 1)
                pool.memset(mask2[:, :], 0.0).then_inc(s.masks, 1)
                pool.memset(kk[:, 0:P], 0.0).then_inc(s.masks, 1)
                pool.memset(sign[:, :], 1.0).then_inc(s.masks, 1)
                pool.wait_ge(s.masks, 4)
                pool.memset(sign[0:64, :], -1.0).then_inc(s.masks, 1)
                pool.wait_ge(s.masks, 5)
                pool.memset(mask[:, 0, 0:P], NEG).then_inc(s.masks, 1)
                pool.affine_select(out=mask[:, 1, 0:P], in_=mask[:, 1, 0:P], compare_op=ALU.is_ge, fill=NEG,
                                   base=0, pattern=[[1, P]], channel_multiplier=-1).then_inc(s.masks, 1)
                for m in (mask[:, 0, P:2 * P], mask[:, 1, P:2 * P], mask2[:, :]):
                    pool.affine_select(out=m, in_=m, compare_op=ALU.is_ge, fill=NEG,
                                       base=0, pattern=[[-1, P]], channel_multiplier=1).then_inc(s.masks, 1)
                pool.wait_ge(s.masks, 10)
                pool.memset(mask2[64:P, 0:64], NEG).then_inc(s.masks, 1)

                for hh in range(HG):
                    for g in range(GROUPS):
                        for n in range(2):
                            i = rope_no(hh, g, n)
                            pool.wait_ge(s.swapped, 2 * (i + 1))
                            if i == 0:
                                pool.wait_ge(s.masks, 11)
                                pool.wait_ge(s.sin_done, 2)
                            pool.tensor_tensor(SW[:, :], SW[:, :], sinT[:, :], ALU.mult).then_inc(s.sw_done, 1)

            @block.tensor
            def _(pe):
                def half(u, f):
                    out = PA[u % 2]
                    if f == 0:
                        pe.wait_ge(k.w_split, base + u + 1)
                        if u >= LAST + 2:
                            pe.wait_ge(s.gate_done, u - LAST - 1)
                        elif u >= 2:
                            hh, g, n = (u - 2) // UN, ((u - 2) % UN) // 3, (u - 2) % 3
                            if n < 2:
                                pe.wait_ge(s.a_done, rope_no(hh, g, n) + 1)
                            else:
                                pe.wait_ge(s.v_read, it(hh, g) + 1)
                    last = product_half(k, pe, base + u, out[:, f * HALF:(f + 1) * HALF], k.xh, k.xl, f)
                    if f == 1:
                        last.then_inc(k.w_used, 1)

                def scores(hh, g, j):
                    out = (SA, SB)[j]
                    if j == 0:
                        pe.wait_ge(s.roped, rope_no(hh, g, 1) + 1)
                        if hh:
                            pe.wait_ge(s.o_added, it(hh - 1, g) + 1)
                    else:
                        if hh:
                            pe.wait_ge(s.prev_copied, 6 * (hh - 1) + 2 * g + 2)
                            pe.wait_ge(s.own_copied, 6 * (hh - 1) + 2 * g + 2)
                    i = it(hh, g)
                    if i:
                        pe.wait_ge(s.s_masked, 2 * (i - 1) + j + 1)
                        if j == 0:
                            pe.wait_ge(s.v_copied, i)
                    for i in range(4):
                        b = 4 * j + i
                        if g < 2:
                            last = pe.matmul(out[:, i * 256:(i + 1) * 256], q[:, b * P:(b + 1) * P],
                                             kk[:, b * P:(b + 2) * P], start=True, stop=True)
                        else:
                            last = pe.matmul(out[:, i * P:(i + 1) * P], q[:, b * P:(b + 1) * P],
                                             kk[:, (b + 1) * P:(b + 2) * P], start=True, stop=True)
                    last.then_inc(s.s_scores, 1)

                def turn_v(hh, g):
                    pe.wait_ge(s.v_read, it(hh, g) + 1)
                    pe.wait_ge(s.s_masked, 2 * it(hh, g) + 1)
                    for b in range(TT):
                        last = pe.transpose(SA[:, b * P:(b + 1) * P], A[:, b * P:(b + 1) * P], k.ident[:, :])
                    last.then_inc(s.v_turned, 1)

                def turn_p(hh, g, j):
                    pe.wait_ge(s.scaled, 2 * it(hh, g) + j + 1)
                    if j == 0:
                        pe.wait_ge(s.s_masked, 2 * min(it(hh + 1, g), 3 * HG))
                    if 6 * hh + 2 * g + j:
                        pe.wait_ge(s.own_copied, 6 * hh + 2 * g + j)
                        pe.wait_ge(s.prev_copied, 6 * hh + 2 * g + j)
                    for i in range(4):
                        b = 4 * j + i
                        own = pr[g][:, b, P:2 * P] if g < 2 else pr[g][:, b, :]
                        last = pe.transpose(SB[:, i * P:(i + 1) * P], own, k.ident[:, :])
                    if g < 2:
                        for i in range(4):
                            last = pe.transpose(SB[:, HALF + i * P:HALF + (i + 1) * P], pr[g][:, 4 * j + i, 0:P], k.ident[:, :])
                    last.then_inc(s.p_turned, 1)

                def has_prev(g, b):
                    return (g == 0 and b > 0) or (g == 1 and b % 2 == 1)

                def pv(hh, g, j):
                    n = 6 * hh + 2 * g + j + 1
                    pe.wait_ge(s.own_copied, n)
                    pe.wait_ge(s.prev_copied, n)
                    pe.wait_ge(s.v_copied, it(hh + 1, g) if hh + 1 < HG else 3 * HG)
                    if j == 0 and it(hh, g):
                        pe.wait_ge(s.o_added, it(hh, g))
                    for i in range(4):
                        b = 4 * j + i
                        out = SA[:, b * P:(b + 1) * P]
                        last = pe.matmul(out, V[g][:, b, :], pT[:, 0, i * P:(i + 1) * P], start=True, stop=not has_prev(g, b))
                        if has_prev(g, b):
                            last = pe.matmul(out, V[g][:, b - 1, :], pT[:, 1, i * P:(i + 1) * P], start=False, stop=True)
                    last.then_inc(s.pv_done, 1)

                for hh in range(HG):
                    for g in range(GROUPS):
                        u = UN * hh + 3 * g
                        half(u, 0)
                        if u:
                            turn_v(*((hh, g - 1) if g else (hh - 1, 2)))
                        half(u, 1)
                        if hh and g < 2:
                            half(u + 1, 0)
                            turn_p(hh - 1, g, 0)
                            half(u + 1, 1)
                            pv(hh - 1, g, 0)
                            turn_p(hh - 1, g, 1)
                            half(u + 2, 0)
                            pv(hh - 1, g, 1)
                            half(u + 2, 1)
                            scores(hh, g, 0)
                            scores(hh, g, 1)
                            continue
                        if hh:
                            turn_p(hh - 1, g, 0)
                        half(u + 1, 0)
                        if hh:
                            pv(hh - 1, g, 0)
                            turn_p(hh - 1, g, 1)
                        half(u + 1, 1)
                        if hh:
                            pv(hh - 1, g, 1)
                        half(u + 2, 0)
                        scores(hh, g, 0)
                        half(u + 2, 1)
                        scores(hh, g, 1)
                half(LAST, 0)
                turn_v(HG - 1, 2)
                half(LAST, 1)
                half(LAST + 1, 0)
                for g in range(GROUPS):
                    for j in range(2):
                        turn_p(HG - 1, g, j)
                        if 2 * g + j < 3:
                            half(LAST + 1 + (2 * g + j + 1) // 2, (2 * g + j + 1) % 2)
                        pv(HG - 1, g, j)

            @block.scalar
            def _(act):
                def copy_p(hh, g, j):
                    n = 6 * hh + 2 * g + j
                    act.wait_ge(s.p_turned, n + 1)
                    if n:
                        act.wait_ge(s.pv_done, n)
                    act.activation(pT[:, 0, :], SB[:, 0:HALF], ACT.Copy).then_inc(s.own_copied, 1)

                def read_v(hh, g, u):
                    act.wait_ge(k.w_used, base + u + 1)
                    i = rope_no(hh, g, 1) + 1
                    act.wait_ge(s.roped, i)
                    act.activation(A[:, :].rearrange("p (r l) -> p r l", r=DILATIONS[g]), by_residue(PA[u % 2][:, :], g),
                                   ACT.Copy).then_inc(s.v_read, 1)

                def put_stats(hh, g):
                    act.wait_ge(s.exp_done, 8 * (it(hh, g) + 1))
                    dst = k.stats[hh]
                    if g == 0:
                        act.dma_start(dst.rearrange("(b p) g c -> p b g c", p=P)[:, :, 0, :], st[:, 0, :, :]).then_inc(stat_put[g], 16)
                    elif g == 1:
                        v = dst.rearrange("(h p r) g c -> p r h g c", h=2, r=4)
                        for r in range(4):
                            act.dma_start(v[:, r, :, 1, :], st[:, 1, 2 * r:2 * r + 2, :]).then_inc(stat_put[g], 16)
                    else:
                        v = dst.rearrange("(l b s) g c -> s l b g c", b=8, s=2)
                        for half in range(2):
                            act.dma_start(v[half, :, :, 2, :], st[64 * half:64 * half + 64, 2, :, :]).then_inc(stat_put[g], 16)

                def load_stats(hh):
                    act.wait_ge(stat_put[0], 16 * (hh + 1))
                    act.wait_ge(stat_put[1], 64 * (hh + 1))
                    act.wait_ge(stat_put[2], 32 * (hh + 1))
                    if hh:
                        act.wait_ge(s.coef_done, 2 * hh)
                    src = k.stats[hh]
                    Rv = R[:, :, :, :].rearrange("p n g c -> p n (g c)")
                    act.dma_start(Rv[:, 0:8, :], src.rearrange("(b p) g c -> p b (g c)", p=P)).then_inc(s.stat_loaded, 16)
                    v = src.rearrange("(h p r) g c -> p r h (g c)", h=2, r=4)
                    for r in range(4):
                        act.dma_start(Rv[:, 8 + 2 * r:10 + 2 * r, :], v[:, r, :, :]).then_inc(s.stat_loaded, 16)
                    v = src.rearrange("(l b s) g c -> s l b (g c)", b=8, s=2)
                    for half in range(2):
                        act.dma_start(Rv[64 * half:64 * half + 64, 16:24, :], v[half]).then_inc(s.stat_loaded, 16)

                split_act(k, act, base + 1)
                split_act(k, act, base + 2)
                split_act(k, act, base + 3)
                act.wait_ge(s.trig, 10)
                act.activation(cosT[:, :], cosT[:, :], ACT.Sin).then_inc(s.sin_done, 1)
                act.wait_ge(s.trig, 16)
                act.wait_ge(s.masks, 5)
                act.activation(sinT[:, :], sinT[:, :], ACT.Sin, scale=sign[:, :]).then_inc(s.sin_done, 1)
                for hh in range(HG):
                    for g in range(GROUPS):
                        u0 = UN * hh + 3 * g
                        for n in range(2):
                            u = u0 + n
                            if u > 1:
                                split_act(k, act, base + u + 2)
                            if g == 0 and hh and n == 0:
                                load_stats(hh - 1)
                            if hh and n == 1:
                                copy_p(hh - 1, g, 0)
                                copy_p(hh - 1, g, 1)
                            act.wait_ge(k.w_used, base + u + 1)
                            if rope_no(hh, g, n):
                                act.wait_ge(s.roped, rope_no(hh, g, n))
                            act.activation(SW[0:64, :], PA[u % 2][64:P, :], ACT.Copy).then_inc(s.swapped, 1)
                            act.activation(SW[64:P, :], PA[u % 2][0:64, :], ACT.Copy).then_inc(s.swapped, 1)
                            if n == 0 and hh and g == 0:
                                act.wait_ge(s.stat_step, 3 * hh)
                                act.activation(ex[:, :, :], ex[:, :, :], ACT.Exp).then_inc(s.ex_done, 1)
                        split_act(k, act, base + u0 + 4)
                        read_v(hh, g, u0 + 2)
                        for j in range(2):
                            act.wait_ge(s.nm_done, 2 * it(hh, g) + j + 1)
                            if hh and j == 0:
                                act.wait_ge(stat_put[g], (16, 64, 32)[g] * hh)
                            for b in range(4 * j, 4 * j + 4):
                                w = pr[g][:, b, :]
                                act.activation(w, w, ACT.Exp, scale=scale, bias=st[:, g, b, 0:1],
                                               accum_out=st[:, g, b, 1:2]).then_inc(s.exp_done, 1)
                        put_stats(hh, g)
                        if hh:
                            if g == 2:
                                act.wait_ge(s.o_added, 3 * hh)
                                act.activation(k.obh[:, hh - 1, :], OT[:, :], ACT.Copy).then_inc(s.ob_rounded, 1)
                load_stats(HG - 1)
                act.wait_ge(s.stat_step, 3 * HG)
                act.activation(ex[:, :, :], ex[:, :, :], ACT.Exp).then_inc(s.ex_done, 1)
                split_act(k, act, base + LAST + 2)

                def sigmoid(e):
                    act.wait_ge(k.w_used, base + LAST + e + 1)
                    if e == 0:
                        act.wait_ge(s.s_scores, 2 * GROUPS * HG)
                    if e == 1:
                        act.wait_ge(s.roped, 2 * GROUPS * HG)
                    act.activation(gate[e], PA[(LAST + e) % 2][:, :], ACT.Sigmoid).then_inc(s.gate_done, 1)

                sigmoid(0)
                split_act(k, act, base + LAST + 3)
                for g in range(GROUPS):
                    for j in range(2):
                        copy_p(HG - 1, g, j)
                        if 2 * g + j in (0, 2):
                            sigmoid(1 + g)
                act.wait_ge(s.o_added, 3 * HG)
                act.activation(k.obh[:, HG - 1, :], OT[:, :], ACT.Copy).then_inc(s.ob_rounded, 1)

            @block.vector
            def _(dve):
                count = [0]

                def trig(ins):
                    ins.then_inc(s.trig, 1)
                    count[0] += 1
                    dve.wait_ge(s.trig, count[0])

                split_dve(k, dve, base + 1)
                dve.wait_ge(s.pos_loaded, 32)
                trig(dve.tensor_copy(A[:, :], OT[:, :].bitcast(I32)))
                trig(dve.tensor_scalar(A[:, :], A[:, :], freq[:, :], None, ALU.mult))
                for out in (cosT, sinT):
                    if out is cosT:
                        trig(dve.tensor_scalar(OT[:, :], A[:, :], 1.0 / TWO_PI, 0.25, ALU.mult, ALU.add))
                        trig(dve.tensor_scalar(OT[:, :], OT[:, :], ROUND, None, ALU.add))
                    else:
                        trig(dve.tensor_scalar(OT[:, :], A[:, :], 1.0 / TWO_PI, ROUND, ALU.mult, ALU.add))
                    trig(dve.tensor_scalar(OT[:, :], OT[:, :], -ROUND, None, ALU.add))
                    trig(dve.scalar_tensor_tensor(out=out[:, :], in0=OT[:, :], scalar=-PI_1, in1=A[:, :], op0=ALU.mult, op1=ALU.add))
                    trig(dve.scalar_tensor_tensor(out=out[:, :], in0=OT[:, :], scalar=-PI_2, in1=out[:, :], op0=ALU.mult, op1=ALU.add))
                    trig(dve.scalar_tensor_tensor(out=out[:, :], in0=OT[:, :], scalar=-PI_3, in1=out[:, :], op0=ALU.mult, op1=ALU.add))
                    if out is cosT:
                        trig(dve.tensor_scalar(out[:, :], out[:, :], 0.5 * math.pi, None, ALU.add))
                    trig(dve.tensor_scalar(out[:, :], out[:, :], PI_MAX, -PI_MAX, ALU.min, ALU.max))
                    split_dve(k, dve, base + 2 + (out is sinT))

                def coefs(hh):
                    dve.wait_ge(s.stat_loaded, 112 * (hh + 1))
                    nm = [R[:, :, g, 0] for g in range(GROUPS)]
                    dve.tensor_tensor(low[:, :], nm[0], nm[1], ALU.min).then_inc(s.stat_step, 1)
                    dve.wait_ge(s.stat_step, 3 * hh + 1)
                    dve.tensor_tensor(low[:, :], low[:, :], nm[2], ALU.min).then_inc(s.stat_step, 1)
                    dve.wait_ge(s.stat_step, 3 * hh + 2)
                    dve.tensor_tensor(ex[:, :, :], bc(low[:, :], GROUPS), R[:, :, :, 0], ALU.subtract).then_inc(s.stat_step, 1)
                    dve.wait_ge(s.ex_done, hh + 1)
                    dve.tensor_tensor(lw[:, :, :], ex[:, :, :], R[:, :, :, 1], ALU.mult).then_inc(s.coef_done, 1)
                    dve.wait_ge(s.coef_done, 2 * hh + 1)
                    dve.reduce_sum(low[:, :], lw[:, :, :], AX_X).then_inc(k.chain, 1)
                    dve.wait_ge(k.chain, 2 * hh + 1)
                    dve.reciprocal(low[:, :], low[:, :]).then_inc(k.chain, 1)
                    dve.wait_ge(k.chain, 2 * hh + 2)
                    for g in range(GROUPS):
                        last = dve.tensor_tensor(coef[:, g * TT:(g + 1) * TT], ex[:, g * TT:(g + 1) * TT, g],
                                                 low[:, g * TT:(g + 1) * TT], ALU.mult)
                    last.then_inc(s.coef_done, 1)

                def scale_p(hh, g):
                    if g == 0:
                        dve.wait_ge(s.coef_done, 2 * hh + 2)
                    for j in range(2):
                        p = pr[g][:, 4 * j:4 * j + 4, :]
                        dve.tensor_tensor(p, p, bc(coef[:, g * TT + 4 * j:g * TT + 4 * j + 4], p.shape[2]),
                                          ALU.mult).then_inc(s.scaled, 1)

                def copy_prev(hh, g, j):
                    n = 6 * hh + 2 * g + j
                    dve.wait_ge(s.p_turned, n + 1)
                    if n:
                        dve.wait_ge(s.pv_done, n)
                    if g < 2:
                        dve.tensor_copy(pT[:, 1, :], SB[:, HALF:2 * HALF]).then_inc(s.prev_copied, 1)
                    else:
                        dve.nop().then_inc(s.prev_copied, 1)

                def add_o(hh, g):
                    dve.wait_ge(s.pv_done, 6 * hh + 2 * g + 2)
                    src = SA[:, :].rearrange("p (r l) -> p r l", r=DILATIONS[g])
                    if g == 0:
                        if hh:
                            dve.wait_ge(s.ob_rounded, hh)
                            dve.wait_ge(s.ob_split, hh)
                        dve.tensor_copy(OT[:, :], SA[:, :]).then_inc(s.o_added, 1)
                    else:
                        dve.wait_ge(s.o_added, it(hh, g))
                        o = by_residue(OT[:, :], g)
                        dve.tensor_tensor(o, src, o, ALU.add).then_inc(s.o_added, 1)

                def rest_o(hh):
                    dve.wait_ge(s.ob_rounded, hh + 1)
                    dve.tensor_tensor(k.obl[:, hh, :], OT[:, :], k.obh[:, hh, :].bitcast(F32), ALU.subtract).then_inc(s.ob_split, 1)

                def copy_v(hh, g):
                    dve.wait_ge(s.v_turned, it(hh, g) + 1)
                    if hh:
                        dve.wait_ge(s.pv_done, 6 * (hh - 1) + 2 * g + 2)
                    dve.tensor_copy(V[g][:, :, :], tiles(SA[:, :])).then_inc(s.v_copied, 1)

                for hh in range(HG):
                    for g in range(GROUPS):
                        u0 = UN * hh + 3 * g
                        for n in range(2):
                            u, i = u0 + n, rope_no(hh, g, n)
                            if u > 1:
                                split_dve(k, dve, base + u + 2)
                            if n == 0 and u:
                                copy_v(*((hh, g - 1) if g else (hh - 1, 2)))
                            if hh and n == 0:
                                if g == 0:
                                    coefs(hh - 1)
                                scale_p(hh - 1, g)
                            if hh and n == 1:
                                copy_prev(hh - 1, g, 0)
                                copy_prev(hh - 1, g, 1)
                            dve.wait_ge(s.swapped, 2 * (i + 1))
                            if i == 0:
                                dve.wait_ge(s.sin_done, 1)
                            else:
                                dve.wait_ge(s.roped, i)
                                if n == 0:
                                    dve.wait_ge(s.v_turned, it(hh, g))
                            dve.tensor_tensor(A[:, :], PA[u % 2][:, :], cosT[:, :], ALU.mult).then_inc(s.a_done, 1)
                            dve.wait_ge(s.sw_done, i + 1)
                            dve.wait_ge(s.a_done, i + 1)
                            if it(hh, g):
                                dve.wait_ge(s.s_scores, 2 * it(hh, g))
                            if i == 0:
                                dve.wait_ge(s.masks, 11)
                            dst = (q[:, :], kk[:, P:P + SEQ])[n].rearrange("p (r l) -> p r l", r=DILATIONS[g])
                            dve.tensor_tensor(dst, by_residue(A[:, :], g), by_residue(SW[:, :], g), ALU.add).then_inc(s.roped, 1)
                        split_dve(k, dve, base + u0 + 4)
                        if hh:
                            add_o(hh - 1, g)
                        for j in range(2):
                            n = 2 * it(hh, g) + j
                            dve.wait_ge(s.s_scores, n + 1)
                            S = (SA, SB)[j]
                            if g == 2:
                                p = pr[g][:, 4 * j:4 * j + 4, :]
                                dve.tensor_tensor(p, tiles(S[:, 0:HALF]), rep(mask2[:, :], 4), ALU.add).then_inc(s.s_masked, 1)
                            elif g == 1:
                                p = pr[g][:, 4 * j:4 * j + 4, :]
                                p4 = p.rearrange("p (a b) n -> p a (b n)", b=2)
                                dve.tensor_tensor(p4, S[:, :].rearrange("p (a n) -> p a n", a=2),
                                                  rep(mask[:, :, :].rearrange("p b n -> p (b n)"), 2), ALU.add).then_inc(s.s_masked, 1)
                            else:
                                p = pr[g][:, 4 * j:4 * j + 4, :]
                                kind = 0 if j == 0 else 1
                                dve.tensor_tensor(p[:, 0, :], S[:, 0:256], mask[:, kind, :], ALU.add)
                                dve.tensor_tensor(p[:, 1:4, :], tiles(S[:, 256:1024], 256), rep(mask[:, 1, :], 3), ALU.add).then_inc(s.s_masked, 1)
                            dve.wait_ge(s.s_masked, n + 1)
                            if n:
                                dve.wait_ge(s.nm_done, n)
                            dve.reduce_max(mx[:, :], p, AX_X).then_inc(s.mx_done, 1)
                            dve.wait_ge(s.mx_done, n + 1)
                            if hh and j == 0:
                                dve.wait_ge(stat_put[g], (16, 64, 32)[g] * hh)
                            dve.tensor_scalar(st[:, g, 4 * j:4 * j + 4, 0], mx[:, :], -scale, None, ALU.mult).then_inc(s.nm_done, 1)
                        if hh and g == 2:
                            rest_o(hh - 1)
                copy_v(HG - 1, 2)
                coefs(HG - 1)
                scale_p(HG - 1, 0)
                split_dve(k, dve, base + LAST + 2)
                split_dve(k, dve, base + LAST + 3)
                for g in range(GROUPS):
                    if g < GROUPS - 1:
                        scale_p(HG - 1, g + 1)
                    copy_prev(HG - 1, g, 0)
                    copy_prev(HG - 1, g, 1)
                    add_o(HG - 1, g)
                rest_o(HG - 1)
        clear_semaphores(nc, k)


def merge(nc, k, a, base):
    with ExitStack() as ctx:
        sb, sem = declare(nc, ctx, k)
        ha = [sb(f"ha{i}", [P, SEQ]) for i in range(2)]
        gb = [sb(f"gbl{i}", [P, SEQ]) for i in range(2)]
        ps = [ctx.enter_context(nc.psum_tensor(f"mg_ps{i}", [P, 1024], F32)) for i in range(4)]
        s = Names()
        s.yb_done = sem("mg_yb_done")
        s.yb_gated = sem("mg_yb_gated")
        s.h_added = sem("mg_h_added")
        s.h_rounded = sem("mg_h_rounded")
        s.h_split = sem("mg_h_split")
        loaded = [queue_sem(nc, k, f"mg_loaded{i}") for i in range(2)]
        w = a["w_br_b"][0]

        with nc.Block() as block:
            @block.sync
            def _(sync):
                for i in range(1, 4):
                    load_unit(k, sync, base + i, w[:, 2 * i * P:2 * (i + 1) * P].rearrange("(k p) n -> p k n", p=P))
                load_unit(k, sync, base + 4, k.next_unit)

            @block.gpsimd
            def _(pool):
                for m in range(KT):
                    if m >= 2:
                        pool.wait_ge(s.h_split, m - 1)
                    pool.dma_start(ha[m % 2][:, :], k.hA[m]).then_inc(loaded[m % 2], 16)
                    pool.dma_start(gb[m % 2][:, :], k.gateB[m]).then_inc(loaded[m % 2], 16)

            @block.tensor
            def _(pe):
                for m in range(KT):
                    u = base + m // 2
                    if m % 2 == 0:
                        pe.wait_ge(k.w_split, u + 1)
                    if m >= 4:
                        pe.wait_ge(s.yb_gated, m - 3)
                    for f in range(2):
                        last = product_half(k, pe, u, ps[m % 4][:, f * HALF:(f + 1) * HALF], k.obh, k.obl, f,
                                            kt=HG, col=(m % 2) * P, width=2 * P)
                    last.then_inc(s.yb_done if m % 2 == 0 else k.w_used, 1)

            @block.scalar
            def _(act):
                for m in range(KT):
                    if m % 2 == 0:
                        split_act(k, act, base + m // 2 + 1)
                    act.wait_ge(s.h_added, m + 1)
                    act.activation(k.xh[:, m, :], gb[m % 2][:, :], ACT.Copy).then_inc(s.h_rounded, 1)

            @block.vector
            def _(dve):
                for m in range(KT):
                    if m % 2 == 0:
                        split_dve(k, dve, base + m // 2 + 1)
                        dve.wait_ge(s.yb_done, m // 2 + 1)
                    else:
                        dve.wait_ge(k.w_used, base + m // 2 + 1)
                    dve.wait_ge(loaded[m % 2], 32 * (m // 2 + 1))
                    g = gb[m % 2][:, :]
                    dve.tensor_tensor(g, ps[m % 4][:, :], g, ALU.mult).then_inc(s.yb_gated, 1)
                    dve.wait_ge(s.yb_gated, m + 1)
                    dve.tensor_tensor(g, g, ha[m % 2][:, :], ALU.add).then_inc(s.h_added, 1)
                    dve.wait_ge(s.h_rounded, m + 1)
                    dve.tensor_tensor(k.xl[:, m, :], g, k.xh[:, m, :].bitcast(F32), ALU.subtract).then_inc(s.h_split, 1)
        clear_semaphores(nc, k)


def project_and_norm(nc, k, name, base, w, inh, inl, residual, res_gain, res_bias, gain, bias, outh, outl, y_dram):
    with ExitStack() as ctx:
        sb0, sem0 = declare(nc, ctx, k)

        def sb(n, *r):
            return sb0(name + n, *r)

        def sem(n):
            return sem0(name + n)
        X = sb("X", [P, TT, D_MODEL])
        gT, bT = sb("gT", [P, KT]), sb("bT", [P, KT])
        rows = sb("rows", [2 * KT, P])
        tmp = sb("tmp", [P, 3, HALF])
        row = tmp[:, 0:2, :].rearrange("p a n -> p (a n)")
        bst, mv = sb("bst", [P, TT, 12]), sb("mv", [P, TT, 2])
        rs, nmr = sb("rs", [P, TT]), sb("nmr", [P, TT])
        ps = [ctx.enter_context(nc.psum_tensor(f"{name}ps{i}", [P, 512], F32)) for i in range(8)]
        s = Names()
        s.loaded = [sem(f"loaded{i}") for i in range(2)]
        s.rows_loaded = sem("rows_loaded")
        s.gain_loaded = queue_sem(nc, k, name + "gain_loaded")
        s.bank_done = sem("bank_done")
        s.summed = sem("summed")
        s.sums_done = sem("sums_done")
        s.stats_done = sem("stats_done")
        s.dev_done = sem("dev_done")
        s.rs_done = sem("rs_done")
        s.normed = sem("normed")
        s.turned = sem("turned")
        s.gain_by_vector = sem("gain_by_vector")
        s.gain_by_scalar = sem("gain_by_scalar")
        s.res_biased = sem("res_biased")
        s.rounded = sem("rounded")
        s.split = sem("split")
        s.gT_turned = sem("gT_turned")
        s.gT_copied = sem("gT_copied")
        s.nmr_done = sem("nmr_done")
        s.res_scaled = sem("res_scaled")
        s.res_ready = sem("res_ready")
        s.y_stored = sem("y_stored")
        NU = 8

        def slot(n):
            return 1 + n // 2 % 2 if n % 2 else 0

        def bank(n):
            return n % 4 if n < 8 else n % 8

        def wait_bank(eng, n, t):
            if t < TT - 1:
                eng.wait_ge(s.bank_done, (TT - 1) * n + t + 1)
            else:
                eng.wait_ge(k.w_used, base + 4 * n + 4)

        with nc.Block() as block:
            @block.sync
            def _(sync):
                def load_residual(t0, t1):
                    for t in range(t0, t1):
                        sync.dma_start(X[:, t, :], residual[t * P:(t + 1) * P, :]).then_inc(s.loaded[t // 4], 16)

                sync.dma_start(rows[0:KT, :], gain.rearrange("l (m p) -> (l m) p", p=P)).then_inc(s.rows_loaded, 16)
                sync.dma_start(rows[KT:2 * KT, :], bias.rearrange("l (m p) -> (l m) p", p=P)).then_inc(s.rows_loaded, 16)
                for i in range(1, NU):
                    load_unit(k, sync, base + i, pair_columns(w, 2 * (i % 4), 512 * (i // 4)))
                    if i < 3:
                        load_residual(4 * i - 4, 4 * i)
                load_unit(k, sync, base + NU, k.next_unit)
                for t in range(TT):
                    sync.wait_ge(s.normed, t + 1)
                    sync.dma_start(y_dram[t * P:(t + 1) * P, :], X[:, t, :]).then_inc(s.y_stored, 16)
                sync.wait_ge(s.y_stored, 16 * TT)

            @block.tensor
            def _(pe):
                def product(n, i, read=None, first=0, rows=TT, final=True):
                    u = base + 4 * n + i
                    pe.wait_ge(k.w_split, u + 1)
                    natural_unit(k, pe, u, [b[:, :] for b in ps], inh, inl, 2 * i, KT - 1, s.bank_done if i == 3 else None,
                                 rows=rows, read=read, first=first, final=final)

                def turn(n0, n1):
                    for n in range(n0, n1):
                        G, m = n // KT, n % KT
                        if n < 4:
                            pe.wait_ge(s.summed, TT + n + 1)
                        elif n < 12:
                            pe.wait_ge((s.gain_by_vector, s.gain_by_scalar)[n % 2], (n - 4) // 2 + 1)
                        else:
                            pe.wait_ge(s.summed, TT + n - 7)
                        for t in range(4):
                            last = pe.transpose(ps[bank(n)][:, t * P:(t + 1) * P], X[:, 4 * G + t, m * P:(m + 1) * P], k.ident[:, :])
                        last.then_inc(s.turned, 1)

                for i in range(4):
                    product(0, i)
                pe.wait_ge(s.summed, 1)
                pe.wait_ge(s.rows_loaded, 32)
                pe.transpose(ps[0][:, 0:2 * KT], rows[:, :], k.ident[0:2 * KT, 0:2 * KT]).then_inc(s.gT_turned, 1)
                pe.wait_ge(s.gT_copied, 1)
                for i in range(4):
                    product(1, i, read=(s.summed, 1) if i == 0 else None, rows=4, final=False)
                for i in range(4):
                    product(1, i, read=(s.summed, 1) if i == 0 else None, first=4)
                    if i < 2:
                        if i == 0:
                            pe.wait_ge(s.normed, 4)
                        turn(4 * i, 4 * i + 4)
                pe.wait_ge(s.normed, 8)
                turn(8, 16)

            @block.scalar
            def _(act):
                split_act(k, act, base + 1)
                for i in range(NU - 2):
                    split_act(k, act, base + i + 2)
                    if i == 3:
                        act.wait_ge(s.gT_turned, 1)
                        act.activation(gT[:, :], ps[0][:, 0:KT], ACT.Copy)
                        act.activation(bT[:, :], ps[0][:, KT:2 * KT], ACT.Copy).then_inc(s.gT_copied, 1)

                def norm(t):
                    act.wait_ge(s.nmr_done, t + 1)
                    act.activation(X[:, t, :], X[:, t, :], ACT.Identity, scale=rs[:, t:t + 1],
                                   bias=nmr[:, t:t + 1]).then_inc(s.normed, 1)

                for G in range(2):
                    for t in range(4 * G, 4 * G + 4):
                        act.wait_ge(s.stats_done, t + 1)
                        act.activation(rs[:, t:t + 1], mv[:, t, 1:2], ACT.Sqrt, bias=k.eps_ln[:, :]).then_inc(s.dev_done, 1)
                        if t % 4:
                            norm(t - 1)
                    norm(4 * G + 3)
                    if G == 0:
                        split_act(k, act, base + NU)
                    for n in range(8 * G, 8 * G + 8):
                        m = n % KT
                        act.wait_ge(s.turned, n + 1)
                        act.activation(outh[:, m, G * HALF:(G + 1) * HALF], ps[bank(n)][:, :], ACT.Identity,
                                       scale=gT[:, m:m + 1], bias=bT[:, m:m + 1]).then_inc(s.rounded, 1)
                        if n % 2:
                            if n >= 4:
                                act.wait_ge(s.split, n - 3)
                            act.activation(tmp[:, slot(n), :], ps[bank(n)][:, :], ACT.Identity,
                                           scale=gT[:, m:m + 1], bias=bT[:, m:m + 1]).then_inc(s.gain_by_scalar, 1)

            def add_up(dve, n, t):
                wait_bank(dve, n, t)
                if n == 0 and res_gain is None:
                    dve.wait_ge(s.loaded[t // 4], 16 * TT // 2)
                elif n == 0 and t < TT // 2:
                    dve.wait_ge(s.res_ready, t + 1)
                elif n == 0:
                    dve.wait_ge(s.res_biased, t - TT // 2 + 1)
                v = X[:, t, n * 512:(n + 1) * 512]
                dve.scalar_tensor_tensor(out=v, in0=v, scalar=ALPHA, in1=ps[t][:, :], op0=ALU.mult, op1=ALU.add).then_inc(s.summed, 1)
                dve.wait_ge(s.summed, n * TT + t + 1)
                dve.bn_stats(bst[:, t, 6 * n:6 * n + 6], v).then_inc(s.sums_done, 1)

            def rest(dve, n):
                G, m = n // 8, n % 8
                dve.wait_ge((s.gain_by_vector, s.gain_by_scalar)[n % 2], n // 2 + 1)
                dve.tensor_tensor(outl[:, m, G * HALF:(G + 1) * HALF], tmp[:, slot(n), :],
                                  outh[:, m, G * HALF:(G + 1) * HALF].bitcast(F32), ALU.subtract).then_inc(s.split, 1)

            def shift(dve, t):
                dve.wait_ge(s.dev_done, t + 1)
                dve.reciprocal(rs[:, t:t + 1], rs[:, t:t + 1]).then_inc(s.rs_done, 1)
                dve.wait_ge(s.rs_done, t + 1)
                dve.tensor_scalar(nmr[:, t:t + 1], mv[:, t, 0:1], rs[:, t:t + 1], -1.0, ALU.mult, ALU.mult).then_inc(s.nmr_done, 1)

            @block.vector
            def _(dve):
                split_dve(k, dve, base + 1)
                for i in range(NU - 2):
                    split_dve(k, dve, base + i + 2)
                    if i < 2 and res_gain is not None:
                        if i == 0:
                            dve.wait_ge(s.gain_loaded, 16)
                        dve.wait_ge(s.loaded[i], 16 * TT // 2)
                        for t in range(4 * i, 4 * i + 4):
                            dve.tensor_tensor(X[:, t, :], X[:, t, :], row, ALU.mult).then_inc(s.res_scaled, 1)
                    if i == 2 and res_gain is not None:
                        dve.wait_ge(s.gain_loaded, 32)
                        for t in range(TT // 2, TT):
                            dve.tensor_tensor(X[:, t, :], X[:, t, :], row, ALU.add).then_inc(s.res_biased, 1)
                    if i == 3:
                        for t in range(TT):
                            add_up(dve, 0, t)
                for G in range(2):
                    for t in range(4 * G, 4 * G + 4):
                        add_up(dve, 1, t)
                        dve.wait_ge(s.sums_done, TT + t + 1)
                        dve.bn_aggr(mv[:, t, :], bst[:, t, :]).then_inc(s.stats_done, 1)
                        if t % 4:
                            shift(dve, t - 1)
                    shift(dve, 4 * G + 3)
                    if G == 0:
                        split_dve(k, dve, base + NU)
                    for n in range(8 * G, 8 * G + 8):
                        m = n % KT
                        if n % 2 == 0:
                            dve.wait_ge(s.rounded, n + 1)
                            if n >= 2:
                                dve.wait_ge(s.split, n - 1)
                            dve.tensor_scalar(tmp[:, 0, :], ps[bank(n)][:, :], gT[:, m:m + 1], bT[:, m:m + 1],
                                              ALU.mult, ALU.add).then_inc(s.gain_by_vector, 1)
                        if n % 8:
                            rest(dve, n - 1)
                    rest(dve, 8 * G + 7)

            @block.gpsimd
            def _(pool):
                if res_gain is None:
                    return
                pool.dma_start(row, res_gain.partition_broadcast(P)).then_inc(s.gain_loaded, 16)
                pool.wait_ge(s.res_scaled, TT)
                pool.dma_start(row, res_bias.partition_broadcast(P)).then_inc(s.gain_loaded, 16)
                pool.wait_ge(s.gain_loaded, 32)
                for t in range(TT // 2):
                    pool.tensor_tensor(X[:, t, :], X[:, t, :], row, ALU.add).then_inc(s.res_ready, 1)
        clear_semaphores(nc, k)


def cross_attention(nc, k, a, base, oh, ol):
    with ExitStack() as ctx:
        sb, sem = declare(nc, ctx, k)
        kT = sb("xkT", [P, KT, MEM])
        v = sb("xv", [P, 2, D_MODEL])
        pr = sb("xp", [P, 4, MEM])
        with ExitStack() as early:
            mh = early.enter_context(nc.sbuf_tensor("memh", [P, KT, MEM], F32R))
            ml = early.enter_context(nc.sbuf_tensor("meml", [P, KT, MEM], F32R))
        qT = sb("xqT", [P, 2, SEQ])
        pT = sb("xpT", [P, 2, HALF])
        mn = [pr[:, :, :].rearrange("p a n -> p (a n)"), v[:, 1, :]]
        mx, nm, l = sb("xmx", [P, 4]), sb("xnm", [P, 4]), sb("xl_", [P, 4])
        ps = [ctx.enter_context(nc.psum_tensor(f"x_ps{i}", [P, 1024], F32)) for i in range(4)]
        s = Names()
        s.m_turned = sem("ca_m_turned")
        s.m_rounded = sem("ca_m_rounded")
        s.m_split = sem("ca_m_split")
        s.k_copied = sem("ca_k_copied")
        s.v_bank = sem("ca_v_bank")
        s.v_copied = sem("ca_v_copied")
        s.q_copied = sem("ca_q_copied")
        s.x_scores = sem("ca_x_scores")
        s.x_max = sem("ca_x_max")
        s.x_nm = sem("ca_x_nm")
        s.x_exp = sem("ca_x_exp")
        s.x_rec = sem("ca_x_rec")
        s.x_norm = sem("ca_x_norm")
        s.x_turned = sem("ca_x_turned")
        s.x_copied = sem("ca_x_copied")
        s.x_copied1 = sem("ca_x_copied1")
        s.x_pv = sem("ca_x_pv")
        s.x_rounded = sem("ca_x_rounded")
        s.x_split_o = sem("ca_x_split_o")
        m_loaded = [sem(f"m_loaded{t}") for t in range(2)]
        w_kv, w_q = a["w_xkv"][0], a["w_xq"][0]
        scale = float(XD) ** -0.5

        def source(i):
            if i < 8:
                return columns(w_kv, i * P)
            if i < 16:
                return pair_columns(w_kv, 2 * (i % 4), D_MODEL + 512 * ((i - 8) // 4))
            return columns(w_q, (i - 16) * P)

        with nc.Block() as block:
            @block.sync
            def _(sync):
                for t in range(2):
                    sync.dma_start(mn[t], a["mem"][0, t * P:(t + 1) * P, :]).then_inc(m_loaded[t], 16)
                for i in range(1, 24):
                    load_unit(k, sync, base + i, source(i))
                load_unit(k, sync, base + 24, k.next_unit)

            @block.tensor
            def _(pe):
                for t in range(2):
                    pe.wait_ge(m_loaded[t], 16)
                    for f in range(2):
                        for i in range(4):
                            last = pe.transpose(ps[t][:, f * HALF + i * P:f * HALF + (i + 1) * P],
                                                mn[t][:, (4 * f + i) * P:(4 * f + i + 1) * P], k.ident[:, :])
                        last.then_inc(s.m_turned, 1)
                for i in range(8):
                    u = base + i
                    pe.wait_ge(k.w_split, u + 1)
                    if i == 0:
                        pe.wait_ge(s.m_split, 4)
                    if i >= 2:
                        pe.wait_ge(s.k_copied, i - 1)
                    product_half(k, pe, u, ps[2 + i % 2][:, 0:MEM], mh, ml, 0, x0=0, n=MEM).then_inc(k.w_used, 1)
                for n in range(2):
                    banks = [ps[n][:, 0:512], ps[n][:, 512:1024]]
                    for i in range(4):
                        u = base + 8 + 4 * n + i
                        pe.wait_ge(k.w_split, u + 1)
                        natural_unit(k, pe, u, banks, mh, ml, 2 * i, KT - 1, s.v_bank if i == 3 else None, rows=2)

                def query(h, d):
                    i = 2 * h + d
                    u = base + 16 + i
                    pe.wait_ge(k.w_split, u + 1)
                    if i >= 1:
                        pe.wait_ge(s.q_copied, 2 * i)
                    if i == 0:
                        pe.wait_ge(s.k_copied, 8)
                    for f in range(2):
                        last = product_half(k, pe, u, ps[3][:, f * HALF:(f + 1) * HALF], k.xh, k.xl, f)
                    last.then_inc(k.w_used, 1)

                def scores(h, j):
                    n = 2 * h + j
                    pe.wait_ge(s.q_copied, 4 * h + 4)
                    if n == 0:
                        pe.wait_ge(s.v_copied, 4)
                    if n:
                        pe.wait_ge(s.x_exp, 4 * n)
                    for i in range(4):
                        for d in range(2):
                            last = pe.matmul(ps[0][:, i * MEM:(i + 1) * MEM], qT[:, d, (4 * j + i) * P:(4 * j + i + 1) * P],
                                             kT[:, 2 * h + d, :], start=(d == 0), stop=(d == 1))
                    last.then_inc(s.x_scores, 1)

                def turn(h, j):
                    n = 2 * h + j
                    pe.wait_ge(s.x_norm, n + 1)
                    if n:
                        pe.wait_ge(s.x_copied, n)
                        pe.wait_ge(s.x_copied1, n)
                    for m in range(2):
                        for i in range(4):
                            last = pe.transpose(ps[1][:, m * HALF + i * P:m * HALF + (i + 1) * P], pr[:, i, m * P:(m + 1) * P], k.ident[:, :])
                    last.then_inc(s.x_turned, 1)

                def pv(h, j):
                    n = 2 * h + j
                    pe.wait_ge(s.x_copied, n + 1)
                    pe.wait_ge(s.x_copied1, n + 1)
                    if n:
                        pe.wait_ge(s.x_split_o, n)
                    for d in range(2):
                        for m in range(2):
                            last = pe.matmul(ps[2][:, d * HALF:(d + 1) * HALF], v[:, m, (2 * h + d) * P:(2 * h + d + 1) * P],
                                             pT[:, m, :], start=(m == 0), stop=(m == 1))
                    last.then_inc(s.x_pv, 1)

                query(0, 0)
                query(0, 1)
                for h in range(XH):
                    scores(h, 0)
                    nxt = h + 1 < XH
                    if nxt:
                        query(h + 1, 0)
                    turn(h, 0)
                    scores(h, 1)
                    pv(h, 0)
                    if nxt:
                        query(h + 1, 1)
                    turn(h, 1)
                    pv(h, 1)

            @block.scalar
            def _(act):
                for n in range(4):
                    t, f = n // 2, n % 2
                    act.wait_ge(s.m_turned, n + 1)
                    act.activation(mh[:, 4 * f:4 * f + 4, t * P:(t + 1) * P], tiles(ps[t][:, f * HALF:(f + 1) * HALF]), ACT.Copy).then_inc(s.m_rounded, 1)
                split_act(k, act, base + 1)
                for i in range(16):
                    split_act(k, act, base + i + 2)
                    if i < 8:
                        act.wait_ge(k.w_used, base + i + 1)
                        act.activation(kT[:, i, :], ps[2 + i % 2][:, 0:MEM], ACT.Copy).then_inc(s.k_copied, 1)
                    elif i % 4 == 3:
                        n = (i - 8) // 4
                        for t in range(2):
                            if t == 0:
                                act.wait_ge(s.v_bank, n + 1)
                            else:
                                act.wait_ge(k.w_used, base + i + 1)
                            act.activation(v[:, t, n * 512:(n + 1) * 512], ps[n][:, t * 512:(t + 1) * 512], ACT.Copy).then_inc(s.v_copied, 1)

                def copy_q(h, d):
                    i = 2 * h + d
                    if h:
                        act.wait_ge(s.x_scores, 2 * h)
                    act.wait_ge(k.w_used, base + 16 + i + 1)
                    for f in range(2):
                        act.activation(qT[:, d, f * HALF:(f + 1) * HALF], ps[3][:, f * HALF:(f + 1) * HALF], ACT.Copy).then_inc(s.q_copied, 1)

                def exps(h, j):
                    n = 2 * h + j
                    act.wait_ge(s.x_nm, n + 1)
                    if n:
                        act.wait_ge(s.x_turned, n)
                        act.wait_ge(s.x_norm, n)
                    for i in range(4):
                        act.activation(pr[:, i, :], ps[0][:, i * MEM:(i + 1) * MEM], ACT.Exp, scale=scale, bias=nm[:, i:i + 1],
                                       accum_out=l[:, i:i + 1]).then_inc(s.x_exp, 1)

                def copy_p1(h, j):
                    n = 2 * h + j
                    act.wait_ge(s.x_turned, n + 1)
                    if n:
                        act.wait_ge(s.x_pv, n)
                    act.activation(pT[:, 1, :], ps[1][:, HALF:2 * HALF], ACT.Copy).then_inc(s.x_copied1, 1)

                def round_o(h, j):
                    n = 2 * h + j
                    act.wait_ge(s.x_pv, n + 1)
                    act.activation(oh[:, 2 * h:2 * h + 2, j * HALF:(j + 1) * HALF], tiles(ps[2][:, :], HALF), ACT.Copy).then_inc(s.x_rounded, 1)

                copy_q(0, 0)
                split_act(k, act, base + 18)
                copy_q(0, 1)
                for h in range(XH):
                    nxt = h + 1 < XH
                    exps(h, 0)
                    if nxt:
                        split_act(k, act, base + 16 + 2 * h + 3)
                    copy_p1(h, 0)
                    if nxt:
                        copy_q(h + 1, 0)
                    exps(h, 1)
                    round_o(h, 0)
                    if nxt:
                        split_act(k, act, base + 16 + 2 * h + 4)
                        copy_q(h + 1, 1)
                    copy_p1(h, 1)
                    round_o(h, 1)

            @block.vector
            def _(dve):
                for n in range(4):
                    t, f = n // 2, n % 2
                    dve.wait_ge(s.m_rounded, n + 1)
                    o = slice(4 * f, 4 * f + 4)
                    dve.tensor_tensor(ml[:, o, t * P:(t + 1) * P], tiles(ps[t][:, f * HALF:(f + 1) * HALF]),
                                      mh[:, o, t * P:(t + 1) * P].bitcast(F32), ALU.subtract).then_inc(s.m_split, 1)
                split_dve(k, dve, base + 1)
                for i in range(16):
                    split_dve(k, dve, base + i + 2)

                def soft(h, j):
                    n = 2 * h + j
                    dve.wait_ge(s.x_scores, n + 1)
                    if n:
                        dve.wait_ge(s.x_nm, n)
                    dve.reduce_max(mx[:, :], tiles(ps[0][:, :], MEM), AX_X).then_inc(s.x_max, 1)
                    dve.wait_ge(s.x_max, n + 1)
                    if n:
                        dve.wait_ge(s.x_exp, 4 * n)
                    dve.tensor_scalar(nm[:, :], mx[:, :], -scale, None, ALU.mult).then_inc(s.x_nm, 1)
                    dve.wait_ge(s.x_exp, 4 * n + 4)
                    dve.reciprocal(l[:, :], l[:, :]).then_inc(s.x_rec, 1)
                    dve.wait_ge(s.x_rec, n + 1)
                    dve.tensor_tensor(pr[:, :, :], pr[:, :, :], bc(l[:, :], MEM), ALU.mult).then_inc(s.x_norm, 1)

                def copy_p(h, j):
                    n = 2 * h + j
                    dve.wait_ge(s.x_turned, n + 1)
                    if n:
                        dve.wait_ge(s.x_pv, n)
                    dve.tensor_copy(pT[:, 0, :], ps[1][:, 0:HALF]).then_inc(s.x_copied, 1)

                def rest_o(h, j):
                    n = 2 * h + j
                    dve.wait_ge(s.x_rounded, n + 1)
                    o = slice(2 * h, 2 * h + 2)
                    dve.tensor_tensor(ol[:, o, j * HALF:(j + 1) * HALF], tiles(ps[2][:, :], HALF),
                                      oh[:, o, j * HALF:(j + 1) * HALF].bitcast(F32), ALU.subtract).then_inc(s.x_split_o, 1)

                split_dve(k, dve, base + 18)
                for h in range(XH):
                    nxt = h + 1 < XH
                    soft(h, 0)
                    if nxt:
                        split_dve(k, dve, base + 16 + 2 * h + 3)
                    copy_p(h, 0)
                    soft(h, 1)
                    if nxt:
                        split_dve(k, dve, base + 16 + 2 * h + 4)
                    rest_o(h, 0)
                    copy_p(h, 1)
                    rest_o(h, 1)
        clear_semaphores(nc, k)


def feed_forward(nc, k, a, base, xh, xl, gh, gl, out):
    parts = (6, 6, 6, 4)
    with ExitStack() as ctx:
        sb, sem = declare(nc, ctx, k)
        X = sb("fX", [P, TT, D_MODEL])
        sa = sb("sa", [P, 2, HALF])
        row = sb("row", [P, HALF])
        bst, mv, rs = sb("fbst", [P, TT, 12]), sb("fmv", [P, TT, 2]), sb("frs", [P, TT])
        by_vector, by_gpsimd = (3, 5, 7), (0, 1, 2, 4, 6)
        nmr = sb("fnmr", [P, TT])
        psall = [ctx.enter_context(nc.psum_tensor(f"f_ps{i}", [P, 1024], F32)) for i in range(4)]
        banks = [psall[i // 2][:, (i % 2) * 512:(i % 2 + 1) * 512] for i in range(8)]
        s = Names()
        s.f_loaded = sem("ff_f_loaded")
        s.f_res = sem("ff_f_res")
        s.silu_a = sem("ff_silu_a")
        s.prod = sem("ff_prod")
        s.rnd = sem("ff_rnd")
        s.rest = sem("ff_rest")
        s.bank_done = sem("ff_bank_done")
        s.y_added = sem("ff_y_added")
        s.f_stat = sem("ff_f_stat")
        s.f_stats = sem("ff_f_stats")
        s.f_dev = sem("ff_f_dev")
        s.f_rs = sem("ff_f_rs")
        s.f_nmr = sem("ff_f_nmr")
        s.f_norm = sem("ff_f_norm")
        s.f_biased = sem("ff_f_biased")
        s.f_gain = sem("ff_f_gain")
        s.f_out = sem("ff_f_out")
        rows_loaded = queue_sem(nc, k, "f_rows")
        row_loaded = queue_sem(nc, k, "f_row")
        w13, w2 = a["w_ffn13"][0], a["w_ffn2"][0]

        plan = []
        f0 = 0
        for p, n in enumerate(parts):
            for f in range(n):
                plan += [("a", p, f0 + f, f), ("b", p, f0 + f, f)]
            for half in range(2):
                plan += [("y", p, f0 + 2 * i, (half, i)) for i in range(n // 2)]
            f0 += n
        NU = len(plan)

        def source(i):
            kind, p, f, x = plan[i]
            if kind == "y":
                return pair_columns(w2, f, 512 * x[0])
            return columns(w13, (0 if kind == "a" else D_FF) + f * P)

        with nc.Block() as block:
            @block.sync
            def _(sync):
                for i in range(1, NU):
                    load_unit(k, sync, base + i, source(i))
                    if i < 5:
                        for t in (2 * i - 2, 2 * i - 1):
                            sync.dma_start(X[:, t, :], k.x2[t * P:(t + 1) * P, :]).then_inc(s.f_loaded, 16)
                for t in range(TT):
                    if t in by_vector:
                        sync.wait_ge(s.f_biased, by_vector.index(t) + 1)
                    else:
                        sync.wait_ge(s.f_out, by_gpsimd.index(t) + 1)
                    sync.dma_start(out[0, t * P:(t + 1) * P, :], X[:, t, :]).then_inc(k.stored, 16)
                sync.wait_ge(k.stored, 16 * TT)

            @block.tensor
            def _(pe):
                for i, (kind, p, f, x) in enumerate(plan):
                    u = base + i
                    pe.wait_ge(k.w_split, u + 1)
                    if kind != "y":
                        o = psall[2 * (f % 2) + (kind == "b")]
                        if x < 2:
                            if p:
                                pe.wait_ge(s.y_added, 16 * p - 8 + 4 * x + (4 if kind == "b" else 2))
                        else:
                            pe.wait_ge(s.silu_a if kind == "a" else s.prod, 2 * (f - 1))
                        for h in range(2):
                            last = product_half(k, pe, u, o[:, h * HALF:(h + 1) * HALF], xh, xl, h)
                        last.then_inc(k.w_used, 1)
                    else:
                        half, j = x
                        n = parts[p]
                        read = None
                        if half == 0:
                            pe.wait_ge(s.rest, 2 * (f + 2))
                        elif j == 0:
                            read = (s.y_added, 16 * p + 1)
                        if half == 0 and j == 0:
                            pe.wait_ge(s.prod, 2 * sum(parts[:p + 1]))
                        natural_unit(k, pe, u, banks, gh, gl, 2 * j, n - 1, s.bank_done if j == n // 2 - 1 else None,
                                     read=read)

            @block.scalar
            def _(act):
                split_act(k, act, base + 1)
                for i, (kind, p, f, x) in enumerate(plan):
                    if i + 2 < NU:
                        split_act(k, act, base + i + 2)
                    if kind == "a":
                        act.wait_ge(k.w_used, base + i + 1)
                        for h in range(2):
                            if f:
                                act.wait_ge(s.rest, 2 * f + h - 1)
                            act.activation(sa[:, h, :], psall[2 * (f % 2)][:, h * HALF:(h + 1) * HALF], ACT.Silu).then_inc(s.silu_a, 1)
                    if kind == "b":
                        for h in range(2):
                            act.wait_ge(s.prod, 2 * f + h + 1)
                            act.activation(gh[:, x, h * HALF:(h + 1) * HALF], sa[:, h, :], ACT.Copy).then_inc(s.rnd, 1)
                for t in range(TT + 1):
                    if t < TT:
                        act.wait_ge(s.f_stats, t + 1)
                        act.activation(rs[:, t:t + 1], mv[:, t, 1:2], ACT.Sqrt, bias=k.eps_ln[:, :]).then_inc(s.f_dev, 1)
                    if t:
                        act.wait_ge(s.f_nmr, t)
                        act.activation(X[:, t - 1, :], X[:, t - 1, :], ACT.Identity, scale=rs[:, t - 1:t],
                                       bias=nmr[:, t - 1:t]).then_inc(s.f_norm, 1)

            def shift(dve, t):
                dve.wait_ge(s.f_dev, t + 1)
                dve.reciprocal(rs[:, t:t + 1], rs[:, t:t + 1]).then_inc(s.f_rs, 1)
                dve.wait_ge(s.f_rs, t + 1)
                dve.tensor_scalar(nmr[:, t:t + 1], mv[:, t, 0:1], rs[:, t:t + 1], -1.0, ALU.mult, ALU.mult).then_inc(s.f_nmr, 1)

            def finish(dve, t):
                dve.wait_ge(s.f_norm, t + 1)
                if t == 0:
                    dve.wait_ge(rows_loaded, 32)
                dve.tensor_tensor(X[:, t, :], X[:, t, :], k.raw[0][:, :], ALU.mult).then_inc(s.f_gain, 1)
                if t in by_vector:
                    dve.wait_ge(s.f_gain, t + 1)
                    dve.tensor_tensor(X[:, t, :], X[:, t, :], k.raw[1][:, :], ALU.add).then_inc(s.f_biased, 1)

            @block.vector
            def _(dve):
                split_dve(k, dve, base + 1)
                for i, (kind, p, f, x) in enumerate(plan):
                    if i + 2 < NU:
                        split_dve(k, dve, base + i + 2)
                    if kind == "b":
                        dve.wait_ge(k.w_used, base + i + 1)
                        for h in range(2):
                            dve.wait_ge(s.silu_a, 2 * f + h + 1)
                            dve.tensor_tensor(sa[:, h, :], psall[2 * (f % 2) + 1][:, h * HALF:(h + 1) * HALF], sa[:, h, :],
                                              ALU.mult).then_inc(s.prod, 1)
                        for h in range(2):
                            o = slice(h * HALF, (h + 1) * HALF)
                            dve.wait_ge(s.rnd, 2 * f + h + 1)
                            dve.tensor_tensor(gl[:, x, o], sa[:, h, :], gh[:, x, o].bitcast(F32), ALU.subtract).then_inc(s.rest, 1)
                    if kind == "y" and x[1] == parts[p] // 2 - 1:
                        half = x[0]
                        for t in range(TT):
                            if t < TT - 1:
                                dve.wait_ge(s.bank_done, (TT - 1) * (2 * p + half) + t + 1)
                            else:
                                dve.wait_ge(k.w_used, base + i + 1)
                            v = X[:, t, half * 512:(half + 1) * 512]
                            if p:
                                if t == 0:
                                    dve.wait_ge(s.y_added, 16 * p)
                                dve.tensor_tensor(v, banks[t], v, ALU.add).then_inc(s.y_added, 1)
                            else:
                                if t == 0:
                                    dve.wait_ge(s.f_res, 4 * TT)
                                dve.scalar_tensor_tensor(out=v, in0=v, scalar=ALPHA, in1=banks[t], op0=ALU.mult, op1=ALU.add).then_inc(s.y_added, 1)
                            if p == len(parts) - 1:
                                dve.wait_ge(s.y_added, 16 * p + 8 * half + t + 1)
                                dve.bn_stats(bst[:, t, 6 * half:6 * half + 6], v).then_inc(s.f_stat, 1)
                                if half == 1:
                                    dve.wait_ge(s.f_stat, TT + t + 1)
                                    dve.bn_aggr(mv[:, t, :], bst[:, t, :]).then_inc(s.f_stats, 1)
                                    if t:
                                        shift(dve, t - 1)
                shift(dve, TT - 1)
                for t in range(TT):
                    finish(dve, t)

            @block.gpsimd
            def _(pool):
                pool.wait_ge(s.f_loaded, 16 * TT)
                for i in range(4):
                    h, what = i // 2, (a["ln2_g"], a["ln2_b"])[i % 2]
                    if i:
                        pool.wait_ge(s.f_res, TT * i)
                    pool.dma_start(row[:, :], what[:, h * HALF:(h + 1) * HALF].partition_broadcast(P)).then_inc(row_loaded, 16)
                    pool.wait_ge(row_loaded, 16 * (i + 1))
                    for t in range(TT):
                        v = X[:, t, h * HALF:(h + 1) * HALF]
                        pool.tensor_tensor(v, v, row[:, :], (ALU.mult, ALU.add)[i % 2]).then_inc(s.f_res, 1)
                pool.wait_ge(k.w_split, base + NU)
                pool.dma_start(k.raw[0][:, :], a["ln3_g"].partition_broadcast(P)).then_inc(rows_loaded, 16)
                pool.dma_start(k.raw[1][:, :], a["ln3_b"].partition_broadcast(P)).then_inc(rows_loaded, 16)
                pool.wait_ge(rows_loaded, 32)
                for t in by_gpsimd:
                    pool.wait_ge(s.f_gain, t + 1)
                    pool.tensor_tensor(X[:, t, :], X[:, t, :], k.raw[1][:, :], ALU.add).then_inc(s.f_out, 1)


def hybrid_layer(nc, a, out, scratch):
    k = Names()
    k.oaT, k.hA, k.gateB, k.stats, k.x1, k.x2 = scratch
    with ExitStack() as ctx:
        k.whole_program = ctx
        k.phase_sems = []

        def sb(name, shape, dt=F32):
            return ctx.enter_context(nc.sbuf_tensor(name, shape, dt))

        def sem(name):
            return ctx.enter_context(nc.semaphore(name))
        k.x_loaded = [sem(f"x_loaded{i}") for i in range(4)]
        k.small_loaded = sem("small_loaded")
        k.const = sem("const")
        k.x_turned = sem("x_turned")
        k.x_rounded = sem("x_rounded")
        k.x_split = sem("x_split")
        k.w_rounded = sem("w_rounded")
        k.w_split = sem("w_split")
        k.w_used = sem("w_used")
        k.db_copied = sem("db_copied")
        k.db_turned = sem("db_turned")
        k.conv_turned = sem("conv_turned")
        k.mag_ready = sem("mag_ready")
        k.sp_step = sem("sp_step")
        k.lnb_ready = sem("lnb_ready")
        k.g_ready = sem("g_ready")
        k.gam_done = sem("gam_done")
        k.gam_read = sem("gam_read")
        k.dve_setup = sem("dve_setup")
        k.s_zero = sem("s_zero")
        k.colb = sem("colb")
        k.chain = sem("chain")
        k.stored = sem("stored")
        k.w_loaded = [ctx.enter_context(nc.semaphore(f"w_loaded{i}")) for i in range(RAW_SLOTS)]
        k.raw = [sb(f"raw{i}", [P, UNIT]) for i in range(RAW_SLOTS)]
        k.whi = [sb(f"whi{i}", [P, UNIT], F32R) for i in range(SPLIT_SLOTS)]
        k.wlo = [sb(f"wlo{i}", [P, UNIT], F32R) for i in range(SPLIT_SLOTS)]
        k.ident = sb("ident", [P, P])
        k.eps_rms = sb("eps_rms", [P, 1])
        k.eps_ln = sb("eps_ln", [P, 1])
        k.one_col = sb("one_col", [P, 1])
        k.dn_g = sb("dn_g", [P, 1])
        k.xh = sb("xh", [P, KT, SEQ], F32R)
        k.xl = sb("xl", [P, KT, SEQ], F32R)
        with ExitStack() as dn:
            def sbd(name, shape, dt=F32):
                return dn.enter_context(nc.sbuf_tensor(name, shape, dt))
            k.ones = sbd("ones", [P, P])
            k.upto = sbd("upto", [P, P])
            k.neg_strict = sbd("neg_strict", [P, P])
            k.neg_incl = sbd("neg_incl", [P, P])
            k.same = sbd("same", [P, P])
            k.other = sbd("other", [P, P])
            k.beta = sbd("beta", [P, HEADS, TT])
            k.lnb = sbd("lnb", [P, HEADS, TT])
            k.gam = sbd("gam", [P, HEADS, TT])
            k.gtot = sbd("gtot", [P, HEADS, TT])
            k.gtot_e = sbd("gtot_e", [P, HEADS, TT])
            k.gl = sbd("gl", [P, HEADS, TT])
            k.gs = sbd("gs", [P, HEADS, TT])
            k.cw = sbd("cw", [P, 96])
            k.xpad = [sbd(f"xpad{i}", [P, CONV - 1 + SEQ]) for i in range(2)]
            setup(nc, k, a)
            k.next_unit = columns(a["w_in"][0], COL_GA)
            deltanet(nc, k, a)
        base = 1 + 4 * (HEADS + 1)
        k.next_unit = columns(a["w_in"][0], COL_BQ)
        branch_a(nc, k, a, base)
        base += 3 * KT - GATES_ELSEWHERE
        with ExitStack() as ob:
            k.obh = ob.enter_context(nc.sbuf_tensor("obh", [P, HG, SEQ], F32R))
            k.obl = ob.enter_context(nc.sbuf_tensor("obl", [P, HG, SEQ], F32R))
            k.next_unit = a["w_br_b"][0][:, 0:2 * P].rearrange("(k p) n -> p k n", p=P)
            attention(nc, k, a, base)
            base += 3 * GROUPS * HG + GATES_LATER
            k.next_unit = pair_columns(a["w_mix_out"][0], 0, 0)
            merge(nc, k, a, base)
            base += 4
        k.next_unit = columns(a["w_xkv"][0], 0)
        project_and_norm(nc, k, "mix_", base, a["w_mix_out"][0], k.xh, k.xl, a["x"][0], None, None,
                         a["ln1_g"], a["ln1_b"], k.xh, k.xl, k.x1)
        base += 8
        oh = sb("oh", [P, KT, SEQ], F32R)
        ol = sb("ol", [P, KT, SEQ], F32R)
        k.next_unit = pair_columns(a["w_xo"][0], 0, 0)
        cross_attention(nc, k, a, base, oh, ol)
        base += 24
        k.next_unit = columns(a["w_ffn13"][0], 0)
        project_and_norm(nc, k, "xo_", base, a["w_xo"][0], oh, ol, k.x1, a["ln1_g"], a["ln1_b"],
                         a["ln2_g"], a["ln2_b"], k.xh, k.xl, k.x2)
        base += 8
        feed_forward(nc, k, a, base, k.xh, k.xl, oh, ol, out)


INPUTS = ("x", "mem", "positions", "w_in", "conv_w", "a_log", "dt_bias", "dn_norm_g", "w_br_a", "w_br_b",
          "w_mix_out", "ln1_g", "ln1_b", "w_xq", "w_xkv", "w_xo", "ln2_g", "ln2_b", "w_ffn13", "w_ffn2",
          "ln3_g", "ln3_b")
SCRATCH = {"oaT": (HEADS, P, SEQ), "hA": (KT, P, SEQ), "gateB": (KT, P, SEQ), "stats": (HG, SEQ, GROUPS, 2),
           "x1": (SEQ, D_MODEL), "x2": (SEQ, D_MODEL)}


def rope_frequencies():
    f = np.float32(10000.0) ** (-np.arange(0, P, 2, dtype=np.float32) / np.float32(P))
    return np.concatenate([f, f]).astype(np.float32).reshape(P, 1)


def kernel(**inputs):
    import concourse.bacc as bacc
    from concourse.bass_utils import run_bass_kernel_spmd

    nc = bacc.Bacc("TRN2", target_bir_lowering=False, num_devices=1)
    arrays = {n: np.ascontiguousarray(inputs[n]) for n in INPUTS}
    arrays["rope_freq"] = rope_frequencies()
    a = {n: nc.dram_tensor(f"in_{n}", v.shape, mybir.dt.from_np(v.dtype), kind="ExternalInput").ap()
         for n, v in arrays.items()}
    out = nc.dram_tensor("out", (1, SEQ, D_MODEL), F32, kind="ExternalOutput").ap()
    scratch = [nc.dram_tensor(f"scratch_{n}", shape, F32, kind="Internal").ap() for n, shape in SCRATCH.items()]
    hybrid_layer(nc, a, out, scratch)
    r = run_bass_kernel_spmd(nc, [{f"in_{n}": v for n, v in arrays.items()}], core_ids=[0])
    return r.results[0]["out"]
```
